# Optimizing a Trainium2 kernel written in Bass

```python
import math
import jax, jax.numpy as jnp
from jax import lax
import numpy as np

D_MODEL = 2048
BATCH = 1
SEQ = 256
DEPTH = 1

CHUNK = 64
Q_BLOCK = 128
D_MIX = D_MODEL
D_ATTN = D_MIX // 2
D_CONV = D_MIX - D_ATTN
V_HEAD_DIM = 128
N_DIFF_HEADS = D_ATTN // V_HEAD_DIM
QK_HEAD_DIM = V_HEAD_DIM // 2
CONV_WIDTH = 3
N_GROUPS = 4
EXPERTS_PER_GROUP = 8
N_EXPERTS = N_GROUPS * EXPERTS_PER_GROUP
TOP_K_INNER = 2
D_EXPERT = 512
MOE_BLOCK = 128
NORM_EPS = 1e-6
SUBLN_EPS = 1e-5
D_IN_PROJ = 3 * D_ATTN + 3 * D_CONV

kernel_name = "hybrid_diffattn_shortconv_hmoe_layer"

def rmsnorm(x, g, eps=NORM_EPS):
    xf = x.astype(jnp.float32)
    y = xf * lax.rsqrt(jnp.mean(xf * xf, axis=-1, keepdims=True) + eps)
    return (y * g.astype(jnp.float32)).astype(x.dtype)

def alibi_slopes(n_heads):
    start = 2.0 ** (-8.0 / n_heads)
    return jnp.asarray(start ** np.arange(1, n_heads + 1), dtype=jnp.float32)

def diff_attention(q, k, v, lam, lam_init, subln_w):
    b, s = q.shape[0], q.shape[1]
    nb = s // Q_BLOCK
    q = q * jnp.asarray(QK_HEAD_DIM ** -0.5, dtype=q.dtype)
    qb = jnp.moveaxis(q.reshape(b, nb, Q_BLOCK, N_DIFF_HEADS, 2, QK_HEAD_DIM), 1, 0)
    starts = jnp.arange(nb, dtype=jnp.int32) * Q_BLOCK
    slopes = alibi_slopes(N_DIFF_HEADS)
    kpos = jnp.arange(s, dtype=jnp.int32)

    def attend(args):
        q_blk, start = args
        sc = jnp.einsum('bqhmd,bkhmd->bmhqk', q_blk, k).astype(jnp.float32)
        qpos = start + jnp.arange(Q_BLOCK, dtype=jnp.int32)
        dist = jnp.abs(qpos[:, None] - kpos[None, :]).astype(jnp.float32)
        allowed = (kpos // CHUNK)[None, :] <= (qpos // CHUNK)[:, None]
        sc = jnp.where(allowed, sc - slopes[:, None, None] * dist, -jnp.inf)
        p = jax.nn.softmax(sc, axis=-1)
        a = p[:, 0] - lam * p[:, 1]
        return jnp.einsum('bhqk,bkhd->bqhd', a.astype(v.dtype), v)

    o = lax.map(attend, (qb, starts))
    o = jnp.moveaxis(o, 0, 1).reshape(b, s, N_DIFF_HEADS, V_HEAD_DIM)
    o = rmsnorm(o, subln_w, SUBLN_EPS) * jnp.asarray(1.0 - lam_init, dtype=o.dtype)
    return o.reshape(b, s, N_DIFF_HEADS * V_HEAD_DIM)

def short_conv(bg, cg, u, w):
    z = cg * u
    conv = lax.conv_general_dilated(
        z, w[:, None, :].astype(z.dtype), window_strides=(1,),
        padding=[(CONV_WIDTH - 1, 0)], dimension_numbers=('NWC', 'WIO', 'NWC'),
        feature_group_count=z.shape[-1])
    return bg * conv

def hier_moe(h, w_rg, b_rg, w_re, b_re, w_gate, w_up, w_down):
    b, s, d = h.shape
    t = h.reshape(-1, d)
    g_prob = jax.nn.softmax((t @ w_rg).astype(jnp.float32) + b_rg.astype(jnp.float32), axis=-1)
    g_w, g_idx = lax.top_k(g_prob, 1)
    e_logits = jnp.einsum('nd,dge->nge', t, w_re).astype(jnp.float32) + b_re.astype(jnp.float32)
    e_logits = jnp.take_along_axis(e_logits, g_idx[:, :, None], axis=1)[:, 0]
    e_w, e_idx = lax.top_k(jax.nn.softmax(e_logits, axis=-1), TOP_K_INNER)
    e_w = e_w / jnp.sum(e_w, axis=-1, keepdims=True)
    gate = g_w * e_w
    flat_idx = g_idx * EXPERTS_PER_GROUP + e_idx
    combine = jnp.sum(jax.nn.one_hot(flat_idx, N_EXPERTS, dtype=jnp.float32) * gate[..., None], axis=1)
    tb = t.reshape(-1, MOE_BLOCK, d)
    cb = combine.reshape(-1, MOE_BLOCK, N_EXPERTS).astype(t.dtype)

    def expert_block(args):
        tk, ck = args
        hg = jnp.einsum('td,edf->tef', tk, w_gate)
        hu = jnp.einsum('td,edf->tef', tk, w_up)
        a = jax.nn.silu(hg) * hu * ck[:, :, None]
        return jnp.einsum('tef,efd->td', a, w_down)

    return lax.map(expert_block, (tb, cb)).reshape(b, s, d)

def setup_inputs(seed: int = 0) -> dict:
    key = jax.random.key(seed)
    ks = jax.random.split(key, 24)
    f32 = jnp.float32
    nrm = lambda k, shape, scale: jax.random.normal(k, shape, f32) * scale
    gain = lambda k, shape: 1.0 + 0.05 * jax.random.normal(k, shape, f32)
    L = DEPTH
    return {
        "x": nrm(ks[0], (BATCH, SEQ, D_MODEL), 1.0),
        "c": nrm(ks[1], (BATCH, D_MODEL), 1.0),
        "w_ada": nrm(ks[2], (L, D_MODEL, 6 * D_MODEL), 0.5 * D_MODEL ** -0.5),
        "b_ada": nrm(ks[3], (L, 6 * D_MODEL), 0.02),
        "g_pre1": gain(ks[4], (L, D_MODEL)),
        "w_in": nrm(ks[5], (L, D_MODEL, D_IN_PROJ), D_MODEL ** -0.5),
        "lam_q1": nrm(ks[6], (L, QK_HEAD_DIM), 0.1),
        "lam_k1": nrm(ks[7], (L, QK_HEAD_DIM), 0.1),
        "lam_q2": nrm(ks[8], (L, QK_HEAD_DIM), 0.1),
        "lam_k2": nrm(ks[9], (L, QK_HEAD_DIM), 0.1),
        "g_subln": gain(ks[10], (L, V_HEAD_DIM)),
        "w_conv": nrm(ks[11], (L, CONV_WIDTH, D_CONV), CONV_WIDTH ** -0.5),
        "w_out": nrm(ks[12], (L, D_MIX, D_MODEL), D_MIX ** -0.5),
        "g_post1": gain(ks[13], (L, D_MODEL)),
        "g_pre2": gain(ks[14], (L, D_MODEL)),
        "w_router_g": nrm(ks[15], (L, D_MODEL, N_GROUPS), D_MODEL ** -0.5),
        "b_router_g": nrm(ks[16], (L, N_GROUPS), 0.01),
        "w_router_e": nrm(ks[17], (L, D_MODEL, N_GROUPS, EXPERTS_PER_GROUP), D_MODEL ** -0.5),
        "b_router_e": nrm(ks[18], (L, N_GROUPS, EXPERTS_PER_GROUP), 0.01),
        "w_gate": nrm(ks[19], (L, N_EXPERTS, D_MODEL, D_EXPERT), D_MODEL ** -0.5),
        "w_up": nrm(ks[20], (L, N_EXPERTS, D_MODEL, D_EXPERT), D_MODEL ** -0.5),
        "w_down": nrm(ks[21], (L, N_EXPERTS, D_EXPERT, D_MODEL), D_EXPERT ** -0.5),
        "g_post2": gain(ks[22], (L, D_MODEL)),
    }

def reference(x, c, w_ada, b_ada, g_pre1, w_in, lam_q1, lam_k1, lam_q2, lam_k2, g_subln,
              w_conv, w_out, g_post1, g_pre2, w_router_g, b_router_g, w_router_e, b_router_e,
              w_gate, w_up, w_down, g_post2):
    b, s, _ = x.shape
    splits = [D_ATTN, 2 * D_ATTN, 3 * D_ATTN, 3 * D_ATTN + D_CONV, 3 * D_ATTN + 2 * D_CONV]
    for l in range(DEPTH):
        lam_init = 0.8 - 0.6 * math.exp(-0.3 * l)
        mod = jax.nn.silu(c) @ w_ada[l] + b_ada[l]
        sh1, sc1, gt1, sh2, sc2, gt2 = jnp.split(mod[:, None, :], 6, axis=-1)

        h = rmsnorm(x, g_pre1[l]) * (1.0 + sc1) + sh1
        proj = h @ w_in[l]
        q, k, v, bg, cg, u = jnp.split(proj, splits, axis=-1)
        q = q.reshape(b, s, N_DIFF_HEADS, 2, QK_HEAD_DIM)
        k = k.reshape(b, s, N_DIFF_HEADS, 2, QK_HEAD_DIM)
        v = v.reshape(b, s, N_DIFF_HEADS, V_HEAD_DIM)
        lam = (jnp.exp(jnp.sum(lam_q1[l] * lam_k1[l]).astype(jnp.float32))
               - jnp.exp(jnp.sum(lam_q2[l] * lam_k2[l]).astype(jnp.float32)) + lam_init)
        y_attn = diff_attention(q, k, v, lam, lam_init, g_subln[l])
        y_conv = short_conv(bg, cg, u, w_conv[l])
        y = jnp.concatenate([y_attn, y_conv], axis=-1) @ w_out[l]
        x = x + gt1 * rmsnorm(y, g_post1[l])

        h = rmsnorm(x, g_pre2[l]) * (1.0 + sc2) + sh2
        y = hier_moe(h, w_router_g[l], b_router_g[l], w_router_e[l], b_router_e[l],
                     w_gate[l], w_up[l], w_down[l])
        x = x + gt2 * rmsnorm(y, g_post2[l])
    return x


_drawn_inputs = setup_inputs


def setup_inputs(seed=0):
    import zlib

    import numpy as np

    out = dict(_drawn_inputs(seed))
    spreads = {}
    factors = {'lam_k2': 28.179,
     'b_router_e': 2.68,
     'g_post2': 3.927,
     'lam_q1': 64.0,
     'lam_k1': 8.0,
     'b_router_g': 8.0}
    for name, (base, spread) in spreads.items():
        noise = np.random.default_rng([zlib.crc32(name.encode()), seed]).standard_normal(out[name].shape)
        drawn = base * np.exp(spread * noise) if base else spread * noise
        out[name] = __import__('jax').numpy.asarray(drawn.astype(out[name].dtype))
    for name, factor in factors.items():
        out[name] = (out[name] * factor).astype(out[name].dtype)
    return out
```

```python
import math
from contextlib import ExitStack

import concourse.bass as bass
from concourse import mybir

ALU = mybir.AluOpType
ACT = mybir.ActivationFunctionType
F32 = mybir.dt.float32
I32 = mybir.dt.int32
U32 = mybir.dt.uint32
AX_X = mybir.AxisListType.X

P = 128
D = 2048
SEQ = 256
TT = SEQ // P
KC = D // P
HEADS = 8
DK = 64
DV = 128
HG = 4
N_GROUPS = 4
PER_GROUP = 8
NE = N_GROUPS * PER_GROUP
FE = 512
CHUNK = 64
LAM_INIT = 0.8 - 0.6 * math.exp(-0.3 * 0)
NORM_EPS = 1e-6
SUBLN_EPS = 1e-5
CAP = 64
MAX_EXTRA = (2 * SEQ - NE) // CAP
ITEMS = 40
NOWHERE = 4096.0

RING = 8
SLOT = 4096
UNROLL = 4

C_ID = 0
C_TRI = C_ID + P
C_ONE = C_TRI + P
C_DIST = C_ONE + P
C_SLOT = C_DIST + P + SEQ
C_IOTA = C_SLOT + P
C_PRI8 = C_IOTA + ITEMS
C_PRI4 = C_PRI8 + 8
C_TOK = C_PRI4 + 4
C_OUT = C_TOK + TT
C_GRP = C_OUT + 2 * TT
C_EPS = C_GRP + 1
C_ALL = C_EPS + 3
A_C = 0
A_GPRE1 = A_C + KC
A_GPOST1 = A_GPRE1 + KC
A_GPRE2 = A_GPOST1 + KC
A_GPOST2 = A_GPRE2 + KC
A_BADA = A_GPOST2 + KC
A_WCONV = A_BADA + 6 * KC
A_GSUB = A_WCONV + 3 * HEADS
A_BRT = A_GSUB + 1
A_ALL = A_BRT + N_GROUPS + NE

R_LOGIT = 0
R_OUTER = R_LOGIT + TT * (N_GROUPS + NE)
R_PICKED = R_OUTER + TT * NE
R_SAME4 = R_PICKED + TT * 8
R_GROUP = R_SAME4 + TT * 4
R_SAME8 = R_GROUP + TT * 4
R_INNER = R_SAME8 + TT * 8
R_MAX = R_INNER + 2 * TT * 8
R_EXP = R_MAX + 6 * TT
R_W = R_EXP + TT * 5
R_HOT = R_W + 2 * TT
R_BOTH = R_HOT + 2 * TT * NE
R_PROD = R_BOTH + TT * NE
R_RED = R_PROD + 3 * 2 * TT * NE
R_POS = R_RED + 3 * 2 * TT
R_EXTRA = R_POS + 5 * 2 * TT
R_ALL = R_EXTRA + 2
assert R_ALL <= HG * TT * DV
T_SLOT = 0
T_ITEM = T_SLOT + 2 * TT * P
T_TABLE = T_ITEM + 2 * TT * 5 * ITEMS
T_MISS = T_TABLE + 5 * ITEMS
assert T_MISS + 2 * ITEMS <= D

BLOCKS = [("q", 0), ("k", 0), ("v", 0), ("C", 0), ("X", 0), ("q", 1), ("k", 1), ("v", 1),
          ("C", 1), ("X", 1), ("B", 0), ("B", 1)]
COL0 = {"q": 0, "k": 1024, "v": 2048, "B": 3072, "C": 4096, "X": 5120}
NB_IN = len(BLOCKS)
NB = NB_IN + D // 512
SUB = 4
MODS = [1, 0, 2, 3, 4, 5]
SH1, SC1, GT1, SH2, SC2, GT2 = range(6)
SCORE_AT = {4 * SUB - 3 + 2 * h if h < HG else 8 * SUB + 1 + 2 * (h - HG): h for h in range(HEADS)}
FINISH_AT = {6 * SUB: 0, 11 * SUB: 1}
COLUMNS_AT = {12 * (i - 1) + 2: i for i in range(2, 6)}
BCAST_AT = {NB_IN * SUB + 4: 0, NB_IN * SUB + 8: 1}


def plan_ring():
    plan = [("ada", i, r) for i in range(2) for r in range(KC // 2)]
    late = [("ada", i, r) for i in range(2, 6) for r in range(KC // 2)]
    for n in range(2 * NB_IN):
        plan.append(("w", n // 2, n % 2))
        plan += late[4 * n // 3:4 * (n + 1) // 3]
    plan += [("w", b, h) for b in range(NB_IN, NB) for h in range(2)]
    return plan


PLAN = plan_ring()
USES0 = len(PLAN) // RING
W_USED0 = 2 * NB
assert len(PLAN) % RING == 0 and (UNROLL * 6) % RING == 0


def hybrid_layer(nc, consts, small, lam, wrt, x, w_ada, w_in, w_out, w_gate, w_up, w_down, out):
    ctx = ExitStack()
    with ctx:
        def sb(name, shape, dt=F32):
            return ctx.enter_context(nc.sbuf_tensor(name, shape, dt))

        def sem(name):
            return ctx.enter_context(nc.semaphore(name))

        h2_rows = nc.dram_tensor("h2_rows", (SEQ, D), F32, kind="Internal").ap()
        y_rows = nc.dram_tensor("y_rows", (4 * SEQ, D // 2), F32, kind="Internal").ap()

        ring = sb("ring", [P, RING, SLOT])
        region_a = sb("region_a", [P, 2 * D])
        region_b = sb("region_b", [P, 2 * D])
        region_c = sb("region_c", [P, 2 * D + 8])
        acc = sb("acc", [P, 2, D])
        soft = sb("soft", [P, 2, P + SEQ])
        o_raw = sb("o_raw", [P, HG, TT, DV])
        a_turned = sb("a_turned", [P, P + SEQ])
        cst = sb("cst", [P, C_ALL])
        par = sb("par", [P, A_ALL])
        sml = sb("sml", [P, 64])
        mods = sb("mods", [P, 6, KC])
        cols = sb("cols", [P, 4, KC])

        bank = [ctx.enter_context(nc.psum_tensor(f"bank{i}", [P, 512], F32)) for i in range(8)]

        x_rows = region_a[:, :].rearrange("p (t d) -> p t d", t=TT)
        y_turned = region_a[:, :].rearrange("p (c s) -> p c s", s=SEQ)
        h_turned = region_b[:, :].rearrange("p (k s) -> p k s", s=SEQ)
        x1 = region_b[:, :].rearrange("p (t d) -> p t d", t=TT)
        q_turned = region_c[:, 0:1024].rearrange("p (c s) -> p c s", s=SEQ)
        k_turned = region_c[:, 1024:2048].rearrange("p (c s) -> p c s", s=SEQ)
        v_rows = region_c[:, 2048:3072].rearrange("p (t n) -> p t n", t=TT)
        conv_in = region_c[:, 3072:3072 + HG * (SEQ + 2)].rearrange("p (c s) -> p c s", s=SEQ + 2)
        y_sb = region_c[:, 0:2 * D].rearrange("p (t d) -> p t d", t=TT)
        wr_sb = soft[:, :, :].rearrange("p a b -> p (a b)")[:, 0:KC * 36].rearrange("p (k n) -> p k n", k=KC)
        rt = o_raw[:, :, :, :].rearrange("p a b c -> p (a b c)")

        ident = cst[:, C_ID:C_ID + P]
        tri = cst[:, C_TRI:C_TRI + P]
        ones = cst[:, C_ONE:C_ONE + P]
        dist = cst[:, C_DIST:C_DIST + P + SEQ]
        eps_norm = cst[:, C_EPS:C_EPS + 1]
        eps_subln = cst[:, C_EPS + 1:C_EPS + 2]
        zero = cst[:, C_EPS + 2:C_EPS + 3]

        c_exp, silu_c = sml[:, 0:16], sml[:, 16:32]
        lam_s, lam_e, neg_lam = sml[:, 32:34], sml[:, 34:36], sml[:, 36:37]
        ssq = sml[:, 37:39]
        rms = sml[:, 39:41]
        junk = sb("junk", [P, DV])
        mx = sb("mx", [P, 4])
        p_sum = sb("p_sum", [P, 4])
        p_rec = sb("p_rec", [P, 4])
        o_ss = sb("o_ss", [P, HG * TT])
        o_rec = sb("o_rec", [P, HG * TT])
        y_ss = sb("y_ss", [P, TT, 4])
        gsub = sml[:, 41:42]
        xrms = sml[:, 42:44]
        yrms = sml[:, 44:46]
        h2rms = sml[:, 46:48]

        s_slot = [sem(f"s_slot{i}") for i in range(RING)]
        s_cst = sem("s_cst")
        s_par = sem("s_par")
        s_x = [sem(f"s_x_in{t}") for t in range(TT)]
        s_ada_used = sem("s_ada_used")
        s_w_used = sem("s_w_used")
        s_dve = sem("s_dve")
        s_act = sem("s_act")
        s_cexp = sem("s_cexp")
        s_ssq = sem("s_ssq")
        s_rms = sem("s_rms")
        s_xn = sem("s_xn")
        s_xt = sem("s_xt")
        s_xt_read = sem("s_xt_read")
        s_turn = sem("s_turn")
        s_turn_read = sem("s_turn_read")
        s_hT = sem("s_hT")
        s_block_act = sem("s_block_act")
        s_block_dve = sem("s_block_dve")
        s_scores = sem("s_scores")
        s_shift = sem("s_shift")
        s_prob = sem("s_prob")
        s_a = sem("s_a")
        s_o = sem("s_o")
        s_o_read = sem("s_o_read")
        s_o_rms = sem("s_o_rms")
        s_o_norm = sem("s_o_norm")
        s_lam_in = sem("s_lam_in")
        s_lam = sem("s_lam")
        s_lam_e = sem("s_lam_e")
        s_cols = sem("s_cols")
        s_wr = sem("s_wr")

        ada_v = w_ada[0].rearrange("(p k) (m n) -> p k m n", k=KC, m=6)
        in_v = w_in[0].rearrange("(p k) n -> p k n", k=KC)
        out_v = w_out[0].rearrange("(c p) n -> p c n", p=P)
        x_v = x[0].rearrange("(t p) d -> t p d", p=P)
        o_v = out[0].rearrange("(t p) d -> t p d", p=P)

        slot_of = {what: n for n, what in enumerate(PLAN)}
        w_slots = [n for n, what in enumerate(PLAN) if what[0] == "w"]
        ada_slots = [n for n, what in enumerate(PLAN) if what[0] == "ada"]

        def landed(eng, what):
            n = slot_of[what]
            eng.wait_ge(s_slot[n % RING], 16 * (n // RING + 1))
            return ring[:, n % RING, :]

        turns = []
        for s in range(-1, NB * SUB + 1):
            if s == -1:
                turns += [("col", 0), ("col", 1)]
            if s - 2 in SCORE_AT:
                turns.append(("head", SCORE_AT[s - 2]))
            if s in FINISH_AT:
                turns += [("fin", FINISH_AT[s], h) for h in range(2)]
            if s in COLUMNS_AT:
                turns.append(("col", COLUMNS_AT[s]))
            if s in BCAST_AT:
                turns += [("bc", BCAST_AT[s], j) for j in range(4)]
        turns += [("bc", n, j) for n in (2, 3) for j in range(4)]
        turn_no = {what: n for n, what in enumerate(turns)}
        N_TURNS_AFTER = len(turns)

        act_evac = [b for b in range(NB) if b >= NB_IN or BLOCKS[b][0] not in "XB"]
        dve_evac = [b for b in range(NB) if b not in act_evac]

        g_rows = region_a[0:CAP, :].rearrange("p (b d) -> p b d", b=2)
        xe_turned = region_c[:, 0:D].rearrange("p (b k s) -> p b k s", b=2, k=KC)
        y_item = region_c[:, D:2 * D].rearrange("p (b n) -> p b n", b=2)
        silu_g = acc[0:CAP, 0, 0:FE]
        act_rows = acc[0:CAP, 0, FE:2 * FE]
        act_turned = acc[:, 0, 2 * FE:2 * FE + 4 * CAP].rearrange("p (j s) -> p j s", j=4)
        g_idx = sb("g_idx", [P, ITEMS], I32)
        s_idx = sb("s_idx", [P, ITEMS], I32)
        e_idx = sb("e_idx", [P, ITEMS], I32)
        n_extra = sb("n_extra", [P, 1], I32)
        g_cur = sb("g_cur", [P, 2], I32)
        s_cur = sb("s_cur", [P, 2], I32)
        weight = sb("weight", [P, ITEMS])
        f_ss = sb("f_ss", [P, TT])

        def hot_slot(n):
            return acc[:, 0, T_SLOT + P * n:T_SLOT + P * (n + 1)]

        def hot_item(n):
            c0 = T_ITEM + 5 * ITEMS * n
            return acc[:, 0, c0:c0 + 5 * ITEMS].rearrange("p (a b) -> p a b", a=5)

        s_h2 = sem("s_h2")
        s_h2_store = sem("s_h2_store")
        s_h2t = sem("s_h2t")
        s_h2t_read = sem("s_h2t_read")
        s_logit = sem("s_logit")
        s_gexp_in = sem("s_gexp_in")
        s_gexp = sem("s_gexp")
        s_picks = sem("s_picks")
        s_rank = sem("s_rank")
        s_extra = sem("s_extra")
        s_base = sem("s_base")
        s_hot = sem("s_hot")
        s_table = sem("s_table")
        s_tables = sem("s_tables")
        s_x1 = sem("s_x1")
        s_xsq = sem("s_xsq")
        s_h2rms = sem("s_h2rms")
        s_ysum = sem("s_ysum")
        s_yrms = sem("s_yrms")
        s_zero = sem("s_zero")

        s_g_cur = sem("s_g_cur")
        s_gather = [sem(f"s_gather{b}") for b in range(2)]
        s_xe_psum = sem("s_xe_psum")
        s_xe_act = sem("s_xe_act")
        s_xe_dve = sem("s_xe_dve")
        s_silu_g = sem("s_silu_g")
        s_act_rows = sem("s_act_rows")
        s_at_psum = sem("s_at_psum")
        s_at = sem("s_at")
        s_y_act = sem("s_y_act")
        s_y_dve = sem("s_y_dve")
        s_s_cur = sem("s_s_cur")
        s_y_free = sem("s_y_free")
        s_scatter = [sem(f"s_scatter{b}") for b in range(2)]
        s_pool_turn = sem("s_pool_turn")
        s_pe_turn = sem("s_pe_turn")

        s_pair = [sem(f"s_pair{t}") for t in range(TT)]
        s_fsum = sem("s_fsum")
        s_fsq = sem("s_fsq")
        s_frms = sem("s_frms")
        s_fin = sem("s_fin")
        s_store = sem("s_store")

        x_scatter = sem("x_scatter")
        x_load = [sem(f"x_load{r}") for r in range(6)]
        x_done = sem("x_done")
        x_gcur = sem("x_gcur")
        x_gather = sem("x_gather")
        x_xe = sem("x_xe")
        x_xe_act = sem("x_xe_act")
        x_xe_dve = sem("x_xe_dve")
        x_gu = sem("x_gu")
        x_silu = sem("x_silu")
        x_rows_done = sem("x_rows_done")
        x_at = sem("x_at")
        x_atc = sem("x_atc")
        x_dn = sem("x_dn")
        x_ya = sem("x_ya")
        x_yd = sem("x_yd")

        gate_v = w_gate[0].rearrange("e (p k) f -> e p (k f)", k=KC)
        up_v = w_up[0].rearrange("e (p k) f -> e p (k f)", k=KC)
        down_v = w_down[0].rearrange("e (p j) n -> e p (j n)", j=4)
        PARTS = [(gate_v, 0), (up_v, 0), (gate_v, 1), (up_v, 1), (down_v, 0), (down_v, 1)]
        N_IT = NE // UNROLL

        block = ctx.enter_context(nc.Block())

        @block.sync
        def _(sp):
            used_w = used_a = 0
            ordinal = []
            for what in PLAN:
                if what[0] == "w":
                    used_w += 1
                    ordinal.append((s_w_used, used_w))
                else:
                    used_a += 1
                    ordinal.append((s_ada_used, used_a))
            for n, what in enumerate(PLAN):
                if n >= RING:
                    sp.wait_ge(*ordinal[n - RING])
                dst = ring[:, n % RING, :]
                if what[0] == "ada":
                    src = ada_v[:, 2 * what[2]:2 * what[2] + 2, MODS[what[1]], :]
                    dst = dst.rearrange("p (k n) -> p k n", k=2)
                else:
                    b, half = what[1], what[2]
                    if b < NB_IN:
                        kind, g = BLOCKS[b]
                        c0 = COL0[kind] + 512 * g
                        src = in_v[:, 8 * half:8 * half + 8, c0:c0 + 512]
                    else:
                        c0 = 512 * (b - NB_IN)
                        src = out_v[:, 8 * half:8 * half + 8, c0:c0 + 512]
                    dst = dst.rearrange("p (k n) -> p k n", k=8)
                sp.dma_start(dst, src).then_inc(s_slot[n % RING], 16)
            with sp.Fori(0, N_IT) as it:
                for u in range(UNROLL):
                    for r, (view, half) in enumerate(PARTS):
                        n = 6 * u + r
                        sp.wait_ge(s_w_used, W_USED0 - RING + 1 + it * (6 * UNROLL) + n)
                        src = view[bass.ds(it * UNROLL + u, 1), :, SLOT * half:SLOT * (half + 1)]
                        sp.dma_start(ring[:, n % RING, :], src.rearrange("a p f -> (a p) f")).then_inc(
                            s_slot[n % RING], 16)
            sp.wait_ge(s_tables, 1)
            nx = sp.value_load(n_extra[0:1, 0:1], min_val=0, max_val=MAX_EXTRA)
            sp.wait_ge(s_w_used, W_USED0 + 6 * NE)
            with sp.If(nx > 0):
                with sp.Fori(0, nx) as j:
                    sp.wait_ge(x_done, j + 1)
                    e = sp.value_load(e_idx[0:1, bass.ds(j + NE, 1)], min_val=0, max_val=NE - 1)
                    for r, (view, half) in enumerate(PARTS):
                        src = view[bass.ds(e, 1), :, SLOT * half:SLOT * (half + 1)]
                        sp.dma_start(ring[:, r, :], src.rearrange("a p f -> (a p) f")).then_inc(x_load[r], 16)
            sp.wait_ge(s_scatter[0], 16 * NE // 2)
            sp.wait_ge(s_scatter[1], 16 * NE // 2)
            sp.wait_ge(x_done, nx + 1)
            yv = y_rows.rearrange("(k t p c) n -> t p k (c n)", k=2, t=TT, p=P)
            for t in range(TT):
                sp.dma_start(ring[:, t, :].rearrange("p (k n) -> p k n", k=2), yv[t]).then_inc(s_pair[t], 16)
            for t in range(TT):
                sp.wait_ge(s_fin, t + 1)
                sp.dma_start(o_v[t], x1[:, t, :]).then_inc(s_store, 16)
            sp.wait_ge(s_store, 16 * TT)

        @block.gpsimd
        def _(pool):
            pool.wait_ge(s_logit, 1)
            pool.memset(g_rows, 0.0).then_inc(s_zero, 1)
            pool.wait_ge(s_zero, 1)
            pool.wait_ge(s_h2_store, 16 * TT)
            pool.wait_ge(s_tables, 1)

            def gather(column, b):
                pool.tensor_copy(g_cur[0:CAP, b:b + 1], g_idx[0:CAP, column]).then_inc(s_g_cur, 1)

            def gather_go(b):
                pool.indirect_dma_start(g_rows[:, b, :], None, h2_rows,
                                        bass.IndirectOffsetOnAxis(ap=g_cur[0:CAP, b:b + 1], axis=0),
                                        bounds_check=SEQ - 1, oob_is_err=False).then_inc(s_gather[b], 16)

            def scatter_go(b, done):
                pool.indirect_dma_start(y_rows, bass.IndirectOffsetOnAxis(ap=s_cur[:, b:b + 1], axis=0),
                                        y_item[:, b, :], None,
                                        bounds_check=4 * SEQ - 1, oob_is_err=False).then_inc(done, 16)

            for b in range(2):
                gather(slice(b, b + 1), b)
                pool.wait_ge(s_g_cur, b + 1)
                gather_go(b)
            pool.sem_inc(s_y_free, 2)
            pool.sem_inc(x_done, 1)
            with pool.Fori(0, N_IT) as it:
                for u in range(UNROLL):
                    b = u % 2
                    i = it * UNROLL + u
                    pool.wait_ge(s_xe_psum, i + 1)
                    pool.sem_inc(s_pool_turn, 1)
                    gather(bass.ds(i + 2, 1), b)
                    pool.wait_ge(s_g_cur, i + 3)
                    pool.sem_inc(s_pool_turn, 1)
                    gather_go(b)
                    pool.wait_ge(s_y_act, i + 2)
                    pool.sem_inc(s_pool_turn, 1)
                    pool.wait_ge(s_y_dve, i + 2)
                    pool.sem_inc(s_pool_turn, 1)
                    pool.tensor_copy(s_cur[:, b:b + 1], s_idx[:, bass.ds(i, 1)]).then_inc(s_s_cur, 1)
                    pool.wait_ge(s_s_cur, i + 1)
                    pool.sem_inc(s_pool_turn, 1)
                    scatter_go(b, s_scatter[b])
                    pool.wait_ge(s_scatter[b], it * 32 + 16 * (u // 2 + 1))
                    pool.sem_inc(s_y_free, 1)
            for b in range(2):
                pool.wait_ge(s_gather[b], 16 * (NE // 2 + 1))
                pool.wait_ge(s_scatter[b], 16 * (NE // 2))
            nx = pool.value_load(n_extra[0:1, 0:1], min_val=0, max_val=MAX_EXTRA)
            with pool.If(nx > 0):
                with pool.Fori(0, nx) as j:
                    pool.tensor_copy(g_cur[0:CAP, 0:1], g_idx[0:CAP, bass.ds(j + NE, 1)]).then_inc(x_gcur, 1)
                    pool.tensor_copy(s_cur[:, 0:1], s_idx[:, bass.ds(j + NE, 1)]).then_inc(x_gcur, 1)
                    pool.wait_ge(x_gcur, j * 2 + 2)
                    pool.sem_inc(s_pool_turn, 1)
                    pool.indirect_dma_start(g_rows[:, 0, :], None, h2_rows,
                                            bass.IndirectOffsetOnAxis(ap=g_cur[0:CAP, 0:1], axis=0),
                                            bounds_check=SEQ - 1, oob_is_err=False).then_inc(x_gather, 16)
                    pool.wait_ge(x_ya, j + 1)
                    pool.sem_inc(s_pool_turn, 1)
                    pool.wait_ge(x_yd, j + 1)
                    pool.sem_inc(s_pool_turn, 1)
                    scatter_go(0, x_scatter)
                    pool.wait_ge(x_scatter, j * 16 + 16)
                    pool.sem_inc(x_done, 1)

        @block.tensor
        def _(pe):
            pe.wait_ge(s_cst, 16)
            pe.wait_ge(s_xn, TT)
            for n in range(KC // 2):
                if n >= 4:
                    pe.wait_ge(s_xt_read, n - 3)
                for j in range(2):
                    for t in range(TT):
                        mm = pe.transpose(bank[n % 4][:, (2 * j + t) * P:(2 * j + t + 1) * P],
                                          x_rows[:, t, 2 * n + j::KC], ident)
                mm.then_inc(s_xt, 1)

            def take_turn(what):
                n = turn_no[what]
                if n >= 1:
                    pe.wait_ge(s_turn_read, n)

            def columns(i):
                take_turn(("col", i))
                pe.wait_ge(s_ada_used, KC // 2 * (i + 1))
                if i == 0:
                    pe.wait_ge(s_par, 16)
                m = MODS[i]
                pe.matmul(bank[6][:, 0:KC], ident, par[:, A_BADA + KC * m:A_BADA + KC * (m + 1)],
                          start=True, stop=False, skip_group_check=True)
                for k in range(KC):
                    mm = pe.matmul(bank[6][:, k:k + 1], acc[:, i % 2, k::KC], ones[:, 0:1],
                                   start=False, stop=(k == KC - 1), skip_group_check=True)
                mm.then_inc(s_turn, 1)

            def head_scores(h):
                hh = h % HG
                if hh == 0:
                    pe.wait_ge(s_block_act, 2 * (act_evac.index(3 + 5 * (h // HG) - 1) + 1))
                if h >= 1:
                    pe.wait_ge(s_shift, h)
                for m in range(2):
                    rows = slice(DK * m, DK * m + DK)
                    pe.matmul(bank[4 + m][:, 0:P], q_turned[rows, hh, 0:P], k_turned[rows, hh, 0:P],
                              start=True, stop=True)
                    mm = pe.matmul(bank[4 + m][:, P:P + SEQ], q_turned[rows, hh, P:SEQ], k_turned[rows, hh, :],
                                   start=True, stop=True)
                mm.then_inc(s_scores, 1)

            def head_turn(h):
                take_turn(("head", h))
                pe.wait_ge(s_a, h + 1)
                for j in range(3):
                    mm = pe.transpose(bank[6][:, j * P:(j + 1) * P], soft[:, 0, j * P:(j + 1) * P], ident)
                mm.then_inc(s_turn, 1)

            def head_out(h):
                hh = h % HG
                pe.wait_ge(s_turn_read, turn_no[("head", h)] + 1)
                if h >= 1:
                    pe.wait_ge(s_o_read, h)
                vh = slice(DV * hh, DV * hh + DV)
                pe.matmul(bank[7][:, 0:DV], a_turned[:, 0:P], v_rows[:, 0, vh], start=True, stop=True)
                pe.matmul(bank[7][:, DV:2 * DV], a_turned[:, P:2 * P], v_rows[:, 0, vh], start=True, stop=False)
                mm = pe.matmul(bank[7][:, DV:2 * DV], a_turned[:, 2 * P:3 * P], v_rows[:, 1, vh],
                               start=False, stop=True)
                mm.then_inc(s_o, 1)

            def finish(g):
                pe.wait_ge(s_o_norm, g + 1)
                for half in range(2):
                    take_turn(("fin", g, half))
                    for j in range(2):
                        for t in range(TT):
                            mm = pe.transpose(bank[6][:, (2 * j + t) * P:(2 * j + t + 1) * P],
                                              o_raw[:, 2 * half + j, t, :], ident)
                    mm.then_inc(s_turn, 1)

            def broadcast(which, col):
                for j in range(4):
                    take_turn(("bc", which, j))
                    for k in range(4):
                        mm = pe.matmul(bank[6][:, k * P:(k + 1) * P],
                                       col[:, 4 * j + k:4 * j + k + 1].to_broadcast([P, P]), ident,
                                       start=True, stop=True)
                    mm.then_inc(s_turn, 1)

            columns(0)
            columns(1)
            for s in range(NB * SUB):
                b, part = divmod(s, SUB)
                if s - 3 in SCORE_AT:
                    head_out(SCORE_AT[s - 3])
                if s - 2 in SCORE_AT:
                    head_turn(SCORE_AT[s - 2])
                if s in SCORE_AT:
                    head_scores(SCORE_AT[s])
                if s in FINISH_AT:
                    finish(FINISH_AT[s])
                if s in COLUMNS_AT:
                    columns(COLUMNS_AT[s])
                if s in BCAST_AT:
                    pe.wait_ge(s_cols, 2 + BCAST_AT[s])
                    broadcast(BCAST_AT[s], cols[:, 1 + BCAST_AT[s], :])
                if part == 0:
                    if b < 2:
                        pe.wait_ge(s_xt_read, KC // 2)
                    elif b - 2 in act_evac:
                        pe.wait_ge(s_block_act, 2 * (act_evac.index(b - 2) + 1))
                    else:
                        pe.wait_ge(s_block_dve, 2 * (dve_evac.index(b - 2) + 1))
                if b == 0:
                    pe.wait_ge(s_hT, 4 * (part + 1))
                if s == NB_IN * SUB:
                    pe.wait_ge(s_turn_read, turn_no[("fin", 1, 1)] + 1)
                if s == NB_IN * SUB + 2:
                    pe.wait_ge(s_block_dve, 2 * len(dve_evac))
                half = part // 2
                w = landed(pe, ("w", b, half)).rearrange("p (k n) -> p k n", k=8)
                lo, hi = bank[2 * (b % 2)], bank[2 * (b % 2) + 1]
                rows = b >= NB_IN or BLOCKS[b][0] == "v"
                src = y_turned if b >= NB_IN else h_turned
                for kk in range(4):
                    k = 4 * part + kk
                    wk = w[:, k % 8, :]
                    if rows:
                        for t in range(TT):
                            mm = pe.matmul((lo, hi)[t][:, :], src[:, k, t * P:(t + 1) * P], wk,
                                           start=(k == 0), stop=(k == KC - 1))
                    else:
                        for c in range(HG):
                            mm = pe.matmul((lo, hi)[c // 2][:, SEQ * (c % 2):SEQ * (c % 2) + SEQ],
                                           wk[:, P * c:P * c + P], src[:, k, :],
                                           start=(k == 0 and c % 2 == 0), stop=(k == KC - 1),
                                           skip_group_check=True)
                if part % 2 == 1:
                    mm.then_inc(s_w_used, 1)
            broadcast(2, mods[:, SH2, :])
            for t in range(TT):
                pe.wait_ge(s_h2, t + 1)
                for j in range(4):
                    n = 4 * t + j
                    if n < 4:
                        pe.wait_ge(s_block_act, 2 * len(act_evac))
                    else:
                        pe.wait_ge(s_h2t_read, n - 3)
                    for k in range(4):
                        mm = pe.transpose(bank[n % 4][:, k * P:(k + 1) * P], y_sb[:, t, 4 * j + k::KC], ident)
                    mm.then_inc(s_h2t, 1)
            h2_turned = y_turned
            pe.wait_ge(s_wr, 16)
            for t in range(TT):
                pe.wait_ge(s_h2t_read, 4 * (t + 1))
                for k in range(KC):
                    mm = pe.matmul(bank[4 + t][:, 0:36], h2_turned[:, k, t * P:(t + 1) * P], wr_sb[:, k, :],
                                   start=(k == 0), stop=(k == KC - 1))
            mm.then_inc(s_logit, 1)
            pe.wait_ge(s_cols, 4)
            broadcast(3, cols[:, 3, :])
            pe.wait_ge(s_picks, 1)
            pe.wait_ge(s_turn_read, N_TURNS_AFTER)
            both = rt[:, R_BOTH:R_BOTH + TT * NE].rearrange("p (t e) -> p t e", t=TT)
            pe.matmul(bank[6][:, 0:NE], tri, both[:, 0, :], start=True, stop=True)
            pe.matmul(bank[6][:, NE:2 * NE], tri, both[:, 1, :], start=True, stop=False)
            mm = pe.matmul(bank[6][:, NE:2 * NE], ones, both[:, 0, :], start=False, stop=True)
            for t in range(TT):
                mm = pe.matmul(bank[7][0:NE, 0:1], both[:, t, :], ones[:, 0:1], start=(t == 0), stop=(t == TT - 1))
            mm.then_inc(s_rank, 1)
            pe.wait_ge(s_extra, 1)
            extra = rt[0:NE, R_EXTRA:R_EXTRA + 1]
            pe.matmul(bank[7][:, 0:NE], extra.to_broadcast([NE, P]), tri[0:NE, 0:NE], start=True, stop=True)
            pe.matmul(bank[7][:, NE:NE + 1], extra.to_broadcast([NE, P]), ones[0:NE, 0:1],
                      start=True, stop=True).then_inc(s_base, 1)
            pe.wait_ge(s_hot, 1)
            for n in range(2 * TT):
                mm = pe.matmul(bank[7][:, 0:5 * ITEMS], hot_slot(n), hot_item(n).rearrange("p a b -> p (a b)"),
                               start=(n == 0), stop=(n == 2 * TT - 1))
            mm.then_inc(s_table, 1)

            def turn_rows(b):
                for k in range(KC):
                    mm = pe.transpose(bank[2 + k // 8][:, CAP * (k % 8):CAP * (k % 8) + CAP],
                                      g_rows[:, b, k::KC], ident[0:CAP, 0:CAP])
                return mm

            def gate_up(b, w, done):
                for k in range(KC):
                    if k % 8 == 0:
                        wg, wu = w(2 * (k // 8)), w(2 * (k // 8) + 1)
                    xk = xe_turned[:, b, k, :]
                    g = pe.matmul(bank[0][CAP:P, :], xk, wg[:, FE * (k % 8):FE * (k % 8 + 1)],
                                  start=(k == 0), stop=(k == KC - 1))
                    mm = pe.matmul(bank[0][0:CAP, :], xk, wu[:, FE * (k % 8):FE * (k % 8 + 1)],
                                   start=(k == 0), stop=(k == KC - 1))
                    if k % 8 == 7 and done is not None:
                        g.then_inc(done, 1)
                        mm.then_inc(done, 1)
                return mm

            def turn_act():
                for j in range(4):
                    mm = pe.transpose(bank[4][:, CAP * j:CAP * j + CAP], act_rows[:, j::4], ident[0:CAP, 0:CAP])
                return mm

            def down(w, done):
                for j in range(4):
                    if j % 2 == 0:
                        wd = w(4 + j // 2)
                    for n in range(2):
                        for half in range(2):
                            c0 = D * (j % 2) + 1024 * half + 512 * n
                            mm = pe.matmul(bank[5 + n][CAP * half:CAP * half + CAP, :], act_turned[:, j, :],
                                           wd[:, c0:c0 + 512], start=(j == 0), stop=(j == 3))
                    if j % 2 == 1 and done is not None:
                        mm.then_inc(done, 1)
                return mm

            pe.wait_ge(s_tables, 1)
            pe.wait_ge(s_gather[0], 16)
            turn_rows(0).then_inc(s_xe_psum, 1)
            with pe.Fori(0, N_IT) as it:
                for u in range(UNROLL):
                    i = it * UNROLL + u
                    b = u % 2

                    def weights(r):
                        n = 6 * u + r
                        pe.wait_ge(s_slot[n % RING], it * (16 * 6 * UNROLL // RING) + 16 * (USES0 + n // RING + 1))
                        return ring[:, n % RING, :]

                    pe.wait_ge(s_xe_act, i + 1)
                    pe.wait_ge(s_xe_dve, i + 1)
                    gate_up(b, weights, s_w_used)
                    pe.wait_ge(s_gather[1 - b], it * 32 + 16 * ((u + 1) // 2 + 1))
                    pe.sem_inc(s_pe_turn, 1)
                    turn_rows(1 - b).then_inc(s_xe_psum, 1)
                    pe.wait_ge(s_act_rows, i + 1)
                    pe.sem_inc(s_pe_turn, 1)
                    turn_act().then_inc(s_at_psum, 1)
                    pe.wait_ge(s_at, i + 1)
                    pe.wait_ge(s_y_act, i + 1)
                    pe.wait_ge(s_y_dve, i + 1)
                    down(weights, s_w_used)
            nx = pe.value_load(n_extra[0:1, 0:1], min_val=0, max_val=MAX_EXTRA)
            pe.wait_ge(s_xe_act, NE + 1)
            pe.wait_ge(s_xe_dve, NE + 1)
            pe.wait_ge(s_y_act, NE + 1)
            pe.wait_ge(s_y_dve, NE + 1)
            with pe.If(nx > 0):
                with pe.Fori(0, nx) as j:
                    def weights_x(r):
                        pe.wait_ge(x_load[r], j * 16 + 16)
                        return ring[:, r, :]

                    pe.wait_ge(x_gather, j * 16 + 16)
                    pe.sem_inc(s_pe_turn, 1)
                    turn_rows(0).then_inc(x_xe, 1)
                    pe.wait_ge(x_xe_act, j + 1)
                    pe.wait_ge(x_xe_dve, j + 1)
                    gate_up(0, weights_x, None).then_inc(x_gu, 1)
                    pe.wait_ge(x_rows_done, j + 1)
                    pe.sem_inc(s_pe_turn, 1)
                    turn_act().then_inc(x_at, 1)
                    pe.wait_ge(x_atc, j + 1)
                    down(weights_x, None).then_inc(x_dn, 1)

        @block.scalar
        def _(act):
            count = [0]

            def link(ins):
                count[0] += 1
                ins.then_inc(s_act, 1)
                act.wait_ge(s_act, count[0])

            act.dma_start(par[:, :], small).then_inc(s_par, 16)
            for t in range(TT):
                act.dma_start(x_rows[:, t, :], x_v[t]).then_inc(s_x[t], 16)
            act.dma_start(cst[:, :], consts).then_inc(s_cst, 16)
            act.dma_start(rt[:, 0:4 * DK], lam).then_inc(s_lam_in, 16)
            act.wait_ge(s_par, 16)
            act.wait_ge(s_cst, 16)
            act.activation(c_exp, par[:, A_C:A_C + KC], ACT.Exp, bias=zero, scale=-1.0).then_inc(s_cexp, 1)
            act.wait_ge(s_lam, 1)
            act.activation(lam_e, lam_s, ACT.Exp, bias=zero).then_inc(s_lam_e, 1)
            for t in range(TT):
                act.wait_ge(s_x[t], 16)
                act.activation(y_sb[:, t, :], x_rows[:, t, :], ACT.Square, bias=zero,
                               accum_out=ssq[:, t:t + 1]).then_inc(s_ssq, 1)
            act.wait_ge(s_ssq, TT)
            act.activation(rms, ssq, ACT.Sqrt, bias=eps_norm, scale=1.0 / D).then_inc(s_rms, 1)
            for n in range(KC // 2):
                act.wait_ge(s_xt, n + 1)
                act.activation(h_turned[:, 2 * n:2 * n + 2, :],
                               bank[n % 4][:, :].rearrange("p (j s) -> p j s", j=2),
                               ACT.Copy).then_inc(s_xt_read, 1)

            def read_turn(what, dst, src, scale=1.0):
                act.wait_ge(s_turn, turn_no[what] + 1)
                act.activation(dst, src, ACT.Copy, scale=scale).then_inc(s_turn_read, 1)

            def columns(i):
                read_turn(("col", i), mods[:, MODS[i], :], bank[6][:, 0:KC])

            def broadcast(which, row):
                v = row.rearrange("p (n k) -> p k n", k=KC)
                for j in range(4):
                    read_turn(("bc", which, j), v[:, 4 * j:4 * j + 4, :],
                              bank[6][:, :].rearrange("p (k n) -> p k n", k=4))

            def take_block(b):
                if b not in act_evac:
                    return
                act.wait_ge(s_w_used, 2 * (b + 1))
                banks = bank[2 * (b % 2)], bank[2 * (b % 2) + 1]
                kind, g = BLOCKS[b] if b < NB_IN else ("y", b - NB_IN)
                for n, pb in enumerate(banks):
                    two = pb[:, :].rearrange("p (c s) -> p c s", c=2)
                    if kind == "q":
                        act.activation(q_turned[:, 2 * n:2 * n + 2, :], two, ACT.Copy,
                                       scale=DK ** -0.5).then_inc(s_block_act, 1)
                    elif kind == "k":
                        act.activation(k_turned[:, 2 * n:2 * n + 2, :], two, ACT.Copy).then_inc(s_block_act, 1)
                    elif kind == "C":
                        c0 = HEADS + HG * g + 2 * n
                        act.activation(y_turned[:, c0:c0 + 2, :], two, ACT.Copy).then_inc(s_block_act, 1)
                    elif kind == "v":
                        act.activation(v_rows[:, n, :], pb[:, :], ACT.Copy).then_inc(s_block_act, 1)
                    else:
                        act.activation(y_sb[:, n, 512 * g:512 * g + 512], pb[:, :], ACT.Copy).then_inc(s_act, 1)
                        count[0] += 1
                        act.activation(rt[:, 0:512], pb[:, :], ACT.Square, bias=zero,
                                       accum_out=y_ss[:, n, g:g + 1]).then_inc(s_block_act, 1)
                        act.wait_ge(s_block_act, 2 * act_evac.index(b) + n + 1)

            def exps(h):
                act.wait_ge(s_shift, h + 1)
                for m in range(2):
                    for t in range(TT):
                        span = slice(0, P) if t == 0 else slice(P, P + SEQ)
                        n = 2 * m + t
                        ins = act.activation(soft[:, m, span], soft[:, m, span], ACT.Exp,
                                             bias=mx[:, n:n + 1], accum_out=p_sum[:, n:n + 1])
                ins.then_inc(s_prob, 1)

            columns(0)
            columns(1)
            for s in range(NB * SUB):
                b, part = divmod(s, SUB)
                if part == 0 and b >= 1:
                    take_block(b - 1)
                if s - 3 in SCORE_AT:
                    h = SCORE_AT[s - 3]
                    act.wait_ge(s_o, h + 1)
                    if h == HG:
                        act.wait_ge(s_turn, turn_no[("fin", 0, 1)] + 1)
                    act.activation(o_raw[:, h % HG, :, :], bank[7][:, 0:2 * DV].rearrange("p (t n) -> p t n", t=TT),
                                   ACT.Copy).then_inc(s_act, 1)
                    count[0] += 1
                    if h >= 1:
                        act.wait_ge(s_o_read, h)
                    for t in range(TT):
                        n = TT * (h % HG) + t
                        ins = act.activation(junk[:, 0:DV], bank[7][:, DV * t:DV * t + DV], ACT.Square, bias=zero,
                                             accum_out=o_ss[:, n:n + 1])
                        if t == 0:
                            link(ins)
                    ins.then_inc(s_o_read, 1)
                    if h % HG == HG - 1:
                        act.wait_ge(s_o_read, h + 1)
                        act.activation(o_ss[:, :], o_ss[:, :], ACT.Sqrt, bias=eps_subln,
                                       scale=1.0 / DV).then_inc(s_o_rms, 1)
                if s - 2 in SCORE_AT:
                    h = SCORE_AT[s - 2]
                    if h >= 1:
                        act.wait_ge(s_o, h)
                    read_turn(("head", h), a_turned[:, :], bank[6][:, 0:P + SEQ])
                if s in SCORE_AT:
                    exps(SCORE_AT[s])
                if s in FINISH_AT:
                    g = FINISH_AT[s]
                    for half in range(2):
                        c0 = HG * g + 2 * half
                        read_turn(("fin", g, half), y_turned[:, c0:c0 + 2, :],
                                  bank[6][:, :].rearrange("p (c s) -> p c s", c=2), scale=gsub)
                if s in COLUMNS_AT:
                    columns(COLUMNS_AT[s])
                if s == NB_IN * SUB + 1:
                    act.wait_ge(s_w_used, 2 * NB_IN)
                    for t in range(TT):
                        act.dma_start(x1[:, t, :], x_v[t]).then_inc(s_x[t], 16)
                    act.wait_ge(s_turn, turn_no[("head", HEADS - 1)] + 1)
                    act.dma_start(wr_sb, wrt.rearrange("(p k) n -> p k n", k=KC)).then_inc(s_wr, 16)
                if s in BCAST_AT:
                    broadcast(BCAST_AT[s], acc[:, BCAST_AT[s], :])
            take_block(NB - 1)
            act.wait_ge(s_ysum, 1)
            act.activation(yrms, yrms, ACT.Sqrt, bias=eps_norm, scale=1.0 / D).then_inc(s_yrms, 1)
            for t in range(TT):
                act.wait_ge(s_x1, t + 1)
                act.activation(y_sb[:, t, :], x1[:, t, :], ACT.Square, bias=zero,
                               accum_out=h2rms[:, t:t + 1]).then_inc(s_xsq, 1)
                act.wait_ge(s_xsq, t + 1)
                act.activation(h2rms[:, t:t + 1], h2rms[:, t:t + 1], ACT.Sqrt, bias=eps_norm,
                               scale=1.0 / D).then_inc(s_h2rms, 1)
                if t == TT - 1:
                    broadcast(2, acc[:, 0, :])
            for t in range(TT):
                act.wait_ge(s_h2, t + 1)
                act.dma_start(h2_rows[t * P:(t + 1) * P, :], y_sb[:, t, :]).then_inc(s_h2_store, 16)
                for j in range(4):
                    act.wait_ge(s_h2t, 4 * t + j + 1)
                    act.activation(y_turned[:, 4 * j:4 * j + 4, t * P:(t + 1) * P],
                                   bank[(4 * t + j) % 4][:, :].rearrange("p (k s) -> p k s", k=4),
                                   ACT.Copy).then_inc(s_h2t_read, 1)
            broadcast(3, acc[:, 1, :])
            act.wait_ge(s_gexp_in, 1)
            act.activation(rt[:, R_EXP:R_EXP + TT * 5], rt[:, R_EXP:R_EXP + TT * 5], ACT.Exp,
                           bias=zero).then_inc(s_gexp, 1)

            def xe_copy(b):
                return act.activation(xe_turned[:, b, 0:8, :], bank[2][:, :].rearrange("p (k s) -> p k s", k=8),
                                      ACT.Copy)

            def silu():
                return act.activation(silu_g, bank[0][CAP:P, :], ACT.Silu, bias=zero[0:CAP, :])

            def turned_copy():
                return act.activation(act_turned, bank[4][:, 0:4 * CAP].rearrange("p (j s) -> p j s", j=4), ACT.Copy)

            def y_copy(b):
                return act.activation(y_item[:, b, 0:512], bank[5][:, :], ACT.Copy)

            act.wait_ge(s_h2_store, 16 * TT)
            act.wait_ge(s_xe_psum, 1)
            xe_copy(0).then_inc(s_xe_act, 1)
            act.sem_inc(s_y_act, 1)
            with act.Fori(0, N_IT) as it:
                for u in range(UNROLL):
                    i = it * UNROLL + u
                    b = u % 2
                    act.wait_ge(s_w_used, it * (6 * UNROLL) + W_USED0 + 6 * u + 4)
                    silu().then_inc(s_silu_g, 1)
                    act.wait_ge(s_xe_psum, i + 2)
                    xe_copy(1 - b).then_inc(s_xe_act, 1)
                    act.wait_ge(s_at_psum, i + 1)
                    turned_copy().then_inc(s_at, 1)
                    act.wait_ge(s_w_used, it * (6 * UNROLL) + W_USED0 + 6 * u + 6)
                    act.wait_ge(s_y_free, i + 1)
                    y_copy(b).then_inc(s_y_act, 1)
            nx = act.value_load(n_extra[0:1, 0:1], min_val=0, max_val=MAX_EXTRA)
            with act.If(nx > 0):
                act.wait_ge(s_scatter[0], 16 * (NE // 2))
                with act.Fori(0, nx) as j:
                    act.wait_ge(x_xe, j + 1)
                    xe_copy(0).then_inc(x_xe_act, 1)
                    act.wait_ge(x_gu, j + 1)
                    silu().then_inc(x_silu, 1)
                    act.wait_ge(x_at, j + 1)
                    turned_copy().then_inc(x_atc, 1)
                    act.wait_ge(x_dn, j + 1)
                    y_copy(0).then_inc(x_ya, 1)

            for t in range(TT):
                act.wait_ge(s_fsum, t + 1)
                act.activation(ring[:, t, D:2 * D], ring[:, t, 0:D], ACT.Square, bias=zero,
                               accum_out=f_ss[:, t:t + 1]).then_inc(s_fsq, 1)
                act.wait_ge(s_fsq, t + 1)
                act.activation(f_ss[:, t:t + 1], f_ss[:, t:t + 1], ACT.Sqrt, bias=eps_norm,
                               scale=1.0 / D).then_inc(s_frms, 1)

        @block.vector
        def _(dve):
            count = [0]

            def link(ins):
                count[0] += 1
                ins.then_inc(s_dve, 1)
                dve.wait_ge(s_dve, count[0])

            def ada(i, r):
                if r == 0 and i >= 2:
                    dve.wait_ge(s_turn, turn_no[("col", i - 2)] + 1)
                w = landed(dve, ("ada", i, r)).rearrange("p (k n) -> p k n", k=2)
                a = acc[:, i % 2, :]
                sc = silu_c[:, 2 * r:2 * r + 1]
                if r == 0:
                    link(dve.tensor_scalar(a, w[:, 0, :], sc, None, ALU.mult))
                else:
                    link(dve.scalar_tensor_tensor(a, w[:, 0, :], sc, a, ALU.mult, ALU.add))
                dve.scalar_tensor_tensor(a, w[:, 1, :], silu_c[:, 2 * r + 1:2 * r + 2], a, ALU.mult,
                                         ALU.add).then_inc(s_ada_used, 1)
                dve.wait_ge(s_ada_used, KC // 2 * i + r + 1)

            dve.wait_ge(s_cexp, 1)
            link(dve.tensor_scalar(c_exp, c_exp, 1.0, None, ALU.add))
            link(dve.reciprocal(c_exp, c_exp))
            link(dve.tensor_tensor(silu_c, c_exp, par[:, A_C:A_C + KC], ALU.mult))
            dve.wait_ge(s_lam_in, 16)
            for n in range(2):
                ins = dve.tensor_tensor_reduce(junk[:, 0:DK], rt[:, 2 * DK * n:2 * DK * n + DK],
                                               rt[:, 2 * DK * n + DK:2 * DK * (n + 1)], 1.0, 0.0,
                                               ALU.mult, ALU.add, lam_s[:, n:n + 1])
                if n == 0:
                    link(ins)
            ins.then_inc(s_lam, 1)
            ada(0, 0)
            dve.wait_ge(s_lam_e, 1)
            link(dve.scalar_tensor_tensor(neg_lam, lam_e[:, 1:2], LAM_INIT, lam_e[:, 0:1],
                                          ALU.subtract, ALU.subtract))
            link(dve.tensor_scalar(gsub, par[:, A_GSUB:A_GSUB + 1], 1.0 - LAM_INIT, None, ALU.mult))
            ada(0, 1)
            dve.wait_ge(s_rms, 1)
            link(dve.reciprocal(xrms, rms))
            for t in range(TT):
                dve.tensor_scalar(x_rows[:, t, :], x_rows[:, t, :], xrms[:, t:t + 1], None,
                                  ALU.mult).then_inc(s_xn, 1)
            for r in range(2, KC // 2):
                ada(0, r)

            def col_ready(i):
                dve.wait_ge(s_turn_read, turn_no[("col", i)] + 1)

            for r in range(KC // 2):
                ada(1, r)
                if r == 2:
                    col_ready(0)
                    link(dve.scalar_tensor_tensor(cols[:, 0, :], mods[:, SC1, :], 1.0,
                                                  par[:, A_GPRE1:A_GPRE1 + KC], ALU.add, ALU.mult))
            col_ready(1)
            dve.wait_ge(s_xt_read, KC // 2)
            for k in range(KC):
                dve.tensor_scalar(h_turned[:, k, :], h_turned[:, k, :], cols[:, 0, k:k + 1],
                                  mods[:, SH1, k:k + 1], ALU.mult, ALU.add).then_inc(s_hT, 1)

            def shift(h):
                dve.wait_ge(s_scores, h + 1)
                for m in range(2):
                    link(dve.scalar_tensor_tensor(soft[:, m, :], dist, -(0.5 ** (8.0 / HEADS)) ** (h + 1),
                                                  bank[4 + m][:, 0:P + SEQ], ALU.mult, ALU.add))
                link(dve.tensor_reduce(mx[:, 0::2], soft[:, :, 0:P], AX_X, ALU.max))
                link(dve.tensor_reduce(mx[:, 1::2], soft[:, :, P:P + SEQ], AX_X, ALU.max))
                dve.tensor_scalar(mx[:, :], mx[:, :], -1.0, None, ALU.mult).then_inc(s_shift, 1)

            def combine(h):
                dve.wait_ge(s_prob, h + 1)
                link(dve.reciprocal(p_rec[:, :], p_sum[:, :]))
                link(dve.tensor_scalar(p_rec[:, 2:4], p_rec[:, 2:4], neg_lam, None, ALU.mult))
                for t, span in enumerate((slice(0, P), slice(P, P + SEQ))):
                    link(dve.tensor_scalar(soft[:, 1, span], soft[:, 1, span], p_rec[:, 2 + t:3 + t], None, ALU.mult))
                    ins = dve.scalar_tensor_tensor(soft[:, 0, span], soft[:, 0, span], p_rec[:, t:t + 1],
                                                   soft[:, 1, span], ALU.mult, ALU.add)
                    if t == 0:
                        link(ins)
                ins.then_inc(s_a, 1)

            def norm_heads(g):
                dve.wait_ge(s_o_rms, g + 1)
                link(dve.reciprocal(o_rec[:, :], o_ss[:, :]))
                for h in range(HG):
                    for t in range(TT):
                        n = TT * h + t
                        ins = dve.tensor_scalar(o_raw[:, h, t, :], o_raw[:, h, t, :], o_rec[:, n:n + 1], None,
                                                ALU.mult)
                        if n < HG * TT - 1:
                            link(ins)
                ins.then_inc(s_o_norm, 1)

            def take_block(b):
                if b not in dve_evac:
                    return
                kind, g = BLOCKS[b]
                dve.wait_ge(s_w_used, 2 * (b + 1))
                c0 = HEADS + HG * g
                if kind == "X":
                    dve.wait_ge(s_block_act, 2 * (act_evac.index(b - 1) + 1))
                    link(dve.memset(conv_in[:, :, 0:2], 0.0))
                for n in range(2):
                    two = bank[2 * (b % 2) + n][:, :].rearrange("p (c s) -> p c s", c=2)
                    yc = y_turned[:, c0 + 2 * n:c0 + 2 * n + 2, :]
                    dst = conv_in[:, 2 * n:2 * n + 2, 2:] if kind == "X" else yc
                    dve.tensor_tensor(dst, two, yc, ALU.mult).then_inc(s_block_dve, 1)
                dve.wait_ge(s_block_dve, 2 * (dve_evac.index(b) + 1))
                if kind == "X":
                    for c in range(HG):
                        y = y_turned[:, c0 + c, :]
                        for i in range(3):
                            w = par[:, A_WCONV + HEADS * i + HG * g + c:A_WCONV + HEADS * i + HG * g + c + 1]
                            z = conv_in[:, c, i:i + SEQ]
                            if i == 0:
                                link(dve.tensor_scalar(y, z, w, None, ALU.mult))
                            else:
                                link(dve.scalar_tensor_tensor(y, z, w, y, ALU.mult, ALU.add))

            late = {}
            for n, what in enumerate(PLAN):
                if what[0] == "w":
                    last = 2 * (2 * what[1] + what[2])
                elif what[1] >= 2:
                    late[last + len([1 for q in late.values() if q[0] == last])] = (last, what)
            for s in range(NB * SUB):
                b, part = divmod(s, SUB)
                if part == 0 and b >= 1:
                    take_block(b - 1)
                if s - 1 in SCORE_AT:
                    combine(SCORE_AT[s - 1])
                if s in SCORE_AT:
                    shift(SCORE_AT[s])
                if s + 1 in FINISH_AT:
                    norm_heads(FINISH_AT[s + 1])
                if s - 1 in COLUMNS_AT:
                    i = COLUMNS_AT[s - 1]
                    if i == 2:
                        col_ready(i)
                        dve.tensor_tensor(cols[:, 1, :], mods[:, GT1, :], par[:, A_GPOST1:A_GPOST1 + KC],
                                          ALU.mult).then_inc(s_cols, 2)
                    if i == 4:
                        col_ready(i)
                        dve.scalar_tensor_tensor(cols[:, 2, :], mods[:, SC2, :], 1.0,
                                                 par[:, A_GPRE2:A_GPRE2 + KC], ALU.add, ALU.mult).then_inc(s_cols, 1)
                    if i == 5:
                        col_ready(i)
                        dve.tensor_tensor(cols[:, 3, :], mods[:, GT2, :], par[:, A_GPOST2:A_GPOST2 + KC],
                                          ALU.mult).then_inc(s_cols, 1)
                if s in late:
                    ada(late[s][1][1], late[s][1][2])

            dve.wait_ge(s_block_act, 2 * len(act_evac))
            dve.tensor_reduce(yrms, y_ss[:, :, :], AX_X, ALU.add).then_inc(s_ysum, 1)
            dve.wait_ge(s_yrms, 1)
            link(dve.reciprocal(yrms, yrms))
            dve.wait_ge(s_turn_read, turn_no[("bc", 1, 3)] + 1)
            for t in range(TT):
                dve.wait_ge(s_x[t], 32)
                link(dve.scalar_tensor_tensor(y_sb[:, t, :], y_sb[:, t, :], yrms[:, t:t + 1], acc[:, 0, :],
                                              ALU.mult, ALU.mult))
                dve.tensor_tensor(x1[:, t, :], x1[:, t, :], y_sb[:, t, :], ALU.add).then_inc(s_x1, 1)
            dve.wait_ge(s_turn_read, turn_no[("bc", 2, 3)] + 1)
            for t in range(TT):
                dve.wait_ge(s_h2rms, t + 1)
                link(dve.reciprocal(h2rms[:, t:t + 1], h2rms[:, t:t + 1]))
                link(dve.scalar_tensor_tensor(y_sb[:, t, :], x1[:, t, :], h2rms[:, t:t + 1], acc[:, 1, :],
                                              ALU.mult, ALU.mult))
                dve.tensor_tensor(y_sb[:, t, :], y_sb[:, t, :], acc[:, 0, :], ALU.add).then_inc(s_h2, 1)

            logit = rt[:, R_LOGIT:R_LOGIT + TT * 36].rearrange("p (t n) -> p t n", t=TT)
            outer = rt[:, R_OUTER:R_OUTER + TT * NE].rearrange("p (t g j) -> p t g j", t=TT, g=N_GROUPS)
            picked = rt[:, R_PICKED:R_PICKED + TT * 8].rearrange("p (t j) -> p t j", t=TT)
            same4 = rt[:, R_SAME4:R_SAME4 + TT * 4].rearrange("p (t g) -> p t g", t=TT)
            group = rt[:, R_GROUP:R_GROUP + TT * 4].rearrange("p (t g) -> p t g", t=TT)
            same8 = rt[:, R_SAME8:R_SAME8 + TT * 8].rearrange("p (t j) -> p t j", t=TT)
            inner = rt[:, R_INNER:R_INNER + 2 * TT * 8].rearrange("p (k t j) -> p k t j", k=2, t=TT)
            top = rt[:, R_MAX:R_MAX + 6 * TT].rearrange("p (n t) -> p n t", t=TT)
            exps = rt[:, R_EXP:R_EXP + TT * 5].rearrange("p (t n) -> p t n", t=TT)
            wts = rt[:, R_W:R_W + 2 * TT].rearrange("p (k t) -> p k t", k=2)
            hot = rt[:, R_HOT:R_HOT + 2 * TT * NE].rearrange("p (k t e) -> p k t e", k=2, t=TT)
            both = rt[:, R_BOTH:R_BOTH + TT * NE].rearrange("p (t e) -> p t e", t=TT)
            prod = rt[:, R_PROD:R_PROD + 6 * TT * NE].rearrange("p (n k t e) -> p n k t e", n=3, k=2, t=TT)
            red = rt[:, R_RED:R_RED + 6 * TT]
            pos = rt[:, R_POS:R_POS + 10 * TT]
            kt = 2 * TT

            def over(ap2, n):
                return ap2.unsqueeze(2).to_broadcast([P, TT, n])

            def first_of(values, n, maxima, same, hot_out, priority):
                link(dve.tensor_reduce(maxima, values, AX_X, ALU.max))
                link(dve.tensor_tensor(same, values, over(maxima, n), ALU.is_equal))
                link(dve.tensor_tensor(same, same, priority.unsqueeze(1).to_broadcast([P, TT, n]), ALU.mult))
                link(dve.tensor_reduce(top[:, 3, :], same, AX_X, ALU.max))
                link(dve.tensor_tensor(hot_out, same, over(top[:, 3, :], n), ALU.is_equal))

            dve.wait_ge(s_logit, 1)
            for t in range(TT):
                link(dve.tensor_tensor(logit[:, t, :], bank[4 + t][:, 0:36], par[:, A_BRT:A_BRT + 36], ALU.add))
            pri4 = cst[:, C_PRI4:C_PRI4 + 4]
            pri8 = cst[:, C_PRI8:C_PRI8 + 8]
            first_of(logit[:, :, 0:4], 4, top[:, 0, :], same4, group, pri4)
            link(dve.tensor_tensor(exps[:, :, 0:4], logit[:, :, 0:4], over(top[:, 0, :], 4), ALU.subtract))
            for t in range(TT):
                link(dve.tensor_tensor(outer[:, t, :, :],
                                       logit[:, t, 4:36].rearrange("p (g j) -> p g j", g=N_GROUPS),
                                       group[:, t, :].unsqueeze(2).to_broadcast([P, N_GROUPS, 8]), ALU.mult))
            link(dve.tensor_reduce(picked, outer.rearrange("p t g j -> p t j g"), AX_X, ALU.add))
            first_of(picked, 8, top[:, 1, :], same8, inner[:, 0, :, :], pri8)
            link(dve.scalar_tensor_tensor(picked, inner[:, 0, :, :], -1e30, picked, ALU.mult, ALU.add))
            first_of(picked, 8, top[:, 2, :], same8, inner[:, 1, :, :], pri8)
            dve.tensor_tensor(exps[:, :, 4:5], over(top[:, 2, :], 1), over(top[:, 1, :], 1),
                              ALU.subtract).then_inc(s_gexp_in, 1)
            for k in range(2):
                for t in range(TT):
                    link(dve.tensor_tensor(hot[:, k, t, :].rearrange("p (g j) -> p g j", g=N_GROUPS),
                                           group[:, t, :].unsqueeze(2).to_broadcast([P, N_GROUPS, 8]),
                                           inner[:, k, t, :].unsqueeze(1).to_broadcast([P, N_GROUPS, 8]), ALU.mult))
            dve.tensor_tensor(both, hot[:, 0, :, :], hot[:, 1, :, :], ALU.add).then_inc(s_picks, 1)
            dve.wait_ge(s_gexp, 1)
            link(dve.tensor_reduce(top[:, 4, :], exps[:, :, 0:4], AX_X, ALU.add))
            link(dve.tensor_scalar(top[:, 5, :].unsqueeze(2), exps[:, :, 4:5], 1.0, None, ALU.add))
            link(dve.tensor_tensor(top[:, 4, :], top[:, 4, :], top[:, 5, :], ALU.mult))
            link(dve.reciprocal(wts[:, 0, :], top[:, 4, :]))
            link(dve.tensor_tensor(wts[:, 1, :].unsqueeze(2), wts[:, 0, :].unsqueeze(2), exps[:, :, 4:5], ALU.mult))
            dve.wait_ge(s_rank, 1)
            n_e = bank[7][0:NE, 0:1]
            extra = rt[0:NE, R_EXTRA:R_EXTRA + 1]
            n_sb = rt[0:NE, R_EXTRA + 1:R_EXTRA + 2]
            link(dve.tensor_copy(n_sb, n_e))
            link(dve.tensor_scalar(extra, n_sb, CAP + 0.5, None, ALU.is_ge))
            link(dve.scalar_tensor_tensor(extra, n_sb, 2 * CAP + 0.5, extra, ALU.is_ge, ALU.add))
            dve.scalar_tensor_tensor(extra, n_sb, 3 * CAP + 0.5, extra, ALU.is_ge, ALU.add).then_inc(s_extra, 1)
            for k in range(2):
                link(dve.tensor_tensor(prod[:, 0, k, :, :], hot[:, k, :, :],
                                       bank[6][:, 0:TT * NE].rearrange("p (t e) -> p t e", t=TT), ALU.mult))
                link(dve.tensor_tensor(prod[:, 2, k, :, :], hot[:, k, :, :],
                                       cst[:, C_IOTA:C_IOTA + NE].unsqueeze(1).to_broadcast([P, TT, NE]), ALU.mult))
            dve.wait_ge(s_base, 1)
            for k in range(2):
                link(dve.tensor_tensor(prod[:, 1, k, :, :], hot[:, k, :, :],
                                       bank[7][:, 0:NE].unsqueeze(1).to_broadcast([P, TT, NE]), ALU.mult))
            link(dve.tensor_copy(n_extra[:, :], bank[7][:, NE:NE + 1]))
            link(dve.tensor_reduce(red, prod.rearrange("p n k t e -> p (n k t) e"), AX_X, ALU.add))
            rank, base, expert = red[:, 0:kt], red[:, kt:2 * kt], red[:, 2 * kt:3 * kt]
            lot, beyond, dlt, slot, item = (pos[:, kt * n:kt * (n + 1)] for n in range(5))
            link(dve.tensor_scalar(beyond, rank, CAP - 0.5, None, ALU.is_ge))
            link(dve.scalar_tensor_tensor(lot, rank, 2 * CAP - 0.5, beyond, ALU.is_ge, ALU.add))
            link(dve.scalar_tensor_tensor(lot, rank, 3 * CAP - 0.5, lot, ALU.is_ge, ALU.add))
            link(dve.scalar_tensor_tensor(slot, lot, -float(CAP), rank, ALU.mult, ALU.add))
            link(dve.tensor_tensor(dlt, base, lot, ALU.add))
            link(dve.scalar_tensor_tensor(dlt, dlt, NE - 1.0, expert, ALU.add, ALU.subtract))
            link(dve.tensor_tensor(dlt, dlt, beyond, ALU.mult))
            link(dve.tensor_tensor(item, dlt, expert, ALU.add))
            for n in range(kt):
                k, t = divmod(n, TT)
                link(dve.tensor_scalar(hot_slot(n), cst[:, C_SLOT:C_SLOT + P], slot[:, n:n + 1], None, ALU.is_equal))
                hi = hot_item(n)
                link(dve.tensor_scalar(hi[:, 3, :], cst[:, C_IOTA:C_IOTA + ITEMS], item[:, n:n + 1], None, ALU.is_equal))
                for col, val in ((0, cst[:, C_TOK + t:C_TOK + t + 1]), (1, cst[:, C_OUT + n:C_OUT + n + 1]),
                                 (2, wts[:, k, t:t + 1]), (4, expert[:, n:n + 1])):
                    ins = dve.tensor_scalar(hi[:, col, :], hi[:, 3, :], val, None, ALU.mult)
                    if (n, col) != (kt - 1, 4):
                        link(ins)
            ins.then_inc(s_hot, 1)
            dve.wait_ge(s_table, 1)
            table = acc[:, 0, T_TABLE:T_TABLE + 5 * ITEMS].rearrange("p (a b) -> p a b", a=5)
            miss = acc[:, 0, T_MISS:T_MISS + ITEMS]
            row = acc[:, 0, T_MISS + ITEMS:T_MISS + 2 * ITEMS]
            link(dve.tensor_copy(table, bank[7][:, 0:5 * ITEMS].rearrange("p (a b) -> p a b", a=5)))
            link(dve.tensor_scalar(miss, table[:, 3, :], -NOWHERE, NOWHERE, ALU.mult, ALU.add))
            link(dve.tensor_tensor(g_idx[:, :], table[:, 0, :], miss, ALU.add))
            link(dve.scalar_tensor_tensor(row, table[:, 1, :], 2.0, miss, ALU.mult, ALU.add))
            link(dve.tensor_scalar(s_idx[:, :], row, cst[:, C_GRP:C_GRP + 1], None, ALU.add))
            link(dve.tensor_copy(e_idx[:, :], table[:, 4, :]))
            dve.tensor_copy(weight[:, :], table[:, 2, :]).then_inc(s_tables, 1)
            dve.wait_ge(s_tables, 1)

            def xe_copy(b):
                return dve.tensor_copy(xe_turned[:, b, 8:16, :], bank[3][:, :].rearrange("p (k s) -> p k s", k=8))

            def weigh(column):
                return dve.scalar_tensor_tensor(act_rows, silu_g, weight[0:CAP, column], bank[0][0:CAP, :],
                                                ALU.mult, ALU.mult)

            def y_copy(b):
                return dve.tensor_copy(y_item[:, b, 512:1024], bank[6][:, :])

            dve.wait_ge(s_h2_store, 16 * TT)
            dve.wait_ge(s_xe_psum, 1)
            xe_copy(0).then_inc(s_xe_dve, 1)
            dve.sem_inc(s_y_dve, 1)
            with dve.Fori(0, N_IT) as it:
                for u in range(UNROLL):
                    i = it * UNROLL + u
                    b = u % 2
                    dve.wait_ge(s_silu_g, i + 1)
                    weigh(bass.ds(i, 1)).then_inc(s_act_rows, 1)
                    dve.wait_ge(s_xe_psum, i + 2)
                    xe_copy(1 - b).then_inc(s_xe_dve, 1)
                    dve.wait_ge(s_w_used, it * (6 * UNROLL) + W_USED0 + 6 * u + 6)
                    dve.wait_ge(s_y_free, i + 1)
                    y_copy(b).then_inc(s_y_dve, 1)
            nx = dve.value_load(n_extra[0:1, 0:1], min_val=0, max_val=MAX_EXTRA)
            with dve.If(nx > 0):
                dve.wait_ge(s_scatter[0], 16 * (NE // 2))
                with dve.Fori(0, nx) as j:
                    dve.wait_ge(x_xe, j + 1)
                    xe_copy(0).then_inc(x_xe_dve, 1)
                    dve.wait_ge(x_silu, j + 1)
                    weigh(bass.ds(j + NE, 1)).then_inc(x_rows_done, 1)
                    dve.wait_ge(x_dn, j + 1)
                    y_copy(0).then_inc(x_yd, 1)
            for t in range(TT):
                dve.wait_ge(s_pair[t], 16)
                dve.tensor_tensor(ring[:, t, 0:D], ring[:, t, 0:D], ring[:, t, D:2 * D], ALU.add).then_inc(s_fsum, 1)
            for t in range(TT):
                dve.wait_ge(s_frms, t + 1)
                link(dve.reciprocal(f_ss[:, t:t + 1], f_ss[:, t:t + 1]))
                link(dve.scalar_tensor_tensor(ring[:, t, 0:D], ring[:, t, 0:D], f_ss[:, t:t + 1], acc[:, 1, :],
                                              ALU.mult, ALU.mult))
                dve.tensor_tensor(x1[:, t, :], x1[:, t, :], ring[:, t, 0:D], ALU.add).then_inc(s_fin, 1)


def constants():
    import numpy as np
    c = np.zeros((P, C_ALL), np.float32)
    p = np.arange(P)
    c[:, C_ID:C_ID + P] = np.eye(P)
    c[:, C_TRI:C_TRI + P] = p[:, None] < p[None, :]
    c[:, C_ONE:C_ONE + P] = 1.0
    for t, (c0, n) in enumerate(((C_DIST, P), (C_DIST + P, SEQ))):
        q, k = t * P + p[:, None], np.arange(n)[None, :]
        c[:, c0:c0 + n] = np.where(k // CHUNK <= q // CHUNK, np.abs(q - k), 1e37)
    c[:, C_SLOT:C_SLOT + P] = p % CAP
    c[:, C_IOTA:C_IOTA + ITEMS] = np.arange(ITEMS)
    c[:, C_PRI8:C_PRI8 + 8] = 8 - np.arange(8)
    c[:, C_PRI4:C_PRI4 + 4] = 4 - np.arange(4)
    for n in range(2 * TT):
        c[:, C_OUT + n] = n * P + p
    for t in range(TT):
        c[:, C_TOK + t] = t * P + p
    c[:, C_GRP] = p >= CAP
    c[:, C_EPS] = NORM_EPS
    c[:, C_EPS + 1] = SUBLN_EPS
    return c


def kernel(**inputs):
    import numpy as np
    import concourse.bacc as bacc
    from concourse.bass_utils import run_bass_kernel_spmd

    a = {name: np.asarray(v) for name, v in inputs.items()}

    def column(v):
        return v.reshape(P, KC)

    def over_partitions(v):
        return np.broadcast_to(v.reshape(1, -1), (P, v.size))

    small = np.concatenate([
        column(a["c"][0]), column(a["g_pre1"][0]), column(a["g_post1"][0]), column(a["g_pre2"][0]),
        column(a["g_post2"][0]),
        a["b_ada"][0].reshape(6, P, KC).transpose(1, 0, 2).reshape(P, 6 * KC),
        a["w_conv"][0].reshape(3, HEADS, P).transpose(2, 0, 1).reshape(P, 3 * HEADS),
        a["g_subln"][0].reshape(P, 1),
        over_partitions(a["b_router_g"][0]), over_partitions(a["b_router_e"][0])], axis=1)
    lam = over_partitions(np.concatenate([a[n][0] for n in ("lam_q1", "lam_k1", "lam_q2", "lam_k2")]))
    router = np.concatenate([a["w_router_g"][0], a["w_router_e"][0].reshape(D, NE)], axis=1)
    feeds = {"consts": constants(), "small": small, "lam": lam, "router": router}
    feeds.update({n: a[n] for n in ("x", "w_ada", "w_in", "w_out", "w_gate", "w_up", "w_down")})

    nc = bacc.Bacc("TRN2", target_bir_lowering=False, num_devices=1)
    arrays, args = {}, []
    for name, v in feeds.items():
        v = np.ascontiguousarray(v)
        arrays[name + "_dram"] = v
        args.append(nc.dram_tensor(name + "_dram", v.shape, mybir.dt.from_np(v.dtype), kind="ExternalInput").ap())
    args.append(nc.dram_tensor("out_dram", (1, SEQ, D), F32, kind="ExternalOutput").ap())
    hybrid_layer(nc, *args)
    r = run_bass_kernel_spmd(nc, [arrays], core_ids=[0])
    return r.results[0]["out_dram"]
```

```python
import math
from contextlib import ExitStack

import concourse.bass as bass
from concourse import mybir

ALU = mybir.AluOpType
ACT = mybir.ActivationFunctionType
F32 = mybir.dt.float32
F32R = mybir.dt.float32r
I32 = mybir.dt.int32
U32 = mybir.dt.uint32
AX_X = mybir.AxisListType.X

P = 128
D = 2048
SEQ = 256
TT = SEQ // P
KC = D // P
KH = KC // 2
HEADS = 8
DK = 64
DV = 128
HG = 4
N_GROUPS = 4
PER_GROUP = 8
NE = N_GROUPS * PER_GROUP
FE = 512
CHUNK = 64
LAM_INIT = 0.8 - 0.6 * math.exp(-0.3 * 0)
NORM_EPS = 1e-6
SUBLN_EPS = 1e-5
CAP = 48
UPPER = 64
MAX_EXTRA = (2 * SEQ - NE) // CAP
ITEMS = NE + MAX_EXTRA
PAIR = UPPER + CAP
NOWHERE = 4096.0

RING = 8
RING1 = 6
SPARE = RING - RING1
HI_SLOT, LO_SLOT = RING1, RING1 + 1
SLOT = 4096
UNROLL = 4

C_ID = 0
C_TRI = C_ID + P
C_ONE = C_TRI + P
C_DIST = C_ONE + P
C_SLOT = C_DIST + P + SEQ
C_IOTA = C_SLOT + P
C_PRI8 = C_IOTA + ITEMS
C_PRI4 = C_PRI8 + 8
C_TOK = C_PRI4 + 4
C_OUT = C_TOK + TT
C_GRP = C_OUT + 2 * TT
C_TILE = C_GRP + 1
C_ALL = C_TILE + 1
A_C = 0
A_GPRE1 = A_C + KC
A_GPOST1 = A_GPRE1 + KC
A_GPRE2 = A_GPOST1 + KC
A_GPOST2 = A_GPRE2 + KC
A_BADA = A_GPOST2 + KC
A_WCONV = A_BADA + 6 * KC
A_GSUB = A_WCONV + 3 * HEADS
A_BRT = A_GSUB + 1
A_EPS = A_BRT + N_GROUPS + NE
A_ALL = A_EPS + 3

R_LOGIT = 0
R_OUTER = R_LOGIT + TT * (N_GROUPS + NE)
R_PICKED = R_OUTER + TT * NE
R_SAME4 = R_PICKED + TT * 8
R_GROUP = R_SAME4 + TT * 4
R_SAME8 = R_GROUP + TT * 4
R_INNER = R_SAME8 + TT * 8
R_MAX = R_INNER + 2 * TT * 8
R_EXP = R_MAX + 6 * TT
R_W = R_EXP + TT * 5
R_HOT = R_W + 2 * TT
R_BOTH = R_HOT + 2 * TT * NE
R_PROD = R_BOTH + TT * NE
R_RED = R_PROD + 3 * 2 * TT * NE
R_POS = R_RED + 3 * 2 * TT
R_EXTRA = R_POS + 5 * 2 * TT
R_ALL = R_EXTRA + 2
assert R_ALL <= HG * TT * DV
T_SLOT = 0
T_ITEM = T_SLOT + 2 * TT * P
T_TABLE = T_ITEM + 2 * TT * 5 * ITEMS
T_MISS = T_TABLE + 5 * ITEMS
assert T_MISS + 2 * ITEMS <= D

BLOCKS = [("q", 0), ("k", 0), ("v", 0), ("C", 0), ("X", 0), ("q", 1), ("k", 1), ("v", 1),
          ("C", 1), ("X", 1), ("B", 0), ("B", 1)]
COL0 = {"q": 0, "k": 1024, "v": 2048, "B": 3072, "C": 4096, "X": 5120}
NB_IN = len(BLOCKS)
NB = NB_IN + D // 512
SUB = 4
UNITS = 2
HI_BUFS = 4
MODS = [1, 0, 2, 3, 4, 5]
SH1, SC1, GT1, SH2, SC2, GT2 = range(6)
W_ORDER = [(b, h) for h in range(2) for b in range(3)] + [(b, h) for b in range(3, NB) for h in range(2)]
SUBSTEPS = [(b, SUB // 2 * h + i) for b, h in W_ORDER for i in range(SUB // 2)]
BLOCK_USED = {b: W_ORDER.index((b, 1)) + 1 for b in range(NB)}
BANKS = {b: (4, 5) if b == 2 else (2 * (b % 2), 2 * (b % 2) + 1) for b in range(NB)}
SCORE_AT = {4 * SUB - 3 + 2 * h if h < HG else 8 * SUB + 1 + 2 * (h - HG): h for h in range(HEADS)}
FINISH_AT = {6 * SUB: 0, 11 * SUB: 1}
ADA_UNITS = 4
QUARTER = D // 4
COL_TILE = 32
DVE_MODS = (2, 4)


def plan_ring():
    def early(h):
        return [("ada", i, h, r) for i in range(2) for r in range(ADA_UNITS)]
    late = [("ada", i + j, h, r) for i in (2, 4) for h in range(2) for r in range(ADA_UNITS) for j in range(2)]
    plan = early(0)
    for b in range(3):
        plan += [("w", b, 0)] + early(1)[2 * b:2 * b + 2]
    plan += early(1)[6:]
    spread = 2 * NB_IN - 3
    for n, (b, h) in enumerate(W_ORDER[3:]):
        plan.append(("w", b, h))
        if n < spread:
            plan += late[len(late) * n // spread:len(late) * (n + 1) // spread]
    return plan


PLAN = plan_ring()
EARLY = [what for what in PLAN if what[0] == "ada" and what[1] < 2]
ADA_AT = {1: EARLY[8:10], 3: EARLY[10:12], 5: EARLY[12:]}
for _what in PLAN:
    if _what[0] == "w":
        _at = 2 * W_ORDER.index(_what[1:])
    elif _what[1] >= 2:
        _s = _at if _at not in ADA_AT else _at + 1
        assert _s not in ADA_AT
        ADA_AT[_s] = [_what]
COLUMNS_AT = {max(s for s, w in ADA_AT.items() if w[-1][1] == i) + 3: i for i in range(2, 6)}
BCAST_AT = {NB_IN * SUB + 1: 0, NB_IN * SUB + 8: 1}
EXPERT_SLOTS = [(len(PLAN) + m) % RING1 for m in range(RING1)] + [HI_SLOT, LO_SLOT]
USES0 = [len(range(i, len(PLAN), RING1)) if i < RING1 else 0 for i in range(RING)]
W_USED0 = 2 * NB + SPARE
assert (UNROLL * 6) % RING == 0 and all(what[0] == "w" for what in PLAN[-RING1:])
AHEAD = 3 * SUB // 2
assert max(COLUMNS_AT) < NB_IN * SUB + 8


def hybrid_layer(nc, consts, small, lam, wrt, x, w_ada, w_in, w_out, w_gate, w_up, w_down, out):
    ctx = ExitStack()
    with ctx:
        def sb(name, shape, dt=F32):
            return ctx.enter_context(nc.sbuf_tensor(name, shape, dt))

        def sem(name):
            return ctx.enter_context(nc.semaphore(name))

        h2_rows = nc.dram_tensor("h2_rows", (SEQ, D), F32, kind="Internal").ap()
        y_rows = nc.dram_tensor("y_rows", (4 * SEQ, D // 2), F32, kind="Internal").ap()

        with ExitStack() as names:
            ring_r = [names.enter_context(nc.sbuf_tensor(f"ring_r{n}", [P, SLOT], F32R)) for n in range(RING)]
            region_a_r = names.enter_context(nc.sbuf_tensor("region_a_r", [P, 2 * D], F32R))
            region_b_r = names.enter_context(nc.sbuf_tensor("region_b_r", [P, 2 * D], F32R))
        ring = sb("ring", [P, RING, SLOT])
        region_a = sb("region_a", [P, 2 * D])
        region_b = sb("region_b", [P, 2 * D])
        region_c = sb("region_c", [P, 2 * D + 8])
        acc = sb("acc", [P, 2, D])
        soft = sb("soft", [P, 2, P + SEQ])
        o_raw = sb("o_raw", [P, HG, TT, DV])
        a_turned = sb("a_turned", [P, P + SEQ])
        cst = sb("cst", [P, C_ALL])
        par = sb("par", [P, A_ALL])
        sml = sb("sml", [P, 64])
        mods = sb("mods", [P, 6, KC])
        cols = sb("cols", [P, 4, KC])

        bank = [ctx.enter_context(nc.psum_tensor(f"bank{i}", [P, 512], F32)) for i in range(8)]

        x_rows = region_a[:, :].rearrange("p (t d) -> p t d", t=TT)
        y_turned = region_a[:, :].rearrange("p (c s) -> p c s", s=SEQ)
        h_turned = region_b[:, :].rearrange("p (k s) -> p k s", s=SEQ)
        h_hi = region_b_r[:, :].rearrange("p (k s) -> p k s", s=SEQ)
        h_lo = y_hi = ring_r[LO_SLOT][:, :].rearrange("p (k s) -> p k s", s=SEQ)
        lo_f32 = ring[:, LO_SLOT, :].rearrange("p (k s) -> p k s", s=SEQ)
        y_lo = region_a_r[:, :].rearrange("p (k s) -> p k s", s=SEQ)
        w_hi = ring_r[HI_SLOT][:, :].rearrange("p (b n) -> p b n", b=HI_BUFS)
        x1 = region_b[:, :].rearrange("p (t d) -> p t d", t=TT)
        q_turned = region_c[:, 0:1024].rearrange("p (c s) -> p c s", s=SEQ)
        k_turned = region_c[:, 1024:2048].rearrange("p (c s) -> p c s", s=SEQ)
        v_rows = region_c[:, 2048:3072].rearrange("p (t n) -> p t n", t=TT)
        conv_in = region_c[:, 3072:3072 + HG * (SEQ + 2)].rearrange("p (c s) -> p c s", s=SEQ + 2)
        y_sb = region_c[:, 0:2 * D].rearrange("p (t d) -> p t d", t=TT)
        wr_sb = soft[:, :, :].rearrange("p a b -> p (a b)")[:, 0:KC * 36].rearrange("p (k n) -> p k n", k=KC)
        rt = o_raw[:, :, :, :].rearrange("p a b c -> p (a b c)")

        ident = cst[:, C_ID:C_ID + P]
        tri = cst[:, C_TRI:C_TRI + P]
        ones = cst[:, C_ONE:C_ONE + P]
        dist = cst[:, C_DIST:C_DIST + P + SEQ]
        eps_norm = par[:, A_EPS:A_EPS + 1]
        eps_subln = par[:, A_EPS + 1:A_EPS + 2]
        zero = par[:, A_EPS + 2:A_EPS + 3]

        c_exp, silu_c = sml[:, 0:16], sml[:, 16:32]
        lam_s, lam_e, neg_lam = sml[:, 32:34], sml[:, 34:36], sml[:, 36:37]
        ssq = sml[:, 37:39]
        rms = sml[:, 39:41]
        junk = sb("junk", [P, DV])
        mx = sb("mx", [P, 4])
        p_sum = sb("p_sum", [P, 4])
        p_rec = sb("p_rec", [P, 4])
        o_ss = sb("o_ss", [P, HG * TT])
        o_rec = sb("o_rec", [P, HG * TT])
        y_ss = sb("y_ss", [P, TT, 4])
        gsub = sml[:, 41:42]
        xrms = sml[:, 42:44]
        yrms = sml[:, 44:46]
        h2rms = sml[:, 46:48]

        s_slot = [sem(f"s_slot{i}") for i in range(RING)]
        s_cst = sem("s_cst")
        s_par = sem("s_par")
        s_x = [sem(f"s_x_in{t}") for t in range(TT)]
        s_ada_used = sem("s_ada_used")
        s_ada_dve = sem("s_ada_dve")
        s_quarter_read = sem("s_quarter_read")
        s_w_used = sem("s_w_used")
        s_dve = sem("s_dve")
        s_act = sem("s_act")
        s_cexp = sem("s_cexp")
        s_silu_c = sem("s_silu_c")
        s_ssq = sem("s_ssq")
        s_rms = sem("s_rms")
        s_xn = sem("s_xn")
        s_xt = sem("s_xt")
        s_xt_read = sem("s_xt_read")
        s_turn = sem("s_turn")
        s_turn_read = sem("s_turn_read")
        s_h = sem("s_h")
        s_h_hi = sem("s_h_hi")
        s_h_lo = sem("s_h_lo")
        s_w_hi = sem("s_w_hi")
        s_w_lo = sem("s_w_lo")
        s_hi_used = sem("s_hi_used")
        s_y_hi = sem("s_y_hi")
        s_y_lo = sem("s_y_lo")
        s_block_act = sem("s_block_act")
        s_block_dve = sem("s_block_dve")
        s_scores = sem("s_scores")
        s_shift = sem("s_shift")
        s_prob = sem("s_prob")
        s_a = sem("s_a")
        s_o_rms = sem("s_o_rms")
        s_o_norm = sem("s_o_norm")
        s_lam_in = sem("s_lam_in")
        s_lam = sem("s_lam")
        s_lam_e = sem("s_lam_e")
        s_cols = sem("s_cols")
        s_wr = sem("s_wr")

        ada_v = w_ada[0].rearrange("(p k) (m q n) -> p k m q n", k=KC, m=6, q=4)
        in_v = w_in[0].rearrange("(h p k) n -> h p k n", h=2, k=KH)
        out_v = w_out[0].rearrange("(c p) n -> p c n", p=P)
        x_v = x[0].rearrange("(t p) d -> t p d", p=P)
        o_v = out[0].rearrange("(t p) d -> t p d", p=P)

        slot_of = {what: n for n, what in enumerate(PLAN)}

        def feature(rows, k):
            h = k // KH
            return rows[:, D // 2 * h + k % KH:D // 2 * (h + 1):KH]

        def landed(eng, what):
            n = slot_of[what]
            eng.wait_ge(s_slot[n % RING1], 16 * (n // RING1 + 1))
            return ring[:, n % RING1, :]

        def unit_weights(v):
            b, part = SUBSTEPS[v // UNITS]
            n = slot_of[("w", b, part // 2)]
            c0 = 1024 * (UNITS * (part % 2) + v % UNITS)
            span = slice(c0, c0 + 1024)
            return ring[:, n % RING1, span], ring_r[n % RING1][:, span], v % HI_BUFS

        turns = []
        for s in range(-1, NB * SUB + 1):
            if s == -1:
                turns += [("col", i, h) for h in range(2) for i in range(2)]
            if s - 3 in SCORE_AT:
                turns.append(("out", SCORE_AT[s - 3]))
            if s - 2 in SCORE_AT:
                turns.append(("head", SCORE_AT[s - 2]))
            if s in FINISH_AT:
                turns += [("fin", FINISH_AT[s], h) for h in range(2)]
            if s in COLUMNS_AT:
                turns += [("col", COLUMNS_AT[s], h) for h in range(2)]
            if s in BCAST_AT:
                turns += [("bc", BCAST_AT[s], j) for j in range(4)]
        turns += [("bc", n, j) for n in (2, 3) for j in range(4)]
        turn_no = {what: n for n, what in enumerate(turns)}

        ada_order = [what for what in PLAN if what[0] == "ada" and what[1] not in DVE_MODS]
        dve_order = [what for what in PLAN if what[0] == "ada" and what[1] in DVE_MODS]

        def quarters_done(i, h):
            return ada_order.index(("ada", i, h, ADA_UNITS - 1)) // 2 + 1

        act_evac = [b for b in range(NB) if b >= NB_IN or BLOCKS[b][0] not in "XB"]
        dve_evac = [b for b in range(NB) if b not in act_evac]

        g_rows = region_a[0:CAP, :].rearrange("p (b d) -> p b d", b=2)
        xe_turned = region_c[:, 0:2 * KC * CAP].rearrange("p (b k s) -> p b k s", b=2, k=KC)
        y_item = region_c[:, D:2 * D].rearrange("p (b n) -> p b n", b=2)
        silu_g = acc[0:CAP, 0, 0:FE]
        act_rows = acc[0:CAP, 0, FE:2 * FE]
        act_turned = acc[:, 0, 2 * FE:2 * FE + 4 * CAP].rearrange("p (j s) -> p j s", j=4)
        g_idx = sb("g_idx", [P, ITEMS], I32)
        s_idx = sb("s_idx", [P, ITEMS], I32)
        e_idx = sb("e_idx", [P, ITEMS], I32)
        n_extra = sb("n_extra", [P, 1], I32)
        g_cur = sb("g_cur", [P, 2], I32)
        s_cur = sb("s_cur", [P, 2], I32)
        weight = sb("weight", [P, ITEMS])
        f_ss = sb("f_ss", [P, TT])

        def hot_slot(n):
            return acc[:, 0, T_SLOT + P * n:T_SLOT + P * (n + 1)]

        def hot_item(n):
            c0 = T_ITEM + 5 * ITEMS * n
            return acc[:, 0, c0:c0 + 5 * ITEMS].rearrange("p (a b) -> p a b", a=5)

        s_h2 = sem("s_h2")
        s_h2_store = sem("s_h2_store")
        s_h2t = sem("s_h2t")
        s_h2t_read = sem("s_h2t_read")
        s_logit = sem("s_logit")
        s_gexp_in = sem("s_gexp_in")
        s_gexp = sem("s_gexp")
        s_picks = sem("s_picks")
        s_rank = sem("s_rank")
        s_rank_used = sem("s_rank_used")
        s_extra = sem("s_extra")
        s_base = sem("s_base")
        s_hot = sem("s_hot")
        s_table = sem("s_table")
        s_tables = sem("s_tables")
        s_y_gated = sem("s_y_gated")
        s_x1 = sem("s_x1")
        s_x1a = sem("s_x1a")
        s_xsq = sem("s_xsq")
        s_h2rms = sem("s_h2rms")
        s_ysum = sem("s_ysum")
        s_yrms = sem("s_yrms")
        s_zero = sem("s_zero")

        s_g_cur = sem("s_g_cur")
        s_gather = [sem(f"s_gather{b}") for b in range(2)]
        s_xe_psum = sem("s_xe_psum")
        s_xe_act = sem("s_xe_act")
        s_xe_dve = sem("s_xe_dve")
        s_silu_g = sem("s_silu_g")
        s_act_rows = sem("s_act_rows")
        s_at_psum = sem("s_at_psum")
        s_at = sem("s_at")
        s_y_act = sem("s_y_act")
        s_y_dve = sem("s_y_dve")
        s_s_cur = sem("s_s_cur")
        s_y_free = sem("s_y_free")
        s_scatter = [sem(f"s_scatter{b}") for b in range(2)]
        s_pool_turn = sem("s_pool_turn")
        s_pe_turn = sem("s_pe_turn")

        s_pair = [sem(f"s_pair{t}") for t in range(TT)]
        s_fsum = sem("s_fsum")
        s_fsq = sem("s_fsq")
        s_frms = sem("s_frms")
        s_fin = sem("s_fin")
        s_store = sem("s_store")

        x_scatter = sem("x_scatter")
        x_load = [sem(f"x_load{r}") for r in range(6)]
        x_done = sem("x_done")
        x_gcur = sem("x_gcur")
        x_gather = sem("x_gather")
        x_xe = sem("x_xe")
        x_xe_act = sem("x_xe_act")
        x_xe_dve = sem("x_xe_dve")
        x_gu = sem("x_gu")
        x_silu = sem("x_silu")
        x_rows_done = sem("x_rows_done")
        x_at = sem("x_at")
        x_atc = sem("x_atc")
        x_dn = sem("x_dn")
        x_ya = sem("x_ya")
        x_yd = sem("x_yd")

        gate_v = w_gate[0].rearrange("e (p k) f -> e p (k f)", k=KC)
        up_v = w_up[0].rearrange("e (p k) f -> e p (k f)", k=KC)
        down_v = w_down[0].rearrange("e (p j) n -> e p (j n)", j=4)
        PARTS = [(gate_v, 0), (up_v, 0), (gate_v, 1), (up_v, 1), (down_v, 0), (down_v, 1)]
        N_IT = NE // UNROLL

        block = ctx.enter_context(nc.Block())

        @block.sync
        def _(sp):
            sp.dma_start(par[:, :], small).then_inc(s_par, 16)
            sp.dma_start(rt[:, 0:4 * DK], lam).then_inc(s_lam_in, 16)
            ordinal = []
            for what in PLAN:
                for used, order in ((s_w_used, [("w", *bh) for bh in W_ORDER]), (s_ada_used, ada_order),
                                    (s_ada_dve, dve_order)):
                    if what in order:
                        ordinal.append((used, order.index(what) + 1))
            for n, what in enumerate(PLAN):
                if n >= RING1:
                    sp.wait_ge(*ordinal[n - RING1])
                dst = ring[:, n % RING1, :]
                if what[0] == "ada":
                    k0 = 8 * (what[3] % 2)
                    src = ada_v[:, k0:k0 + 8, MODS[what[1]], 2 * what[2] + what[3] // 2, :]
                else:
                    b, half = what[1], what[2]
                    if b < NB_IN:
                        kind, g = BLOCKS[b]
                        c0 = COL0[kind] + 512 * g
                        src = in_v[half, :, :, c0:c0 + 512]
                    else:
                        c0 = 512 * (b - NB_IN)
                        src = out_v[:, 8 * half:8 * half + 8, c0:c0 + 512]
                dst = dst.rearrange("p (k n) -> p k n", k=8)
                sp.dma_start(dst, src).then_inc(s_slot[n % RING1], 16)
                if n == 0:
                    for t in range(TT):
                        sp.dma_start(x_rows[:, t, :], x_v[t]).then_inc(s_x[t], 16)
                    sp.dma_start(cst[:, :], consts).then_inc(s_cst, 16)
            with sp.Fori(0, N_IT) as it:
                for u in range(UNROLL):
                    for r, (view, half) in enumerate(PARTS):
                        n = 6 * u + r
                        slot = EXPERT_SLOTS[n % RING]
                        sp.wait_ge(s_w_used, W_USED0 - RING + 1 + it * (6 * UNROLL) + n)
                        src = view[bass.ds(it * UNROLL + u, 1), :, SLOT * half:SLOT * (half + 1)]
                        sp.dma_start(ring[:, slot, :], src.rearrange("a p f -> (a p) f")).then_inc(s_slot[slot], 16)
            sp.wait_ge(s_tables, 1)
            nx = sp.value_load(n_extra[0:1, 0:1], min_val=0, max_val=MAX_EXTRA)
            sp.wait_ge(s_w_used, W_USED0 + 6 * NE)
            with sp.If(nx > 0):
                with sp.Fori(0, nx) as j:
                    sp.wait_ge(x_done, j + 1)
                    e = sp.value_load(e_idx[0:1, bass.ds(j + NE, 1)], min_val=0, max_val=NE - 1)
                    for r, (view, half) in enumerate(PARTS):
                        src = view[bass.ds(e, 1), :, SLOT * half:SLOT * (half + 1)]
                        sp.dma_start(ring[:, r, :], src.rearrange("a p f -> (a p) f")).then_inc(x_load[r], 16)
            sp.wait_ge(s_scatter[0], 16 * NE // 2)
            sp.wait_ge(s_scatter[1], 16 * NE // 2)
            sp.wait_ge(x_done, nx + 1)
            yv = y_rows.rearrange("(k t p c) n -> t p k (c n)", k=2, t=TT, p=P)
            for t in range(TT):
                sp.dma_start(ring[:, t, :].rearrange("p (k n) -> p k n", k=2), yv[t]).then_inc(s_pair[t], 16)
            for t in range(TT):
                sp.wait_ge(s_fin, t + 1)
                sp.dma_start(o_v[t], x1[:, t, :]).then_inc(s_store, 16)
            sp.wait_ge(s_store, 16 * TT)

        @block.gpsimd
        def _(pool):
            pool.wait_ge(s_logit, 1)
            pool.memset(g_rows, 0.0).then_inc(s_zero, 1)
            pool.wait_ge(s_zero, 1)
            pool.wait_ge(s_h2_store, 16 * TT)
            pool.wait_ge(s_tables, 1)

            def gather(column, b):
                pool.tensor_copy(g_cur[0:CAP, b:b + 1], g_idx[0:CAP, column]).then_inc(s_g_cur, 1)

            def gather_go(b):
                pool.indirect_dma_start(g_rows[:, b, :], None, h2_rows,
                                        bass.IndirectOffsetOnAxis(ap=g_cur[0:CAP, b:b + 1], axis=0),
                                        bounds_check=SEQ - 1, oob_is_err=False).then_inc(s_gather[b], 16)

            def scatter_go(b, done):
                pool.indirect_dma_start(y_rows, bass.IndirectOffsetOnAxis(ap=s_cur[0:PAIR, b:b + 1], axis=0),
                                        y_item[0:PAIR, b, :], None,
                                        bounds_check=4 * SEQ - 1, oob_is_err=False).then_inc(done, 16)

            for b in range(2):
                gather(slice(b, b + 1), b)
                pool.wait_ge(s_g_cur, b + 1)
                gather_go(b)
            pool.sem_inc(s_y_free, 2)
            pool.sem_inc(x_done, 1)
            with pool.Fori(0, N_IT) as it:
                for u in range(UNROLL):
                    b = u % 2
                    i = it * UNROLL + u
                    pool.wait_ge(s_xe_psum, i + 1)
                    pool.sem_inc(s_pool_turn, 1)
                    gather(bass.ds(i + 2, 1), b)
                    pool.wait_ge(s_g_cur, i + 3)
                    pool.sem_inc(s_pool_turn, 1)
                    gather_go(b)
                    pool.wait_ge(s_y_act, i + 2)
                    pool.sem_inc(s_pool_turn, 1)
                    pool.wait_ge(s_y_dve, i + 2)
                    pool.sem_inc(s_pool_turn, 1)
                    pool.tensor_copy(s_cur[:, b:b + 1], s_idx[:, bass.ds(i, 1)]).then_inc(s_s_cur, 1)
                    pool.wait_ge(s_s_cur, i + 1)
                    pool.sem_inc(s_pool_turn, 1)
                    scatter_go(b, s_scatter[b])
                    pool.wait_ge(s_scatter[b], it * 32 + 16 * (u // 2 + 1))
                    pool.sem_inc(s_y_free, 1)
            for b in range(2):
                pool.wait_ge(s_gather[b], 16 * (NE // 2 + 1))
                pool.wait_ge(s_scatter[b], 16 * (NE // 2))
            nx = pool.value_load(n_extra[0:1, 0:1], min_val=0, max_val=MAX_EXTRA)
            with pool.If(nx > 0):
                with pool.Fori(0, nx) as j:
                    pool.tensor_copy(g_cur[0:CAP, 0:1], g_idx[0:CAP, bass.ds(j + NE, 1)]).then_inc(x_gcur, 1)
                    pool.tensor_copy(s_cur[:, 0:1], s_idx[:, bass.ds(j + NE, 1)]).then_inc(x_gcur, 1)
                    pool.wait_ge(x_gcur, j * 2 + 2)
                    pool.sem_inc(s_pool_turn, 1)
                    pool.indirect_dma_start(g_rows[:, 0, :], None, h2_rows,
                                            bass.IndirectOffsetOnAxis(ap=g_cur[0:CAP, 0:1], axis=0),
                                            bounds_check=SEQ - 1, oob_is_err=False).then_inc(x_gather, 16)
                    pool.wait_ge(x_ya, j + 1)
                    pool.sem_inc(s_pool_turn, 1)
                    pool.wait_ge(x_yd, j + 1)
                    pool.sem_inc(s_pool_turn, 1)
                    scatter_go(0, x_scatter)
                    pool.wait_ge(x_scatter, j * 16 + 16)
                    pool.sem_inc(x_done, 1)

        @block.tensor
        def _(pe):
            def take_turn(what):
                n = turn_no[what]
                if n >= 1:
                    pe.wait_ge(s_turn_read, n)

            def columns(i, h):
                take_turn(("col", i, h))
                if i in DVE_MODS:
                    pe.wait_ge(s_ada_dve, dve_order.index(("ada", i, h, ADA_UNITS - 1)) + 1)
                    summed = ones[:, 0:1]
                else:
                    pe.wait_ge(s_quarter_read, quarters_done(i, h))
                    summed = cst[:, C_TILE:C_TILE + 1]
                c0 = A_BADA + KC * MODS[i] + KH * h
                pe.matmul(bank[6][:, 0:KH], ident, par[:, c0:c0 + KH],
                          start=True, stop=False, skip_group_check=True)
                for k in range(KH):
                    mm = pe.matmul(bank[6][:, k:k + 1], feature(acc[:, i % 2, :], KH * h + k), summed,
                                   start=False, stop=(k == KH - 1), skip_group_check=True)
                mm.then_inc(s_turn, 1)

            def ada(what):
                n = ada_order.index(what)
                if n % 2 == 0 and n >= 2:
                    pe.wait_ge(s_quarter_read, n // 2)
                w = landed(pe, what).rearrange("p (k n) -> p k n", k=8)
                for k in range(8):
                    tile = slice(COL_TILE * (k % 4), COL_TILE * (k % 4 + 1))
                    row = 8 * (n % 2) + k
                    mm = pe.matmul(bank[7][tile, :], silu_c[:, row:row + 1].to_broadcast([P, COL_TILE]), w[:, k, :],
                                   start=(row < 4), stop=(row >= KC - 4))
                mm.then_inc(s_ada_used, 1)

            def head_scores(h):
                hh = h % HG
                if hh == 0:
                    pe.wait_ge(s_block_act, 2 * (act_evac.index(3 + 5 * (h // HG) - 1) + 1))
                if h >= 1:
                    pe.wait_ge(s_shift, h)
                for m in range(2):
                    rows = slice(DK * m, DK * m + DK)
                    pe.matmul(bank[4 + m][:, 0:P], q_turned[rows, hh, 0:P], k_turned[rows, hh, 0:P],
                              start=True, stop=True)
                    mm = pe.matmul(bank[4 + m][:, P:P + SEQ], q_turned[rows, hh, P:SEQ], k_turned[rows, hh, :],
                                   start=True, stop=True)
                mm.then_inc(s_scores, 1)

            def head_turn(h):
                take_turn(("head", h))
                pe.wait_ge(s_a, h + 1)
                for j in range(3):
                    mm = pe.transpose(bank[6][:, j * P:(j + 1) * P], soft[:, 0, j * P:(j + 1) * P], ident)
                mm.then_inc(s_turn, 1)

            def head_out(h):
                hh = h % HG
                take_turn(("out", h))
                vh = slice(DV * hh, DV * hh + DV)
                pe.matmul(bank[6][:, 0:DV], a_turned[:, 0:P], v_rows[:, 0, vh], start=True, stop=True)
                pe.matmul(bank[6][:, DV:2 * DV], a_turned[:, P:2 * P], v_rows[:, 0, vh], start=True, stop=False)
                mm = pe.matmul(bank[6][:, DV:2 * DV], a_turned[:, 2 * P:3 * P], v_rows[:, 1, vh],
                               start=False, stop=True)
                mm.then_inc(s_turn, 1)

            def finish(g):
                pe.wait_ge(s_o_norm, g + 1)
                for half in range(2):
                    take_turn(("fin", g, half))
                    for j in range(2):
                        for t in range(TT):
                            mm = pe.transpose(bank[6][:, (2 * j + t) * P:(2 * j + t + 1) * P],
                                              o_raw[:, 2 * half + j, t, :], ident)
                    mm.then_inc(s_turn, 1)

            def broadcast(which, col):
                for j in range(4):
                    take_turn(("bc", which, j))
                    for k in range(4):
                        mm = pe.matmul(bank[6][:, k * P:(k + 1) * P],
                                       col[:, 4 * j + k:4 * j + k + 1].to_broadcast([P, P]), ident,
                                       start=True, stop=True)
                    mm.then_inc(s_turn, 1)

            pe.wait_ge(s_silu_c, 1)
            for what in EARLY[:3]:
                ada(what)
            pe.wait_ge(s_cst, 16)
            pe.wait_ge(s_par, 16)
            pe.wait_ge(s_xn, TT)
            for n in range(KC // 2):
                if n >= 4:
                    pe.wait_ge(s_xt_read, n - 3)
                for j in range(2):
                    for t in range(TT):
                        mm = pe.transpose(bank[n % 4][:, (2 * j + t) * P:(2 * j + t + 1) * P],
                                          feature(x_rows[:, t, :], 2 * n + j), ident)
                mm.then_inc(s_xt, 1)
            for what in EARLY[3:4]:
                ada(what)
            columns(0, 0)
            for what in EARLY[4:8]:
                ada(what)
            columns(1, 0)
            for s, (b, part) in enumerate(SUBSTEPS):
                if s == 4:
                    columns(0, 1)
                if s == AHEAD:
                    columns(1, 1)
                if s - 3 in SCORE_AT:
                    head_out(SCORE_AT[s - 3])
                if s - 2 in SCORE_AT:
                    head_turn(SCORE_AT[s - 2])
                if s in SCORE_AT:
                    head_scores(SCORE_AT[s])
                if s in FINISH_AT:
                    finish(FINISH_AT[s])
                if s in COLUMNS_AT:
                    for h in range(2):
                        columns(COLUMNS_AT[s], h)
                if s in BCAST_AT:
                    pe.wait_ge(s_cols, 2 + BCAST_AT[s])
                    broadcast(BCAST_AT[s], cols[:, 1 + BCAST_AT[s], :])
                if part == 0:
                    if b < 3:
                        pe.wait_ge(s_xt_read, KC // 2)
                    elif b - 2 >= NB_IN:
                        pe.wait_ge(s_y_gated, 2 * (b - 1 - NB_IN))
                    elif b - 2 in act_evac:
                        pe.wait_ge(s_block_act, 2 * (act_evac.index(b - 2) + 1))
                    else:
                        pe.wait_ge(s_block_dve, 2 * (dve_evac.index(b - 2) + 1))
                if b == 0:
                    pe.wait_ge(s_h_lo, part + 1)
                if b == NB_IN:
                    pe.wait_ge(s_y_lo, part + 1)
                lo, hi = (bank[n] for n in BANKS[b])
                rows = b >= NB_IN or BLOCKS[b][0] == "v"
                src_hi, src_lo = (y_hi, y_lo) if b >= NB_IN else (h_hi, h_lo)
                for v in range(UNITS * s, UNITS * s + UNITS):
                    _, w_lo, buf = unit_weights(v)
                    for n_pass, src in enumerate((src_hi, src_lo, src_hi)):
                        if n_pass == 0:
                            pe.wait_ge(s_w_hi, v + 1)
                        if n_pass == 2:
                            pe.wait_ge(s_w_lo, v + 1)
                        w = w_hi[:, buf, :] if n_pass < 2 else w_lo
                        for kk in range(2):
                            k = 4 * part + 2 * (v % UNITS) + kk
                            wk = w[:, 512 * kk:512 * kk + 512]
                            first = k == 0 and n_pass == 0
                            last = k == KC - 1 and n_pass == 2
                            if rows:
                                for t in range(TT):
                                    mm = pe.matmul((lo, hi)[t][:, :], src[:, k, t * P:(t + 1) * P], wk,
                                                   start=first, stop=last)
                            else:
                                for c in range(HG):
                                    mm = pe.matmul((lo, hi)[c // 2][:, SEQ * (c % 2):SEQ * (c % 2) + SEQ],
                                                   wk[:, P * c:P * c + P], src[:, k, :],
                                                   start=(first and c % 2 == 0), stop=last, skip_group_check=True)
                        if n_pass == 1:
                            mm.then_inc(s_hi_used, 1)
                if part % 2 == 1:
                    mm.then_inc(s_w_used, 1 + (SPARE if s == len(SUBSTEPS) - 1 else 0))
                for what in ADA_AT.get(s, []):
                    if what in ada_order:
                        ada(what)
            broadcast(2, mods[:, SH2, :])
            h2_turned = y_turned
            pe.wait_ge(s_wr, 16)
            for t in range(TT):
                pe.wait_ge(s_h2, t + 1)
                for j in range(4):
                    n = 4 * t + j
                    if n < 4:
                        pe.wait_ge(s_y_gated, 2 * (NB - NB_IN))
                    else:
                        pe.wait_ge(s_h2t_read, n - 3)
                    for k in range(4):
                        mm = pe.transpose(bank[n % 4][:, k * P:(k + 1) * P], y_sb[:, t, 4 * j + k::KC], ident)
                    mm.then_inc(s_h2t, 1)
                pe.wait_ge(s_h2t_read, 4 * (t + 1))
                for k in range(KC):
                    mm = pe.matmul(bank[4 + t][:, 0:36], h2_turned[:, k, t * P:(t + 1) * P], wr_sb[:, k, :],
                                   start=(k == 0), stop=(k == KC - 1))
            mm.then_inc(s_logit, 1)
            pe.wait_ge(s_picks, 1)
            pe.wait_ge(s_turn_read, turn_no[("bc", 2, 3)] + 1)
            both = rt[:, R_BOTH:R_BOTH + TT * NE].rearrange("p (t e) -> p t e", t=TT)
            pe.matmul(bank[6][:, 0:NE], tri, both[:, 0, :], start=True, stop=True)
            pe.matmul(bank[6][:, NE:2 * NE], tri, both[:, 1, :], start=True, stop=False)
            mm = pe.matmul(bank[6][:, NE:2 * NE], ones, both[:, 0, :], start=False, stop=True)
            for t in range(TT):
                mm = pe.matmul(bank[7][0:NE, 0:1], both[:, t, :], ones[:, 0:1], start=(t == 0), stop=(t == TT - 1))
            mm.then_inc(s_rank, 1)
            pe.wait_ge(s_extra, 1)
            extra = rt[0:NE, R_EXTRA:R_EXTRA + 1]
            pe.matmul(bank[7][:, 0:NE], extra.to_broadcast([NE, P]), tri[0:NE, 0:NE], start=True, stop=True)
            pe.matmul(bank[7][:, NE:NE + 1], extra.to_broadcast([NE, P]), ones[0:NE, 0:1],
                      start=True, stop=True).then_inc(s_base, 1)
            pe.wait_ge(s_hot, 1)
            for n in range(2 * TT):
                mm = pe.matmul(bank[7][:, 0:5 * ITEMS], hot_slot(n), hot_item(n).rearrange("p a b -> p (a b)"),
                               start=(n == 0), stop=(n == 2 * TT - 1))
            mm.then_inc(s_table, 1)
            pe.wait_ge(s_cols, 4)
            pe.wait_ge(s_rank_used, 2)
            broadcast(3, cols[:, 3, :])

            def turn_rows(b):
                for k in range(KC):
                    mm = pe.transpose(bank[2 + k // 8][:, CAP * (k % 8):CAP * (k % 8) + CAP],
                                      g_rows[:, b, k::KC], ident[0:CAP, 0:CAP])
                return mm

            def gate_up(b, w, done):
                for k in range(KC):
                    if k % 8 == 0:
                        wg, wu = w(2 * (k // 8)), w(2 * (k // 8) + 1)
                    xk = xe_turned[:, b, k, :]
                    g = pe.matmul(bank[0][UPPER:UPPER + CAP, :], xk, wg[:, FE * (k % 8):FE * (k % 8 + 1)],
                                  start=(k == 0), stop=(k == KC - 1))
                    mm = pe.matmul(bank[0][0:CAP, :], xk, wu[:, FE * (k % 8):FE * (k % 8 + 1)],
                                   start=(k == 0), stop=(k == KC - 1))
                    if k % 8 == 7 and done is not None:
                        g.then_inc(done, 1)
                        mm.then_inc(done, 1)
                return mm

            def turn_act():
                for j in range(4):
                    mm = pe.transpose(bank[4][:, CAP * j:CAP * j + CAP], act_rows[:, j::4], ident[0:CAP, 0:CAP])
                return mm

            def down(w, done):
                for j in range(4):
                    if j % 2 == 0:
                        wd = w(4 + j // 2)
                    for n in range(2):
                        for half in range(2):
                            c0 = D * (j % 2) + 1024 * half + 512 * n
                            mm = pe.matmul(bank[5 + n][UPPER * half:UPPER * half + CAP, :], act_turned[:, j, :],
                                           wd[:, c0:c0 + 512], start=(j == 0), stop=(j == 3))
                    if j % 2 == 1 and done is not None:
                        mm.then_inc(done, 1)
                return mm

            pe.wait_ge(s_tables, 1)
            pe.wait_ge(s_gather[0], 16)
            turn_rows(0).then_inc(s_xe_psum, 1)
            with pe.Fori(0, N_IT) as it:
                for u in range(UNROLL):
                    i = it * UNROLL + u
                    b = u % 2

                    def weights(r):
                        n = 6 * u + r
                        slot = EXPERT_SLOTS[n % RING]
                        pe.wait_ge(s_slot[slot], it * (16 * 6 * UNROLL // RING) + 16 * (USES0[slot] + n // RING + 1))
                        return ring[:, slot, :]

                    pe.wait_ge(s_xe_act, i + 1)
                    pe.wait_ge(s_xe_dve, i + 1)
                    gate_up(b, weights, s_w_used)
                    pe.wait_ge(s_gather[1 - b], it * 32 + 16 * ((u + 1) // 2 + 1))
                    pe.sem_inc(s_pe_turn, 1)
                    turn_rows(1 - b).then_inc(s_xe_psum, 1)
                    pe.wait_ge(s_act_rows, i + 1)
                    pe.sem_inc(s_pe_turn, 1)
                    turn_act().then_inc(s_at_psum, 1)
                    pe.wait_ge(s_at, i + 1)
                    pe.wait_ge(s_y_act, i + 1)
                    pe.wait_ge(s_y_dve, i + 1)
                    down(weights, s_w_used)
            nx = pe.value_load(n_extra[0:1, 0:1], min_val=0, max_val=MAX_EXTRA)
            pe.wait_ge(s_xe_act, NE + 1)
            pe.wait_ge(s_xe_dve, NE + 1)
            pe.wait_ge(s_y_act, NE + 1)
            pe.wait_ge(s_y_dve, NE + 1)
            with pe.If(nx > 0):
                with pe.Fori(0, nx) as j:
                    def weights_x(r):
                        pe.wait_ge(x_load[r], j * 16 + 16)
                        return ring[:, r, :]

                    pe.wait_ge(x_gather, j * 16 + 16)
                    pe.sem_inc(s_pe_turn, 1)
                    turn_rows(0).then_inc(x_xe, 1)
                    pe.wait_ge(x_xe_act, j + 1)
                    pe.wait_ge(x_xe_dve, j + 1)
                    gate_up(0, weights_x, None).then_inc(x_gu, 1)
                    pe.wait_ge(x_rows_done, j + 1)
                    pe.sem_inc(s_pe_turn, 1)
                    turn_act().then_inc(x_at, 1)
                    pe.wait_ge(x_atc, j + 1)
                    down(weights_x, None).then_inc(x_dn, 1)

        @block.scalar
        def _(act):
            count = [0]

            def link(ins):
                count[0] += 1
                ins.then_inc(s_act, 1)
                act.wait_ge(s_act, count[0])

            act.wait_ge(s_par, 16)
            act.activation(c_exp, par[:, A_C:A_C + KC], ACT.Exp, bias=zero, scale=-1.0).then_inc(s_cexp, 1)
            act.wait_ge(s_lam, 1)
            act.activation(lam_e, lam_s, ACT.Exp, bias=zero).then_inc(s_lam_e, 1)
            for t in range(TT):
                act.wait_ge(s_x[t], 16)
                act.activation(y_sb[:, t, :], x_rows[:, t, :], ACT.Square, bias=zero,
                               accum_out=ssq[:, t:t + 1]).then_inc(s_ssq, 1)
            act.wait_ge(s_ssq, TT)
            act.activation(rms, ssq, ACT.Sqrt, bias=eps_norm, scale=1.0 / D).then_inc(s_rms, 1)

            def take_quarter(what):
                if what not in ada_order or ada_order.index(what) % 2 == 0:
                    return
                n = ada_order.index(what)
                i, q = what[1], 2 * what[2] + what[3] // 2
                act.wait_ge(s_ada_used, n + 1)
                if i >= 2 and q == 0:
                    act.wait_ge(s_turn, turn_no[("col", i - 2, 1)] + 1)
                act.activation(acc[:, i % 2, QUARTER * q:QUARTER * (q + 1)], bank[7][:, :],
                               ACT.Copy).then_inc(s_quarter_read, 1)

            for what in EARLY[:3]:
                take_quarter(what)
            for n in range(KC // 2):
                act.wait_ge(s_xt, n + 1)
                act.activation(h_turned[:, 2 * n:2 * n + 2, :],
                               bank[n % 4][:, :].rearrange("p (j s) -> p j s", j=2),
                               ACT.Copy).then_inc(s_xt_read, 1)

            def read_turn(what, dst, src, scale=1.0):
                act.wait_ge(s_turn, turn_no[what] + 1)
                act.activation(dst, src, ACT.Copy, scale=scale).then_inc(s_turn_read, 1)

            def columns(i, h):
                read_turn(("col", i, h), mods[:, MODS[i], KH * h:KH * h + KH], bank[6][:, 0:KH])

            def broadcast(which, row):
                v = row.rearrange("p (h n k) -> p h k n", h=2, k=KH)
                for j in range(4):
                    read_turn(("bc", which, j), v[:, j // 2, 4 * (j % 2):4 * (j % 2) + 4, :],
                              bank[6][:, :].rearrange("p (k n) -> p k n", k=4))

            def take_block(b):
                if b not in act_evac:
                    return
                act.wait_ge(s_w_used, BLOCK_USED[b])
                banks = [bank[n] for n in BANKS[b]]
                kind, g = BLOCKS[b] if b < NB_IN else ("y", b - NB_IN)
                for n, pb in enumerate(banks):
                    two = pb[:, :].rearrange("p (c s) -> p c s", c=2)
                    if kind == "q":
                        act.activation(q_turned[:, 2 * n:2 * n + 2, :], two, ACT.Copy,
                                       scale=DK ** -0.5).then_inc(s_block_act, 1)
                    elif kind == "k":
                        act.activation(k_turned[:, 2 * n:2 * n + 2, :], two, ACT.Copy).then_inc(s_block_act, 1)
                    elif kind == "C":
                        c0 = HEADS + HG * g + 2 * n
                        act.activation(y_turned[:, c0:c0 + 2, :], two, ACT.Copy).then_inc(s_block_act, 1)
                    elif kind == "v":
                        act.activation(v_rows[:, n, :], pb[:, :], ACT.Copy).then_inc(s_block_act, 1)
                    else:
                        act.activation(rt[:, 0:512], pb[:, :], ACT.Square, bias=zero,
                                       accum_out=y_ss[:, n, g:g + 1]).then_inc(s_block_act, 1)
                        act.wait_ge(s_block_act, 2 * act_evac.index(b) + n + 1)

            def split_h(j):
                act.wait_ge(s_h, j + 1)
                act.activation(h_hi[:, 4 * j:4 * j + 4, :], lo_f32[:, 4 * j:4 * j + 4, :],
                               ACT.Copy).then_inc(s_h_hi, 1)

            def split_w(s):
                for v in range(UNITS * s, UNITS * s + UNITS):
                    b, part = SUBSTEPS[s]
                    landed(act, ("w", b, part // 2))
                    w_f32, _, buf = unit_weights(v)
                    if v >= HI_BUFS:
                        act.wait_ge(s_hi_used, v - HI_BUFS + 1)
                        act.wait_ge(s_w_lo, v - HI_BUFS + 1)
                    act.activation(w_hi[:, buf, :], w_f32, ACT.Copy).then_inc(s_w_hi, 1)

            def exps(h):
                act.wait_ge(s_shift, h + 1)
                for m in range(2):
                    for t in range(TT):
                        span = slice(0, P) if t == 0 else slice(P, P + SEQ)
                        n = 2 * m + t
                        ins = act.activation(soft[:, m, span], soft[:, m, span], ACT.Exp,
                                             bias=mx[:, n:n + 1], accum_out=p_sum[:, n:n + 1])
                ins.then_inc(s_prob, 1)

            take_quarter(EARLY[3])
            columns(0, 0)
            for what in EARLY[4:8]:
                take_quarter(what)
            columns(1, 0)
            for j in range(2):
                split_h(j)
            for s in range(AHEAD):
                split_w(s)
                for what in ADA_AT.get(s - 2, []):
                    take_quarter(what)
                if s == 5:
                    columns(0, 1)
            for what in ADA_AT[AHEAD - 1]:
                take_quarter(what)
            columns(1, 1)
            for j in range(2, 4):
                split_h(j)
            for s, (b, part) in enumerate(SUBSTEPS):
                if AHEAD <= s + 1 < len(SUBSTEPS):
                    split_w(s + 1)
                if s > AHEAD:
                    for what in ADA_AT.get(s - 1, []):
                        take_quarter(what)
                if s >= 1 and SUBSTEPS[s - 1][1] == SUB - 1:
                    take_block(SUBSTEPS[s - 1][0])
                if s == NB_IN * SUB:
                    act.wait_ge(s_w_used, 2 * NB_IN)
                    act.wait_ge(s_turn_read, turn_no[("fin", 1, 1)] + 1)
                    for j in range(4):
                        if j == 2:
                            act.wait_ge(s_block_dve, 2 * len(dve_evac))
                        act.activation(y_hi[:, 4 * j:4 * j + 4, :], y_turned[:, 4 * j:4 * j + 4, :],
                                       ACT.Copy).then_inc(s_y_hi, 1)
                if s - 3 in SCORE_AT:
                    h = SCORE_AT[s - 3]
                    act.wait_ge(s_turn, turn_no[("out", h)] + 1)
                    if h == HG:
                        act.wait_ge(s_turn, turn_no[("fin", 0, 1)] + 1)
                    act.activation(o_raw[:, h % HG, :, :], bank[6][:, 0:2 * DV].rearrange("p (t n) -> p t n", t=TT),
                                   ACT.Copy).then_inc(s_act, 1)
                    count[0] += 1
                    if h >= 1:
                        act.wait_ge(s_turn_read, turn_no[("out", h - 1)] + 1)
                    for t in range(TT):
                        n = TT * (h % HG) + t
                        ins = act.activation(junk[:, 0:DV], bank[6][:, DV * t:DV * t + DV], ACT.Square, bias=zero,
                                             accum_out=o_ss[:, n:n + 1])
                        if t == 0:
                            link(ins)
                    ins.then_inc(s_turn_read, 1)
                    if h % HG == HG - 1:
                        act.wait_ge(s_turn_read, turn_no[("out", h)] + 1)
                        act.activation(o_ss[:, :], o_ss[:, :], ACT.Sqrt, bias=eps_subln,
                                       scale=1.0 / DV).then_inc(s_o_rms, 1)
                if s - 2 in SCORE_AT:
                    h = SCORE_AT[s - 2]
                    if h >= 1:
                        act.wait_ge(s_turn, turn_no[("out", h - 1)] + 1)
                    read_turn(("head", h), a_turned[:, :], bank[6][:, 0:P + SEQ])
                if s in SCORE_AT:
                    exps(SCORE_AT[s])
                if s in FINISH_AT:
                    g = FINISH_AT[s]
                    for half in range(2):
                        c0 = HG * g + 2 * half
                        read_turn(("fin", g, half), y_turned[:, c0:c0 + 2, :],
                                  bank[6][:, :].rearrange("p (c s) -> p c s", c=2), scale=gsub)
                if s in COLUMNS_AT:
                    for h in range(2):
                        columns(COLUMNS_AT[s], h)
                if s == NB_IN * SUB + 1:
                    act.wait_ge(s_w_used, 2 * NB_IN)
                    for t in range(TT):
                        act.dma_start(x1[:, t, :], x_v[t]).then_inc(s_x[t], 16)
                    act.wait_ge(s_turn, turn_no[("head", HEADS - 1)] + 1)
                    act.dma_start(wr_sb, wrt.rearrange("(p k) n -> p k n", k=KC)).then_inc(s_wr, 16)
                if s in BCAST_AT:
                    broadcast(BCAST_AT[s], acc[:, BCAST_AT[s], :])
            take_block(NB - 1)
            act.wait_ge(s_ysum, 1)
            act.activation(yrms, yrms, ACT.Sqrt, bias=eps_norm, scale=1.0 / D).then_inc(s_yrms, 1)
            act.wait_ge(s_y_gated, 2 * (NB - NB_IN))
            broadcast(2, acc[:, 0, :])
            for t in range(TT):
                act.wait_ge(s_x1, t + 1)
                act.activation(x_rows[:, t, :], x1[:, t, :], ACT.Square, bias=zero,
                               accum_out=h2rms[:, t:t + 1]).then_inc(s_xsq, 1)
                act.wait_ge(s_xsq, t + 1)
                act.activation(h2rms[:, t:t + 1], h2rms[:, t:t + 1], ACT.Sqrt, bias=eps_norm,
                               scale=1.0 / D).then_inc(s_h2rms, 1)
            for t in range(TT):
                act.wait_ge(s_h2, t + 1)
                act.dma_start(h2_rows[t * P:(t + 1) * P, :], y_sb[:, t, :]).then_inc(s_h2_store, 16)
                for j in range(4):
                    act.wait_ge(s_h2t, 4 * t + j + 1)
                    act.activation(y_turned[:, 4 * j:4 * j + 4, t * P:(t + 1) * P],
                                   bank[(4 * t + j) % 4][:, :].rearrange("p (k s) -> p k s", k=4),
                                   ACT.Copy).then_inc(s_h2t_read, 1)
            act.wait_ge(s_gexp_in, 1)
            act.activation(rt[:, R_EXP:R_EXP + TT * 5], rt[:, R_EXP:R_EXP + TT * 5], ACT.Exp,
                           bias=zero).then_inc(s_gexp, 1)

            broadcast(3, acc[:, 1, :])

            def xe_copy(b):
                return act.activation(xe_turned[:, b, 0:8, :], bank[2][:, 0:8 * CAP].rearrange("p (k s) -> p k s", k=8),
                                      ACT.Copy)

            def silu():
                return act.activation(silu_g, bank[0][UPPER:UPPER + CAP, :], ACT.Silu, bias=zero[0:CAP, :])

            def turned_copy():
                return act.activation(act_turned, bank[4][:, 0:4 * CAP].rearrange("p (j s) -> p j s", j=4), ACT.Copy)

            def y_copy(b):
                return act.activation(y_item[:, b, 0:512], bank[5][:, :], ACT.Copy)

            act.wait_ge(s_h2_store, 16 * TT)
            act.wait_ge(s_xe_psum, 1)
            xe_copy(0).then_inc(s_xe_act, 1)
            act.sem_inc(s_y_act, 1)
            with act.Fori(0, N_IT) as it:
                for u in range(UNROLL):
                    i = it * UNROLL + u
                    b = u % 2
                    act.wait_ge(s_w_used, it * (6 * UNROLL) + W_USED0 + 6 * u + 4)
                    silu().then_inc(s_silu_g, 1)
                    act.wait_ge(s_xe_psum, i + 2)
                    xe_copy(1 - b).then_inc(s_xe_act, 1)
                    act.wait_ge(s_at_psum, i + 1)
                    turned_copy().then_inc(s_at, 1)
                    act.wait_ge(s_w_used, it * (6 * UNROLL) + W_USED0 + 6 * u + 6)
                    act.wait_ge(s_y_free, i + 1)
                    y_copy(b).then_inc(s_y_act, 1)
            nx = act.value_load(n_extra[0:1, 0:1], min_val=0, max_val=MAX_EXTRA)
            with act.If(nx > 0):
                act.wait_ge(s_scatter[0], 16 * (NE // 2))
                with act.Fori(0, nx) as j:
                    act.wait_ge(x_xe, j + 1)
                    xe_copy(0).then_inc(x_xe_act, 1)
                    act.wait_ge(x_gu, j + 1)
                    silu().then_inc(x_silu, 1)
                    act.wait_ge(x_at, j + 1)
                    turned_copy().then_inc(x_atc, 1)
                    act.wait_ge(x_dn, j + 1)
                    y_copy(0).then_inc(x_ya, 1)

            for t in range(TT):
                act.wait_ge(s_fsum, t + 1)
                act.activation(ring[:, t, D:2 * D], ring[:, t, 0:D], ACT.Square, bias=zero,
                               accum_out=f_ss[:, t:t + 1]).then_inc(s_fsq, 1)
                act.wait_ge(s_fsq, t + 1)
                act.activation(f_ss[:, t:t + 1], f_ss[:, t:t + 1], ACT.Sqrt, bias=eps_norm,
                               scale=1.0 / D).then_inc(s_frms, 1)

        @block.vector
        def _(dve):
            count = [0]

            def link(ins):
                count[0] += 1
                ins.then_inc(s_dve, 1)
                dve.wait_ge(s_dve, count[0])

            def ada(what):
                i, q = what[1], 2 * what[2] + what[3] // 2
                n = dve_order.index(what)
                if q == 0 and what[3] == 0:
                    dve.wait_ge(s_turn, turn_no[("col", i - 2, 1)] + 1)
                w = landed(dve, what).rearrange("p (k n) -> p k n", k=8)
                a = acc[:, i % 2, QUARTER * q:QUARTER * (q + 1)]
                for k in range(8):
                    row = 8 * (n % 2) + k
                    sc = silu_c[:, row:row + 1]
                    if row == 0:
                        ins = dve.tensor_scalar(a, w[:, k, :], sc, None, ALU.mult)
                    else:
                        ins = dve.scalar_tensor_tensor(a, w[:, k, :], sc, a, ALU.mult, ALU.add)
                    if k < 7:
                        link(ins)
                ins.then_inc(s_ada_dve, 1)
                dve.wait_ge(s_ada_dve, n + 1)

            dve.wait_ge(s_cexp, 1)
            link(dve.tensor_scalar(c_exp, c_exp, 1.0, None, ALU.add))
            link(dve.reciprocal(c_exp, c_exp))
            dve.tensor_tensor(silu_c, c_exp, par[:, A_C:A_C + KC], ALU.mult).then_inc(s_silu_c, 1)
            dve.wait_ge(s_lam_in, 16)
            for n in range(2):
                ins = dve.tensor_tensor_reduce(junk[:, 0:DK], rt[:, 2 * DK * n:2 * DK * n + DK],
                                               rt[:, 2 * DK * n + DK:2 * DK * (n + 1)], 1.0, 0.0,
                                               ALU.mult, ALU.add, lam_s[:, n:n + 1])
                if n == 0:
                    link(ins)
            ins.then_inc(s_lam, 1)
            dve.wait_ge(s_lam_e, 1)
            link(dve.scalar_tensor_tensor(neg_lam, lam_e[:, 1:2], LAM_INIT, lam_e[:, 0:1],
                                          ALU.subtract, ALU.subtract))
            link(dve.tensor_scalar(gsub, par[:, A_GSUB:A_GSUB + 1], 1.0 - LAM_INIT, None, ALU.mult))
            dve.wait_ge(s_rms, 1)
            link(dve.reciprocal(xrms, rms))
            for t in range(TT):
                dve.tensor_scalar(x_rows[:, t, :], x_rows[:, t, :], xrms[:, t:t + 1], None,
                                  ALU.mult).then_inc(s_xn, 1)

            def col_ready(i, h=1):
                dve.wait_ge(s_turn_read, turn_no[("col", i, h)] + 1)

            def split_w(s, units=range(UNITS)):
                for u in units:
                    v = UNITS * s + u
                    w_f32, w_lo, buf = unit_weights(v)
                    dve.wait_ge(s_w_hi, v + 1)
                    dve.tensor_tensor(w_lo, w_f32, w_hi[:, buf, :].bitcast(F32),
                                      ALU.subtract).then_inc(s_w_lo, 1)

            for h in range(2):
                half = slice(KH * h, KH * h + KH)
                col_ready(0, h)
                link(dve.scalar_tensor_tensor(cols[:, 0, half], mods[:, SC1, half], 1.0,
                                              par[:, A_GPRE1 + KH * h:A_GPRE1 + KH * h + KH],
                                              ALU.add, ALU.mult))
                col_ready(1, h)
                if h == 0:
                    dve.wait_ge(s_xt_read, KC // 2)
                for j in range(2 * h, 2 * h + 2):
                    for k in range(4 * j, 4 * j + 4):
                        ins = dve.tensor_scalar(lo_f32[:, k, :], h_turned[:, k, :], cols[:, 0, k:k + 1],
                                                mods[:, SH1, k:k + 1], ALU.mult, ALU.add)
                    ins.then_inc(s_h, 1)
                for j in range(2 * h, 2 * h + 2):
                    dve.wait_ge(s_h_hi, j + 1)
                    dve.tensor_tensor(h_lo[:, 4 * j:4 * j + 4, :], lo_f32[:, 4 * j:4 * j + 4, :],
                                      h_hi[:, 4 * j:4 * j + 4, :].bitcast(F32), ALU.subtract).then_inc(s_h_lo, 1)
                if h == 0:
                    for s in range(AHEAD):
                        split_w(s)

            def shift(h):
                dve.wait_ge(s_scores, h + 1)
                for m in range(2):
                    link(dve.scalar_tensor_tensor(soft[:, m, :], dist, -(0.5 ** (8.0 / HEADS)) ** (h + 1),
                                                  bank[4 + m][:, 0:P + SEQ], ALU.mult, ALU.add))
                link(dve.tensor_reduce(mx[:, 0::2], soft[:, :, 0:P], AX_X, ALU.max))
                link(dve.tensor_reduce(mx[:, 1::2], soft[:, :, P:P + SEQ], AX_X, ALU.max))
                dve.tensor_scalar(mx[:, :], mx[:, :], -1.0, None, ALU.mult).then_inc(s_shift, 1)

            def combine(h):
                dve.wait_ge(s_prob, h + 1)
                link(dve.reciprocal(p_rec[:, :], p_sum[:, :]))
                link(dve.tensor_scalar(p_rec[:, 2:4], p_rec[:, 2:4], neg_lam, None, ALU.mult))
                for t, span in enumerate((slice(0, P), slice(P, P + SEQ))):
                    link(dve.tensor_scalar(soft[:, 1, span], soft[:, 1, span], p_rec[:, 2 + t:3 + t], None, ALU.mult))
                    ins = dve.scalar_tensor_tensor(soft[:, 0, span], soft[:, 0, span], p_rec[:, t:t + 1],
                                                   soft[:, 1, span], ALU.mult, ALU.add)
                    if t == 0:
                        link(ins)
                ins.then_inc(s_a, 1)

            def split_y(groups):
                for j in groups:
                    dve.wait_ge(s_y_hi, j + 1)
                    dve.tensor_tensor(y_lo[:, 4 * j:4 * j + 4, :], y_turned[:, 4 * j:4 * j + 4, :],
                                      y_hi[:, 4 * j:4 * j + 4, :].bitcast(F32), ALU.subtract).then_inc(s_y_lo, 1)

            def norm_heads(g):
                dve.wait_ge(s_o_rms, g + 1)
                link(dve.reciprocal(o_rec[:, :], o_ss[:, :]))
                for h in range(HG):
                    for t in range(TT):
                        n = TT * h + t
                        ins = dve.tensor_scalar(o_raw[:, h, t, :], o_raw[:, h, t, :], o_rec[:, n:n + 1], None,
                                                ALU.mult)
                        if n < HG * TT - 1:
                            link(ins)
                ins.then_inc(s_o_norm, 1)

            def take_block(b):
                if b >= NB_IN:
                    g = b - NB_IN
                    dve.wait_ge(s_turn_read, turn_no[("bc", 0, 3)] + 1)
                    for n in range(TT):
                        dve.wait_ge(s_block_act, 2 * act_evac.index(b) + n + 1)
                        span = slice(512 * g, 512 * g + 512)
                        dve.tensor_tensor(y_sb[:, n, span], bank[BANKS[b][n]][:, :], acc[:, 0, span],
                                          ALU.mult).then_inc(s_y_gated, 1)
                    return
                if b not in dve_evac:
                    return
                kind, g = BLOCKS[b]
                dve.wait_ge(s_w_used, BLOCK_USED[b])
                c0 = HEADS + HG * g
                if kind == "X":
                    dve.wait_ge(s_block_act, 2 * (act_evac.index(b - 1) + 1))
                    link(dve.memset(conv_in[:, :, 0:2], 0.0))
                for n in range(2):
                    two = bank[BANKS[b][n]][:, :].rearrange("p (c s) -> p c s", c=2)
                    yc = y_turned[:, c0 + 2 * n:c0 + 2 * n + 2, :]
                    dst = conv_in[:, 2 * n:2 * n + 2, 2:] if kind == "X" else yc
                    dve.tensor_tensor(dst, two, yc, ALU.mult).then_inc(s_block_dve, 1)
                dve.wait_ge(s_block_dve, 2 * (dve_evac.index(b) + 1))
                if kind == "X":
                    for c in range(HG):
                        y = y_turned[:, c0 + c, :]
                        for i in range(3):
                            w = par[:, A_WCONV + HEADS * i + HG * g + c:A_WCONV + HEADS * i + HG * g + c + 1]
                            z = conv_in[:, c, i:i + SEQ]
                            if i == 0:
                                link(dve.tensor_scalar(y, z, w, None, ALU.mult))
                            else:
                                link(dve.scalar_tensor_tensor(y, z, w, y, ALU.mult, ALU.add))

            for s, (b, part) in enumerate(SUBSTEPS):
                if s == NB_IN * SUB:
                    split_y(range(2))
                if s >= 1 and SUBSTEPS[s - 1][1] == SUB - 1:
                    take_block(SUBSTEPS[s - 1][0])
                if s == NB_IN * SUB:
                    split_y(range(2, 4))
                if s - 1 in SCORE_AT:
                    combine(SCORE_AT[s - 1])
                ahead = AHEAD <= s + 1 < len(SUBSTEPS)
                if ahead:
                    split_w(s + 1, [0])
                if s in SCORE_AT:
                    shift(SCORE_AT[s])
                if ahead:
                    split_w(s + 1, [1])
                if s + 1 in FINISH_AT:
                    norm_heads(FINISH_AT[s + 1])
                for what in ADA_AT.get(s, []):
                    if what in dve_order:
                        ada(what)
                if s - 1 in COLUMNS_AT:
                    i = COLUMNS_AT[s - 1]
                    if i == 2:
                        col_ready(i)
                        dve.tensor_tensor(cols[:, 1, :], mods[:, GT1, :], par[:, A_GPOST1:A_GPOST1 + KC],
                                          ALU.mult).then_inc(s_cols, 2)
                    if i == 4:
                        col_ready(i)
                        dve.scalar_tensor_tensor(cols[:, 2, :], mods[:, SC2, :], 1.0,
                                                 par[:, A_GPRE2:A_GPRE2 + KC], ALU.add, ALU.mult).then_inc(s_cols, 1)
                    if i == 5:
                        col_ready(i)
                        dve.tensor_tensor(cols[:, 3, :], mods[:, GT2, :], par[:, A_GPOST2:A_GPOST2 + KC],
                                          ALU.mult).then_inc(s_cols, 1)
            take_block(NB - 1)

            dve.wait_ge(s_block_act, 2 * len(act_evac))
            dve.tensor_reduce(yrms, y_ss[:, :, :], AX_X, ALU.add).then_inc(s_ysum, 1)
            dve.wait_ge(s_yrms, 1)
            link(dve.reciprocal(yrms, yrms))
            dve.wait_ge(s_turn_read, turn_no[("bc", 1, 3)] + 1)
            dve.wait_ge(s_y_gated, 2 * (NB - NB_IN))

            def residual(t):
                dve.wait_ge(s_x[t], 32)
                dve.scalar_tensor_tensor(x1[:, t, :], y_sb[:, t, :], yrms[:, t:t + 1], x1[:, t, :],
                                         ALU.mult, ALU.add).then_inc(s_x1, 1)
                dve.wait_ge(s_x1, t + 1)
                dve.tensor_tensor(y_sb[:, t, :], x1[:, t, :], acc[:, 1, :], ALU.mult).then_inc(s_x1a, 1)

            def second_norm(t):
                dve.wait_ge(s_h2rms, t + 1)
                link(dve.reciprocal(h2rms[:, t:t + 1], h2rms[:, t:t + 1]))
                dve.wait_ge(s_x1a, t + 1)
                dve.scalar_tensor_tensor(y_sb[:, t, :], y_sb[:, t, :], h2rms[:, t:t + 1], acc[:, 0, :],
                                         ALU.mult, ALU.add).then_inc(s_h2, 1)

            residual(0)
            dve.wait_ge(s_turn_read, turn_no[("bc", 2, 3)] + 1)
            second_norm(0)
            residual(1)
            second_norm(1)

            logit = rt[:, R_LOGIT:R_LOGIT + TT * 36].rearrange("p (t n) -> p t n", t=TT)
            outer = rt[:, R_OUTER:R_OUTER + TT * NE].rearrange("p (t g j) -> p t g j", t=TT, g=N_GROUPS)
            picked = rt[:, R_PICKED:R_PICKED + TT * 8].rearrange("p (t j) -> p t j", t=TT)
            same4 = rt[:, R_SAME4:R_SAME4 + TT * 4].rearrange("p (t g) -> p t g", t=TT)
            group = rt[:, R_GROUP:R_GROUP + TT * 4].rearrange("p (t g) -> p t g", t=TT)
            same8 = rt[:, R_SAME8:R_SAME8 + TT * 8].rearrange("p (t j) -> p t j", t=TT)
            inner = rt[:, R_INNER:R_INNER + 2 * TT * 8].rearrange("p (k t j) -> p k t j", k=2, t=TT)
            top = rt[:, R_MAX:R_MAX + 6 * TT].rearrange("p (n t) -> p n t", t=TT)
            exps = rt[:, R_EXP:R_EXP + TT * 5].rearrange("p (t n) -> p t n", t=TT)
            wts = rt[:, R_W:R_W + 2 * TT].rearrange("p (k t) -> p k t", k=2)
            hot = rt[:, R_HOT:R_HOT + 2 * TT * NE].rearrange("p (k t e) -> p k t e", k=2, t=TT)
            both = rt[:, R_BOTH:R_BOTH + TT * NE].rearrange("p (t e) -> p t e", t=TT)
            prod = rt[:, R_PROD:R_PROD + 6 * TT * NE].rearrange("p (n k t e) -> p n k t e", n=3, k=2, t=TT)
            red = rt[:, R_RED:R_RED + 6 * TT]
            pos = rt[:, R_POS:R_POS + 10 * TT]
            kt = 2 * TT

            def over(ap2, n):
                return ap2.unsqueeze(2).to_broadcast([P, TT, n])

            def first_of(values, n, maxima, same, hot_out, priority):
                link(dve.tensor_reduce(maxima, values, AX_X, ALU.max))
                link(dve.tensor_tensor(same, values, over(maxima, n), ALU.is_equal))
                link(dve.tensor_tensor(same, same, priority.unsqueeze(1).to_broadcast([P, TT, n]), ALU.mult))
                link(dve.tensor_reduce(top[:, 3, :], same, AX_X, ALU.max))
                link(dve.tensor_tensor(hot_out, same, over(top[:, 3, :], n), ALU.is_equal))

            dve.wait_ge(s_logit, 1)
            for t in range(TT):
                link(dve.tensor_tensor(logit[:, t, :], bank[4 + t][:, 0:36], par[:, A_BRT:A_BRT + 36], ALU.add))
            pri4 = cst[:, C_PRI4:C_PRI4 + 4]
            pri8 = cst[:, C_PRI8:C_PRI8 + 8]
            first_of(logit[:, :, 0:4], 4, top[:, 0, :], same4, group, pri4)
            link(dve.tensor_tensor(exps[:, :, 0:4], logit[:, :, 0:4], over(top[:, 0, :], 4), ALU.subtract))
            for t in range(TT):
                link(dve.tensor_tensor(outer[:, t, :, :],
                                       logit[:, t, 4:36].rearrange("p (g j) -> p g j", g=N_GROUPS),
                                       group[:, t, :].unsqueeze(2).to_broadcast([P, N_GROUPS, 8]), ALU.mult))
            link(dve.tensor_reduce(picked, outer.rearrange("p t g j -> p t j g"), AX_X, ALU.add))
            first_of(picked, 8, top[:, 1, :], same8, inner[:, 0, :, :], pri8)
            link(dve.scalar_tensor_tensor(picked, inner[:, 0, :, :], -1e30, picked, ALU.mult, ALU.add))
            first_of(picked, 8, top[:, 2, :], same8, inner[:, 1, :, :], pri8)
            dve.tensor_tensor(exps[:, :, 4:5], over(top[:, 2, :], 1), over(top[:, 1, :], 1),
                              ALU.subtract).then_inc(s_gexp_in, 1)
            for k in range(2):
                for t in range(TT):
                    link(dve.tensor_tensor(hot[:, k, t, :].rearrange("p (g j) -> p g j", g=N_GROUPS),
                                           group[:, t, :].unsqueeze(2).to_broadcast([P, N_GROUPS, 8]),
                                           inner[:, k, t, :].unsqueeze(1).to_broadcast([P, N_GROUPS, 8]), ALU.mult))
            dve.tensor_tensor(both, hot[:, 0, :, :], hot[:, 1, :, :], ALU.add).then_inc(s_picks, 1)
            dve.wait_ge(s_gexp, 1)
            link(dve.tensor_reduce(top[:, 4, :], exps[:, :, 0:4], AX_X, ALU.add))
            link(dve.tensor_scalar(top[:, 5, :].unsqueeze(2), exps[:, :, 4:5], 1.0, None, ALU.add))
            link(dve.tensor_tensor(top[:, 4, :], top[:, 4, :], top[:, 5, :], ALU.mult))
            link(dve.reciprocal(wts[:, 0, :], top[:, 4, :]))
            link(dve.tensor_tensor(wts[:, 1, :].unsqueeze(2), wts[:, 0, :].unsqueeze(2), exps[:, :, 4:5], ALU.mult))
            dve.wait_ge(s_rank, 1)
            n_e = bank[7][0:NE, 0:1]
            extra = rt[0:NE, R_EXTRA:R_EXTRA + 1]
            n_sb = rt[0:NE, R_EXTRA + 1:R_EXTRA + 2]
            link(dve.tensor_copy(n_sb, n_e))
            link(dve.tensor_scalar(extra, n_sb, CAP + 0.5, None, ALU.is_ge))
            for full in range(2 * CAP, SEQ, CAP):
                ins = dve.scalar_tensor_tensor(extra, n_sb, full + 0.5, extra, ALU.is_ge, ALU.add)
                if full + CAP < SEQ:
                    link(ins)
            ins.then_inc(s_extra, 1)
            for k in range(2):
                dve.tensor_tensor(prod[:, 0, k, :, :], hot[:, k, :, :],
                                  bank[6][:, 0:TT * NE].rearrange("p (t e) -> p t e", t=TT),
                                  ALU.mult).then_inc(s_rank_used, 1)
            dve.wait_ge(s_rank_used, 2)
            for k in range(2):
                link(dve.tensor_tensor(prod[:, 2, k, :, :], hot[:, k, :, :],
                                       cst[:, C_IOTA:C_IOTA + NE].unsqueeze(1).to_broadcast([P, TT, NE]), ALU.mult))
            dve.wait_ge(s_base, 1)
            for k in range(2):
                link(dve.tensor_tensor(prod[:, 1, k, :, :], hot[:, k, :, :],
                                       bank[7][:, 0:NE].unsqueeze(1).to_broadcast([P, TT, NE]), ALU.mult))
            link(dve.tensor_copy(n_extra[:, :], bank[7][:, NE:NE + 1]))
            link(dve.tensor_reduce(red, prod.rearrange("p n k t e -> p (n k t) e"), AX_X, ALU.add))
            rank, base, expert = red[:, 0:kt], red[:, kt:2 * kt], red[:, 2 * kt:3 * kt]
            lot, beyond, dlt, slot, item = (pos[:, kt * n:kt * (n + 1)] for n in range(5))
            link(dve.tensor_scalar(beyond, rank, CAP - 0.5, None, ALU.is_ge))
            for full in range(2 * CAP, SEQ, CAP):
                link(dve.scalar_tensor_tensor(lot, rank, full - 0.5, beyond if full == 2 * CAP else lot,
                                              ALU.is_ge, ALU.add))
            link(dve.scalar_tensor_tensor(slot, lot, -float(CAP), rank, ALU.mult, ALU.add))
            link(dve.tensor_tensor(dlt, base, lot, ALU.add))
            link(dve.scalar_tensor_tensor(dlt, dlt, NE - 1.0, expert, ALU.add, ALU.subtract))
            link(dve.tensor_tensor(dlt, dlt, beyond, ALU.mult))
            link(dve.tensor_tensor(item, dlt, expert, ALU.add))
            for n in range(kt):
                k, t = divmod(n, TT)
                link(dve.tensor_scalar(hot_slot(n), cst[:, C_SLOT:C_SLOT + P], slot[:, n:n + 1], None, ALU.is_equal))
                hi = hot_item(n)
                link(dve.tensor_scalar(hi[:, 3, :], cst[:, C_IOTA:C_IOTA + ITEMS], item[:, n:n + 1], None, ALU.is_equal))
                for col, val in ((0, cst[:, C_TOK + t:C_TOK + t + 1]), (1, cst[:, C_OUT + n:C_OUT + n + 1]),
                                 (2, wts[:, k, t:t + 1]), (4, expert[:, n:n + 1])):
                    ins = dve.tensor_scalar(hi[:, col, :], hi[:, 3, :], val, None, ALU.mult)
                    if (n, col) != (kt - 1, 4):
                        link(ins)
            ins.then_inc(s_hot, 1)
            dve.wait_ge(s_table, 1)
            table = acc[:, 0, T_TABLE:T_TABLE + 5 * ITEMS].rearrange("p (a b) -> p a b", a=5)
            miss = acc[:, 0, T_MISS:T_MISS + ITEMS]
            row = acc[:, 0, T_MISS + ITEMS:T_MISS + 2 * ITEMS]
            link(dve.tensor_copy(table, bank[7][:, 0:5 * ITEMS].rearrange("p (a b) -> p a b", a=5)))
            link(dve.tensor_scalar(miss, table[:, 3, :], -NOWHERE, NOWHERE, ALU.mult, ALU.add))
            link(dve.tensor_tensor(g_idx[:, :], table[:, 0, :], miss, ALU.add))
            link(dve.scalar_tensor_tensor(row, table[:, 1, :], 2.0, miss, ALU.mult, ALU.add))
            link(dve.tensor_scalar(s_idx[:, :], row, cst[:, C_GRP:C_GRP + 1], None, ALU.add))
            link(dve.tensor_copy(e_idx[:, :], table[:, 4, :]))
            dve.tensor_copy(weight[:, :], table[:, 2, :]).then_inc(s_tables, 1)
            dve.wait_ge(s_tables, 1)

            def xe_copy(b):
                return dve.tensor_copy(xe_turned[:, b, 8:16, :], bank[3][:, 0:8 * CAP].rearrange("p (k s) -> p k s", k=8))

            def weigh(column):
                return dve.scalar_tensor_tensor(act_rows, silu_g, weight[0:CAP, column], bank[0][0:CAP, :],
                                                ALU.mult, ALU.mult)

            def y_copy(b):
                return dve.tensor_copy(y_item[:, b, 512:1024], bank[6][:, :])

            dve.wait_ge(s_h2_store, 16 * TT)
            dve.wait_ge(s_xe_psum, 1)
            xe_copy(0).then_inc(s_xe_dve, 1)
            dve.sem_inc(s_y_dve, 1)
            with dve.Fori(0, N_IT) as it:
                for u in range(UNROLL):
                    i = it * UNROLL + u
                    b = u % 2
                    dve.wait_ge(s_silu_g, i + 1)
                    weigh(bass.ds(i, 1)).then_inc(s_act_rows, 1)
                    dve.wait_ge(s_xe_psum, i + 2)
                    xe_copy(1 - b).then_inc(s_xe_dve, 1)
                    dve.wait_ge(s_w_used, it * (6 * UNROLL) + W_USED0 + 6 * u + 6)
                    dve.wait_ge(s_y_free, i + 1)
                    y_copy(b).then_inc(s_y_dve, 1)
            nx = dve.value_load(n_extra[0:1, 0:1], min_val=0, max_val=MAX_EXTRA)
            with dve.If(nx > 0):
                dve.wait_ge(s_scatter[0], 16 * (NE // 2))
                with dve.Fori(0, nx) as j:
                    dve.wait_ge(x_xe, j + 1)
                    xe_copy(0).then_inc(x_xe_dve, 1)
                    dve.wait_ge(x_silu, j + 1)
                    weigh(bass.ds(j + NE, 1)).then_inc(x_rows_done, 1)
                    dve.wait_ge(x_dn, j + 1)
                    y_copy(0).then_inc(x_yd, 1)
            for t in range(TT):
                dve.wait_ge(s_pair[t], 16)
                dve.tensor_tensor(ring[:, t, 0:D], ring[:, t, 0:D], ring[:, t, D:2 * D], ALU.add).then_inc(s_fsum, 1)
            for t in range(TT):
                dve.wait_ge(s_frms, t + 1)
                link(dve.reciprocal(f_ss[:, t:t + 1], f_ss[:, t:t + 1]))
                link(dve.scalar_tensor_tensor(ring[:, t, 0:D], ring[:, t, 0:D], f_ss[:, t:t + 1], acc[:, 1, :],
                                              ALU.mult, ALU.mult))
                dve.tensor_tensor(x1[:, t, :], x1[:, t, :], ring[:, t, 0:D], ALU.add).then_inc(s_fin, 1)


def constants():
    import numpy as np
    c = np.zeros((P, C_ALL), np.float32)
    p = np.arange(P)
    c[:, C_ID:C_ID + P] = np.eye(P)
    c[:, C_TRI:C_TRI + P] = p[:, None] < p[None, :]
    c[:, C_ONE:C_ONE + P] = 1.0
    for t, (c0, n) in enumerate(((C_DIST, P), (C_DIST + P, SEQ))):
        q, k = t * P + p[:, None], np.arange(n)[None, :]
        c[:, c0:c0 + n] = np.where(k // CHUNK <= q // CHUNK, np.abs(q - k), 1e37)
    c[:, C_SLOT:C_SLOT + P] = p % UPPER
    c[:, C_IOTA:C_IOTA + ITEMS] = np.arange(ITEMS)
    c[:, C_PRI8:C_PRI8 + 8] = 8 - np.arange(8)
    c[:, C_PRI4:C_PRI4 + 4] = 4 - np.arange(4)
    for n in range(2 * TT):
        c[:, C_OUT + n] = n * P + p
    for t in range(TT):
        c[:, C_TOK + t] = t * P + p
    c[:, C_GRP] = p >= UPPER
    c[:, C_TILE] = p % COL_TILE == 0
    return c


def kernel(**inputs):
    import numpy as np
    import concourse.bacc as bacc
    from concourse.bass_utils import run_bass_kernel_spmd

    a = {name: np.asarray(v) for name, v in inputs.items()}

    def column(v):
        return v.reshape(2, P, KH).transpose(1, 0, 2).reshape(P, KC)

    def over_partitions(v):
        return np.broadcast_to(v.reshape(1, -1), (P, v.size))

    small = np.concatenate([
        a["c"][0].reshape(P, KC), column(a["g_pre1"][0]), column(a["g_post1"][0]), column(a["g_pre2"][0]),
        column(a["g_post2"][0]),
        a["b_ada"][0].reshape(6, 2, P, KH).transpose(2, 0, 1, 3).reshape(P, 6 * KC),
        a["w_conv"][0].reshape(3, HEADS, P).transpose(2, 0, 1).reshape(P, 3 * HEADS),
        a["g_subln"][0].reshape(P, 1),
        over_partitions(a["b_router_g"][0]), over_partitions(a["b_router_e"][0]),
        over_partitions(np.array([NORM_EPS, SUBLN_EPS, 0.0], np.float32))], axis=1)
    lam = over_partitions(np.concatenate([a[n][0] for n in ("lam_q1", "lam_k1", "lam_q2", "lam_k2")]))
    router = np.concatenate([a["w_router_g"][0], a["w_router_e"][0].reshape(D, NE)], axis=1)
    feeds = {"consts": constants(), "small": small, "lam": lam, "router": router}
    feeds.update({n: a[n] for n in ("x", "w_ada", "w_in", "w_out", "w_gate", "w_up", "w_down")})

    nc = bacc.Bacc("TRN2", target_bir_lowering=False, num_devices=1)
    arrays, args = {}, []
    for name, v in feeds.items():
        v = np.ascontiguousarray(v)
        arrays[name + "_dram"] = v
        args.append(nc.dram_tensor(name + "_dram", v.shape, mybir.dt.from_np(v.dtype), kind="ExternalInput").ap())
    args.append(nc.dram_tensor("out_dram", (1, SEQ, D), F32, kind="ExternalOutput").ap())
    hybrid_layer(nc, *args)
    r = run_bass_kernel_spmd(nc, [arrays], core_ids=[0])
    return r.results[0]["out_dram"]
```

```python
import math
from contextlib import ExitStack

import concourse.bass as bass
from concourse import mybir

ALU = mybir.AluOpType
ACT = mybir.ActivationFunctionType
F32 = mybir.dt.float32
F32R = mybir.dt.float32r
I32 = mybir.dt.int32
AX_X = mybir.AxisListType.X

P = 128
D = 2048
SEQ = 256
TT = SEQ // P
KC = D // P
KH = KC // 2
HEADS = 8
DK = 64
DV = 128
HG = 4
N_GROUPS = 4
PER_GROUP = 8
NE = N_GROUPS * PER_GROUP
N_LOGITS = N_GROUPS + NE
FE = 512
CHUNK = 64
LAM_INIT = 0.8 - 0.6 * math.exp(-0.3 * 0)
NORM_EPS = 1e-6
SUBLN_EPS = 1e-5
CAP = 40
UPPER = 64
MAX_EXTRA = (2 * SEQ - NE) // CAP
ITEMS = NE + MAX_EXTRA
PAIR = UPPER + CAP
NOWHERE = 4096.0

RING = 8
RING1 = 6
SPARE = RING - RING1
HI_SLOT, LO_SLOT = RING1, RING1 + 1
SLOT = 4096
UNROLL = 4

C_ID = 0
C_TRI = C_ID + P
C_ONE = C_TRI + P
C_DIST = C_ONE + P
C_SLOT = C_DIST + P + SEQ
C_IOTA = C_SLOT + P
C_PRI8 = C_IOTA + ITEMS
C_PRI4 = C_PRI8 + 8
C_VALS = C_PRI4 + 4
N_LOTS = (SEQ - 1) // CAP
C_FULL = C_VALS + 8 * TT
C_GRP = C_FULL + N_LOTS
C_TILE = C_GRP + 1
C_ALL = C_TILE + 1
A_C = 0
A_GPRE1 = A_C + KC
A_GPOST1 = A_GPRE1 + KC
A_GPRE2 = A_GPOST1 + KC
A_GPOST2 = A_GPRE2 + KC
A_BADA = A_GPOST2 + KC
A_WCONV = A_BADA + 6 * KC
A_GSUB = A_WCONV + 3 * HEADS
A_BRT = A_GSUB + 1
A_EPS = A_BRT + N_GROUPS + NE
A_ALL = A_EPS + 3

R_LOGIT = 0
R_OUTER = R_LOGIT + TT * (N_GROUPS + NE)
R_PICKED = R_OUTER + TT * NE
R_SAME4 = R_PICKED + TT * 8
R_GROUP = R_SAME4 + TT * 4
R_SAME8 = R_GROUP + TT * 4
R_INNER = R_SAME8 + TT * 8
R_MAX = R_INNER + 2 * TT * 8
R_EXP = R_MAX + 6 * TT
R_VALS = R_EXP + TT * 5
R_HOT = R_VALS + 8 * TT
R_BOTH = R_HOT + 2 * TT * NE
R_PROD = R_BOTH + TT * NE
R_RED = R_PROD + 3 * 2 * TT * NE
R_POS = R_RED + 3 * 2 * TT
R_EXTRA = R_POS + 5 * 2 * TT
R_OVER = R_EXTRA + 2
R_ALL = R_OVER + 2 * TT * N_LOTS
assert R_ALL <= HG * TT * DV
T_SLOT = 0
T_ITEM = T_SLOT + 2 * TT * P
T_TABLE = T_ITEM + 2 * TT * 4 * ITEMS
T_MISS = T_TABLE + 4 * ITEMS
assert T_MISS + 2 * ITEMS <= D
G_SLOT = 0
G_ITEM = G_SLOT + 2 * TT * CAP
G_PICK = G_ITEM + 2 * TT * ITEMS
assert G_PICK + 2 * TT * CAP <= 2 * (P + SEQ) and CAP <= ITEMS

BLOCKS = [("q", 0), ("k", 0), ("v", 0), ("C", 0), ("X", 0), ("q", 1), ("k", 1), ("v", 1),
          ("C", 1), ("X", 1), ("B", 0), ("B", 1)]
COL0 = {"q": 0, "k": 1024, "v": 2048, "B": 3072, "C": 4096, "X": 5120}
NB_IN = len(BLOCKS)
NB = NB_IN + D // 512
SUB = 4
UNITS = 2
HI_BUFS = 4
MODS = [1, 0, 2, 3, 4, 5]
SH1, SC1, GT1, SH2, SC2, GT2 = range(6)
W_ORDER = [(b, h) for h in range(2) for b in range(3)] + [(b, h) for b in range(3, NB) for h in range(2)]
SUBSTEPS = [(b, SUB // 2 * h + i) for b, h in W_ORDER for i in range(SUB // 2)]
BANKS = {b: (4, 5) if b == 2 else (2 * (b % 2), 2 * (b % 2) + 1) for b in range(NB)}
SCORE_AT = {4 * SUB - 3 + 2 * h if h < HG else 8 * SUB + 1 + 2 * (h - HG): h for h in range(HEADS)}
FINISH_AT = {6 * SUB: 0, 11 * SUB: 1}
ADA_UNITS = 4
QUARTER = D // 4
COL_TILE = 32
DVE_HALVES = ((2, 0), (2, 1), (4, 0))
LAST_MOD = 5


def plan_ring():
    def early(h):
        return [("ada", i, h, r) for i in range(2) for r in range(ADA_UNITS)]
    late = [("ada", 2 + j, h, r) for h in range(2) for r in range(ADA_UNITS) for j in range(2)]
    late += [("ada", 4, 1 - j, r) for r in range(ADA_UNITS) for j in range(2)]
    last = [("ada", LAST_MOD, h, r) for h in range(2) for r in range(ADA_UNITS)]
    plan = early(0)
    for b in range(3):
        plan += [("w", b, 0)] + early(1)[2 * b:2 * b + 2]
    plan += early(1)[6:]
    spread = 2 * NB_IN - 3
    for n, (b, h) in enumerate(W_ORDER[3:]):
        plan.append(("w", b, h))
        if n < spread:
            plan += late[len(late) * n // spread:len(late) * (n + 1) // spread]
        plan += last[max(n - spread + 1, 0):max(n - spread + 2, 0)]
    return plan


PLAN = plan_ring()
EARLY = [what for what in PLAN if what[0] == "ada" and what[1] < 2]
ADA_AT = {1: EARLY[8:10], 3: EARLY[10:12], 5: EARLY[12:]}
for _what in PLAN:
    if _what[0] == "w":
        _at = 2 * W_ORDER.index(_what[1:])
    elif _what[1] >= 2:
        _s = _at if _at not in ADA_AT and _what[1] != LAST_MOD else _at + 1
        ADA_AT.setdefault(_s, []).append(_what)
LAST_STEP = {w[1:3]: s for s, q in ADA_AT.items() for w in q}
COLUMNS_AT = {}
for (_i, _h), _s in sorted(LAST_STEP.items()):
    if _i >= 2:
        COLUMNS_AT.setdefault(max(LAST_STEP[(_i, 0)], LAST_STEP[(_i, 1)]) + 3 if _i < LAST_MOD else _s + 2, []).append((_i, _h))
BCAST_AT = {NB_IN * SUB + s: w for s, w in
            {2: (0, 0), 3: (0, 1), 5: (0, 2), 6: (0, 3), 8: (1, 0), 9: (1, 1), 10: (1, 2), 11: (1, 3),
             13: (2, 0), 14: (2, 1)}.items()}
EXPERT_SLOTS = [(len(PLAN) + m) % RING1 for m in range(RING1)] + [HI_SLOT, LO_SLOT]
USES0 = [len(range(i, len(PLAN), RING1)) if i < RING1 else 0 for i in range(RING)]
W_USED0 = 2 * NB + 2 * ADA_UNITS + SPARE
assert (UNROLL * 6) % RING == 0
AHEAD = 3 * SUB // 2
W_SLOTS = [what for what in PLAN if what[0] == "w" or what[1] == LAST_MOD]
BLOCK_USED = {b: W_SLOTS.index(("w", b, 1)) + 1 for b in range(NB)}
assert all(what in W_SLOTS for what in PLAN[-RING1:])
assert min(s for s, q in COLUMNS_AT.items() if (4, 1) in q) <= min(BCAST_AT)
assert max(COLUMNS_AT) < len(SUBSTEPS)


def hybrid_layer(nc, consts, small, lam, wrt, x, w_ada, w_in, w_out, w_gate, w_up, w_down, out):
    ctx = ExitStack()
    with ctx:
        def sb(name, shape, dt=F32):
            return ctx.enter_context(nc.sbuf_tensor(name, shape, dt))

        def sem(name):
            return ctx.enter_context(nc.semaphore(name))

        y_rows = nc.dram_tensor("y_rows", (4 * SEQ, D // 2), F32, kind="Internal").ap()

        with ExitStack() as names:
            ring_r = [names.enter_context(nc.sbuf_tensor(f"ring_r{n}", [P, SLOT], F32R)) for n in range(RING)]
            region_a_r = names.enter_context(nc.sbuf_tensor("region_a_r", [P, 2 * D], F32R))
            region_b_r = names.enter_context(nc.sbuf_tensor("region_b_r", [P, 2 * D], F32R))
        ring = sb("ring", [P, RING, SLOT])
        region_a = sb("region_a", [P, 2 * D])
        region_b = sb("region_b", [P, 2 * D])
        region_c = sb("region_c", [P, 2 * D + 8])
        acc = sb("acc", [P, 2, D])
        soft = sb("soft", [P, 2, P + SEQ])
        o_raw = sb("o_raw", [P, HG, TT, DV])
        a_turned = sb("a_turned", [P, P + SEQ])
        cst = sb("cst", [P, C_ALL])
        par = sb("par", [P, A_ALL])
        sml = sb("sml", [P, 64])
        mods = sb("mods", [P, 6, KC])
        cols = sb("cols", [P, 4, KC])

        bank = [ctx.enter_context(nc.psum_tensor(f"bank{i}", [P, 512], F32)) for i in range(8)]

        x_rows = region_a[:, :].rearrange("p (t d) -> p t d", t=TT)
        y_turned = region_a[:, :].rearrange("p (c s) -> p c s", s=SEQ)
        h_turned = region_b[:, :].rearrange("p (k s) -> p k s", s=SEQ)
        h_hi = region_b_r[:, :].rearrange("p (k s) -> p k s", s=SEQ)
        h_lo = y_hi = ring_r[LO_SLOT][:, :].rearrange("p (k s) -> p k s", s=SEQ)
        lo_f32 = ring[:, LO_SLOT, :].rearrange("p (k s) -> p k s", s=SEQ)
        y_lo = region_a_r[:, :].rearrange("p (k s) -> p k s", s=SEQ)
        w_hi = ring_r[HI_SLOT][:, :].rearrange("p (b n) -> p b n", b=HI_BUFS)
        x1 = region_b[:, :].rearrange("p (t d) -> p t d", t=TT)
        q_turned = region_c[:, 0:1024].rearrange("p (c s) -> p c s", s=SEQ)
        k_turned = region_c[:, 1024:2048].rearrange("p (c s) -> p c s", s=SEQ)
        v_rows = region_c[:, 2048:3072].rearrange("p (t n) -> p t n", t=TT)
        conv_in = region_c[:, 3072:3072 + HG * (SEQ + 2)].rearrange("p (c s) -> p c s", s=SEQ + 2)
        y_sb = region_c[:, 0:2 * D].rearrange("p (t d) -> p t d", t=TT)
        wr_sb = soft[:, :, :].rearrange("p a b -> p (a b)")[:, 0:KC * N_LOGITS].rearrange("p (k n) -> p k n", k=KC)
        rt = o_raw[:, :, :, :].rearrange("p a b c -> p (a b c)")

        ident = cst[:, C_ID:C_ID + P]
        tri = cst[:, C_TRI:C_TRI + P]
        ones = cst[:, C_ONE:C_ONE + P]
        dist = cst[:, C_DIST:C_DIST + P + SEQ]
        eps_norm = par[:, A_EPS:A_EPS + 1]
        eps_subln = par[:, A_EPS + 1:A_EPS + 2]
        zero = par[:, A_EPS + 2:A_EPS + 3]

        c_exp, silu_c = sml[:, 0:16], sml[:, 16:32]
        lam_s, lam_e, neg_lam = sml[:, 32:34], sml[:, 34:36], sml[:, 36:37]
        ssq = sml[:, 37:39]
        rms = sml[:, 39:41]
        junk = sb("junk", [P, DV])
        mx = sb("mx", [P, 4])
        p_sum = sb("p_sum", [P, 4])
        p_rec = sb("p_rec", [P, 4])
        o_ss = sb("o_ss", [P, HG * TT])
        o_rec = sb("o_rec", [P, HG * TT])
        y_ss = sb("y_ss", [P, TT, 4])
        gsub = sml[:, 41:42]
        xrms = sml[:, 42:44]
        yrms = sml[:, 44:46]
        h2rms = sml[:, 46:48]

        s_slot = [sem(f"s_slot{i}") for i in range(RING)]
        s_cst = sem("s_cst")
        s_par = sem("s_par")
        s_x = [sem(f"s_x_in{t}") for t in range(TT)]
        s_ada_used = sem("s_ada_used")
        s_ada_dve = sem("s_ada_dve")
        s_quarter_read = sem("s_quarter_read")
        s_w_used = sem("s_w_used")
        s_dve = sem("s_dve")
        s_act = sem("s_act")
        s_cexp = sem("s_cexp")
        s_silu_c = sem("s_silu_c")
        s_ssq = sem("s_ssq")
        s_rms = sem("s_rms")
        s_xn = sem("s_xn")
        s_xt = sem("s_xt")
        s_xt_read = sem("s_xt_read")
        s_turn = sem("s_turn")
        s_turn_read = sem("s_turn_read")
        s_h = sem("s_h")
        s_h_hi = sem("s_h_hi")
        s_h_lo = sem("s_h_lo")
        s_w_hi = sem("s_w_hi")
        s_w_lo = sem("s_w_lo")
        s_hi_used = sem("s_hi_used")
        s_y_hi = sem("s_y_hi")
        s_y_lo = sem("s_y_lo")
        s_block_act = sem("s_block_act")
        s_block_dve = sem("s_block_dve")
        s_scores = sem("s_scores")
        s_shift = sem("s_shift")
        s_prob = sem("s_prob")
        s_a = sem("s_a")
        s_o_rms = sem("s_o_rms")
        s_o_norm = sem("s_o_norm")
        s_lam_in = sem("s_lam_in")
        s_lam = sem("s_lam")
        s_lam_e = sem("s_lam_e")
        s_cols = sem("s_cols")
        s_wr = sem("s_wr")

        ada_v = w_ada[0].rearrange("(p k) (m q n) -> p k m q n", k=KC, m=6, q=4)
        in_v = w_in[0].rearrange("(h p k) n -> h p k n", h=2, k=KH)
        out_v = w_out[0].rearrange("(c p) n -> p c n", p=P)
        x_v = x[0].rearrange("(t p) d -> t p d", p=P)
        o_v = out[0].rearrange("(t p) d -> t p d", p=P)

        slot_of = {what: n for n, what in enumerate(PLAN)}

        def feature(rows, k):
            h = k // KH
            return rows[:, D // 2 * h + k % KH:D // 2 * (h + 1):KH]

        def landed(eng, what):
            n = slot_of[what]
            eng.wait_ge(s_slot[n % RING1], 16 * (n // RING1 + 1))
            return ring[:, n % RING1, :]

        def unit_weights(v):
            b, part = SUBSTEPS[v // UNITS]
            n = slot_of[("w", b, part // 2)]
            c0 = 1024 * (UNITS * (part % 2) + v % UNITS)
            span = slice(c0, c0 + 1024)
            return ring[:, n % RING1, span], ring_r[n % RING1][:, span], v % HI_BUFS

        turns = []
        for s in range(-1, NB * SUB + 1):
            if s == -1:
                turns += [("col", i, h) for h in range(2) for i in range(2)]
            if s - 3 in SCORE_AT:
                turns.append(("out", SCORE_AT[s - 3]))
            if s - 2 in SCORE_AT:
                turns.append(("head", SCORE_AT[s - 2]))
            if s in FINISH_AT:
                turns += [("fin", FINISH_AT[s], h) for h in range(2)]
            if s in COLUMNS_AT:
                turns += [("col", *ih) for ih in COLUMNS_AT[s]]
            if s in BCAST_AT:
                turns.append(("bc", *BCAST_AT[s]))
        turns += [("bc", 2, 2), ("bc", 2, 3)] + [("bc", 3, j) for j in range(4)]
        turn_no = {what: n for n, what in enumerate(turns)}

        ada_order = [what for what in PLAN if what[0] == "ada" and what[1:3] not in DVE_HALVES]
        dve_order = [what for what in PLAN if what[0] == "ada" and what[1:3] in DVE_HALVES]
        assert all(one[:3] == two[:3] for one, two in zip(ada_order[::2], ada_order[1::2]))

        def used(what):
            for count, order in ((s_w_used, W_SLOTS), (s_ada_used, ada_order), (s_ada_dve, dve_order)):
                if what in order:
                    return count, order.index(what) + 1

        def sums(i, h):
            return rt[:, :] if i == LAST_MOD else acc[:, i % 2, D // 2 * h:D // 2 * (h + 1)]

        def quarters_done(i, h):
            return ada_order.index(("ada", i, h, ADA_UNITS - 1)) // 2 + 1

        act_evac = [b for b in range(NB) if b >= NB_IN or BLOCKS[b][0] not in "XB"]
        dve_evac = [b for b in range(NB) if b not in act_evac]

        h2_rows = y_sb.rearrange("p t (q k) -> p t k q", k=KC)
        item_rows = rt.rearrange("p (k q) -> p k q", q=P)
        picks = soft[:, :, :].rearrange("p a b -> p (a b)")
        xe_turned = region_a[:, 0:2 * KC * CAP].rearrange("p (b k s) -> p b k s", b=2, k=KC)
        y_item = region_a[:, D:2 * D].rearrange("p (b n) -> p b n", b=2)
        silu_g = acc[0:CAP, 0, 0:FE]
        act_rows = acc[0:CAP, 0, FE:2 * FE]
        act_turned = acc[:, 0, 2 * FE:2 * FE + 4 * CAP].rearrange("p (j s) -> p j s", j=4)
        s_idx = sb("s_idx", [P, ITEMS], I32)
        e_idx = sb("e_idx", [P, ITEMS], I32)
        n_extra = sb("n_extra", [P, 1], I32)
        s_cur = sb("s_cur", [P, 2], I32)
        weight = sb("weight", [P, ITEMS])
        f_ss = sb("f_ss", [P, TT])

        def hot_slot(n):
            return acc[:, 0, T_SLOT + P * n:T_SLOT + P * (n + 1)]

        def hot_item(n):
            c0 = T_ITEM + 4 * ITEMS * n
            return acc[:, 0, c0:c0 + 4 * ITEMS].rearrange("p (a b) -> p a b", a=4)

        def pick(b, t):
            c0 = G_PICK + CAP * (TT * b + t)
            return picks[:, c0:c0 + CAP]

        s_h2 = sem("s_h2")
        s_h2t = sem("s_h2t")
        s_h2t_read = sem("s_h2t_read")
        s_logit = sem("s_logit")
        s_gexp_in = sem("s_gexp_in")
        s_gexp = sem("s_gexp")
        s_picks = sem("s_picks")
        s_rank = sem("s_rank")
        s_rank_used = sem("s_rank_used")
        s_extra = sem("s_extra")
        s_base = sem("s_base")
        s_hot = sem("s_hot")
        s_table = sem("s_table")
        s_tables = sem("s_tables")
        s_y_gated = sem("s_y_gated")
        s_logit_act = sem("s_logit_act")
        s_logit_dve = sem("s_logit_dve")
        s_logit_sum = sem("s_logit_sum")
        s_x1 = sem("s_x1")
        s_x1a = sem("s_x1a")
        s_xsq = sem("s_xsq")
        s_h2rms = sem("s_h2rms")
        s_ysum = sem("s_ysum")
        s_yrms = sem("s_yrms")

        s_one_slot = sem("s_one_slot")
        s_half_pick = sem("s_half_pick")
        s_pick = sem("s_pick")
        s_rows_psum = sem("s_rows_psum")
        s_rows_act = sem("s_rows_act")
        s_rows_dve = sem("s_rows_dve")
        s_xe_psum = sem("s_xe_psum")
        s_xe_act = sem("s_xe_act")
        s_xe_dve = sem("s_xe_dve")
        s_silu_g = sem("s_silu_g")
        s_act_rows = sem("s_act_rows")
        s_at_psum = sem("s_at_psum")
        s_at = sem("s_at")
        s_y_act = sem("s_y_act")
        s_y_dve = sem("s_y_dve")
        s_s_cur = sem("s_s_cur")
        s_y_free = sem("s_y_free")
        s_scatter = [sem(f"s_scatter{b}") for b in range(2)]
        s_pool_turn = sem("s_pool_turn")
        s_pe_turn = sem("s_pe_turn")

        s_pair = [sem(f"s_pair{n}") for n in range(2 * TT)]
        s_fsum = sem("s_fsum")
        s_gated = sem("s_gated")
        s_fsq = sem("s_fsq")
        s_frms = sem("s_frms")
        s_fin = sem("s_fin")
        s_store = sem("s_store")

        x_scatter = sem("x_scatter")
        x_load = [sem(f"x_load{r}") for r in range(6)]
        x_done = sem("x_done")
        x_scur = sem("x_scur")
        x_half_pick = sem("x_half_pick")
        x_pick = sem("x_pick")
        x_rows_psum = sem("x_rows_psum")
        x_rows_act = sem("x_rows_act")
        x_rows_dve = sem("x_rows_dve")
        x_xe = sem("x_xe")
        x_xe_act = sem("x_xe_act")
        x_xe_dve = sem("x_xe_dve")
        x_gu = sem("x_gu")
        x_silu = sem("x_silu")
        x_rows_done = sem("x_rows_done")
        x_at = sem("x_at")
        x_atc = sem("x_atc")
        x_dn = sem("x_dn")
        x_ya = sem("x_ya")
        x_yd = sem("x_yd")

        gate_v = w_gate[0].rearrange("e (p k) f -> e p (k f)", k=KC)
        up_v = w_up[0].rearrange("e (p k) f -> e p (k f)", k=KC)
        down_v = w_down[0].rearrange("e (p j) n -> e p (j n)", j=4)
        PARTS = [(gate_v, 0), (up_v, 0), (gate_v, 1), (up_v, 1), (down_v, 0), (down_v, 1)]
        N_IT = NE // UNROLL

        block = ctx.enter_context(nc.Block())

        @block.sync
        def _(sp):
            sp.dma_start(par[:, :], small).then_inc(s_par, 16)
            sp.dma_start(rt[:, 0:4 * DK], lam).then_inc(s_lam_in, 16)
            for n, what in enumerate(PLAN):
                if n >= RING1:
                    sp.wait_ge(*used(PLAN[n - RING1]))
                dst = ring[:, n % RING1, :]
                if what[0] == "ada":
                    k0 = 8 * (what[3] % 2)
                    src = ada_v[:, k0:k0 + 8, MODS[what[1]], 2 * what[2] + what[3] // 2, :]
                else:
                    b, half = what[1], what[2]
                    if b < NB_IN:
                        kind, g = BLOCKS[b]
                        c0 = COL0[kind] + 512 * g
                        src = in_v[half, :, :, c0:c0 + 512]
                    else:
                        c0 = 512 * (b - NB_IN)
                        src = out_v[:, 8 * half:8 * half + 8, c0:c0 + 512]
                dst = dst.rearrange("p (k n) -> p k n", k=8)
                sp.dma_start(dst, src).then_inc(s_slot[n % RING1], 16)
                if n == 0:
                    for t in range(TT):
                        sp.dma_start(x_rows[:, t, :], x_v[t]).then_inc(s_x[t], 16)
                    sp.dma_start(cst[:, :], consts).then_inc(s_cst, 16)
            with sp.Fori(0, N_IT) as it:
                for u in range(UNROLL):
                    for r, (view, half) in enumerate(PARTS):
                        n = 6 * u + r
                        slot = EXPERT_SLOTS[n % RING]
                        sp.wait_ge(s_w_used, W_USED0 - RING + 1 + it * (6 * UNROLL) + n)
                        src = view[bass.ds(it * UNROLL + u, 1), :, SLOT * half:SLOT * (half + 1)]
                        sp.dma_start(ring[:, slot, :], src.rearrange("a p f -> (a p) f")).then_inc(s_slot[slot], 16)
            sp.wait_ge(s_tables, 1)
            nx = sp.value_load(n_extra[0:1, 0:1], min_val=0, max_val=MAX_EXTRA)
            sp.wait_ge(s_w_used, W_USED0 + 6 * NE)
            with sp.If(nx > 0):
                with sp.Fori(0, nx) as j:
                    sp.wait_ge(x_done, j + 1)
                    e = sp.value_load(e_idx[0:1, bass.ds(j + NE, 1)], min_val=0, max_val=NE - 1)
                    for r, (view, half) in enumerate(PARTS):
                        src = view[bass.ds(e, 1), :, SLOT * half:SLOT * (half + 1)]
                        sp.dma_start(ring[:, r, :], src.rearrange("a p f -> (a p) f")).then_inc(x_load[r], 16)
            sp.wait_ge(s_scatter[0], 16 * NE // 2)
            sp.wait_ge(s_scatter[1], 16 * NE // 2)
            sp.wait_ge(x_done, nx + 1)
            yv = y_rows.rearrange("(k t p c) n -> t c p k n", k=2, t=TT, p=P)
            for t in range(TT):
                dst = ring[:, t, :].rearrange("p (k c n) -> p k c n", k=2, c=2)
                for c in range(2):
                    sp.dma_start(dst[:, :, c, :], yv[t, c]).then_inc(s_pair[2 * t + c], 16)
            for n in range(2 * TT):
                t, span = n // 2, slice(D // 2 * (n % 2), D // 2 * (n % 2 + 1))
                sp.wait_ge(s_fin, n + 1)
                sp.dma_start(o_v[t][:, span], x1[:, t, span]).then_inc(s_store, 16)
            sp.wait_ge(s_store, 16 * 2 * TT)

        @block.gpsimd
        def _(pool):
            def scatter_go(b, done):
                pool.indirect_dma_start(y_rows, bass.IndirectOffsetOnAxis(ap=s_cur[0:PAIR, b:b + 1], axis=0),
                                        y_item[0:PAIR, b, :], None,
                                        bounds_check=4 * SEQ - 1, oob_is_err=False).then_inc(done, 16)

            pool.wait_ge(s_tables, 1)
            pool.sem_inc(s_y_free, 2)
            pool.sem_inc(x_done, 1)
            with pool.Fori(0, N_IT) as it:
                for u in range(UNROLL):
                    b = u % 2
                    i = it * UNROLL + u
                    pool.wait_ge(s_y_act, i + 2)
                    pool.sem_inc(s_pool_turn, 1)
                    pool.wait_ge(s_y_dve, i + 2)
                    pool.sem_inc(s_pool_turn, 1)
                    pool.tensor_copy(s_cur[:, b:b + 1], s_idx[:, bass.ds(i, 1)]).then_inc(s_s_cur, 1)
                    pool.wait_ge(s_s_cur, i + 1)
                    pool.sem_inc(s_pool_turn, 1)
                    scatter_go(b, s_scatter[b])
                    pool.wait_ge(s_scatter[b], it * 32 + 16 * (u // 2 + 1))
                    pool.sem_inc(s_y_free, 1)
            for b in range(2):
                pool.wait_ge(s_scatter[b], 16 * (NE // 2))
            nx = pool.value_load(n_extra[0:1, 0:1], min_val=0, max_val=MAX_EXTRA)
            with pool.If(nx > 0):
                with pool.Fori(0, nx) as j:
                    pool.tensor_copy(s_cur[:, 0:1], s_idx[:, bass.ds(j + NE, 1)]).then_inc(x_scur, 1)
                    pool.wait_ge(x_scur, j + 1)
                    pool.sem_inc(s_pool_turn, 1)
                    pool.wait_ge(x_ya, j + 1)
                    pool.sem_inc(s_pool_turn, 1)
                    pool.wait_ge(x_yd, j + 1)
                    pool.sem_inc(s_pool_turn, 1)
                    scatter_go(0, x_scatter)
                    pool.wait_ge(x_scatter, j * 16 + 16)
                    pool.sem_inc(x_done, 1)

        @block.tensor
        def _(pe):
            def take_turn(what):
                n = turn_no[what]
                if n >= 1:
                    pe.wait_ge(s_turn_read, n)

            def columns(i, h):
                take_turn(("col", i, h))
                if (i, h) in DVE_HALVES:
                    pe.wait_ge(s_ada_dve, dve_order.index(("ada", i, h, ADA_UNITS - 1)) + 1)
                    summed = ones[:, 0:1]
                else:
                    pe.wait_ge(s_quarter_read, quarters_done(i, h))
                    summed = cst[:, C_TILE:C_TILE + 1]
                c0 = A_BADA + KC * MODS[i] + KH * h
                pe.matmul(bank[6][:, 0:KH], ident, par[:, c0:c0 + KH],
                          start=True, stop=False, skip_group_check=True)
                for k in range(KH):
                    mm = pe.matmul(bank[6][:, k:k + 1], sums(i, h)[:, k::KH], summed,
                                   start=False, stop=(k == KH - 1), skip_group_check=True)
                mm.then_inc(s_turn, 1)

            def ada(what):
                n = ada_order.index(what)
                if n % 2 == 0 and n >= 2:
                    pe.wait_ge(s_quarter_read, n // 2)
                w = landed(pe, what).rearrange("p (k n) -> p k n", k=8)
                for k in range(8):
                    tile = slice(COL_TILE * (k % 4), COL_TILE * (k % 4 + 1))
                    row = 8 * (n % 2) + k
                    mm = pe.matmul(bank[7][tile, :], silu_c[:, row:row + 1].to_broadcast([P, COL_TILE]), w[:, k, :],
                                   start=(row < 4), stop=(row >= KC - 4))
                mm.then_inc(used(what)[0], 1)

            def head_scores(h):
                hh = h % HG
                if hh == 0:
                    pe.wait_ge(s_block_act, 2 * (act_evac.index(3 + 5 * (h // HG) - 1) + 1))
                if h >= 1:
                    pe.wait_ge(s_shift, h)
                for m in range(2):
                    rows = slice(DK * m, DK * m + DK)
                    pe.matmul(bank[4 + m][:, 0:P], q_turned[rows, hh, 0:P], k_turned[rows, hh, 0:P],
                              start=True, stop=True)
                    mm = pe.matmul(bank[4 + m][:, P:P + SEQ], q_turned[rows, hh, P:SEQ], k_turned[rows, hh, :],
                                   start=True, stop=True)
                mm.then_inc(s_scores, 1)

            def head_turn(h):
                take_turn(("head", h))
                pe.wait_ge(s_a, h + 1)
                for j in range(3):
                    mm = pe.transpose(bank[6][:, j * P:(j + 1) * P], soft[:, 0, j * P:(j + 1) * P], ident)
                mm.then_inc(s_turn, 1)

            def head_out(h):
                hh = h % HG
                take_turn(("out", h))
                vh = slice(DV * hh, DV * hh + DV)
                pe.matmul(bank[6][:, 0:DV], a_turned[:, 0:P], v_rows[:, 0, vh], start=True, stop=True)
                pe.matmul(bank[6][:, DV:2 * DV], a_turned[:, P:2 * P], v_rows[:, 0, vh], start=True, stop=False)
                mm = pe.matmul(bank[6][:, DV:2 * DV], a_turned[:, 2 * P:3 * P], v_rows[:, 1, vh],
                               start=False, stop=True)
                mm.then_inc(s_turn, 1)

            def finish(g):
                pe.wait_ge(s_o_norm, g + 1)
                for half in range(2):
                    take_turn(("fin", g, half))
                    for j in range(2):
                        for t in range(TT):
                            mm = pe.transpose(bank[6][:, (2 * j + t) * P:(2 * j + t + 1) * P],
                                              o_raw[:, 2 * half + j, t, :], ident)
                    mm.then_inc(s_turn, 1)

            def broadcast(which, j):
                col = mods[:, SH2, :] if which == 2 else cols[:, (1, 2, None, 3)[which], :]
                take_turn(("bc", which, j))
                for k in range(4):
                    mm = pe.matmul(bank[6][:, k * P:(k + 1) * P],
                                   col[:, 4 * j + k:4 * j + k + 1].to_broadcast([P, P]), ident,
                                   start=True, stop=True)
                mm.then_inc(s_turn, 1)

            pe.wait_ge(s_silu_c, 1)
            for what in EARLY[:3]:
                ada(what)
            pe.wait_ge(s_cst, 16)
            pe.wait_ge(s_par, 16)
            pe.wait_ge(s_xn, TT)
            for n in range(KC // 2):
                if n >= 4:
                    pe.wait_ge(s_xt_read, n - 3)
                for j in range(2):
                    for t in range(TT):
                        mm = pe.transpose(bank[n % 4][:, (2 * j + t) * P:(2 * j + t + 1) * P],
                                          feature(x_rows[:, t, :], 2 * n + j), ident)
                mm.then_inc(s_xt, 1)
            for what in EARLY[3:4]:
                ada(what)
            columns(0, 0)
            for what in EARLY[4:8]:
                ada(what)
            columns(1, 0)
            for s, (b, part) in enumerate(SUBSTEPS):
                if s == 4:
                    columns(0, 1)
                if s == AHEAD:
                    columns(1, 1)
                if s - 3 in SCORE_AT:
                    head_out(SCORE_AT[s - 3])
                if s - 2 in SCORE_AT:
                    head_turn(SCORE_AT[s - 2])
                if s in SCORE_AT:
                    head_scores(SCORE_AT[s])
                if s in FINISH_AT:
                    finish(FINISH_AT[s])
                if s in COLUMNS_AT:
                    for i, h in COLUMNS_AT[s]:
                        columns(i, h)
                if s in BCAST_AT:
                    pe.wait_ge(s_cols, 2 + min(BCAST_AT[s][0], 1))
                    broadcast(*BCAST_AT[s])
                if part == 0:
                    if b < 3:
                        pe.wait_ge(s_xt_read, KC // 2)
                    elif b - 2 >= NB_IN:
                        pe.wait_ge(s_y_gated, 2 * (b - 1 - NB_IN))
                    elif b - 2 in act_evac:
                        pe.wait_ge(s_block_act, 2 * (act_evac.index(b - 2) + 1))
                    else:
                        pe.wait_ge(s_block_dve, 2 * (dve_evac.index(b - 2) + 1))
                if b == 0:
                    pe.wait_ge(s_h_lo, part + 1)
                if b == NB_IN:
                    pe.wait_ge(s_y_lo, part + 1)
                lo, hi = (bank[n] for n in BANKS[b])
                rows = b >= NB_IN or BLOCKS[b][0] == "v"
                src_hi, src_lo = (y_hi, y_lo) if b >= NB_IN else (h_hi, h_lo)
                for v in range(UNITS * s, UNITS * s + UNITS):
                    _, w_lo, buf = unit_weights(v)
                    for n_pass, src in enumerate((src_hi, src_lo, src_hi)):
                        if n_pass == 0:
                            pe.wait_ge(s_w_hi, v + 1)
                        if n_pass == 2:
                            pe.wait_ge(s_w_lo, v + 1)
                        w = w_hi[:, buf, :] if n_pass < 2 else w_lo
                        for kk in range(2):
                            k = 4 * part + 2 * (v % UNITS) + kk
                            wk = w[:, 512 * kk:512 * kk + 512]
                            first = k == 0 and n_pass == 0
                            last = k == KC - 1 and n_pass == 2
                            if rows:
                                for t in range(TT):
                                    mm = pe.matmul((lo, hi)[t][:, :], src[:, k, t * P:(t + 1) * P], wk,
                                                   start=first, stop=last)
                            else:
                                for c in range(HG):
                                    mm = pe.matmul((lo, hi)[c // 2][:, SEQ * (c % 2):SEQ * (c % 2) + SEQ],
                                                   wk[:, P * c:P * c + P], src[:, k, :],
                                                   start=(first and c % 2 == 0), stop=last, skip_group_check=True)
                        if n_pass == 1:
                            mm.then_inc(s_hi_used, 1)
                if part % 2 == 1:
                    mm.then_inc(s_w_used, 1 + (SPARE if s == len(SUBSTEPS) - 1 else 0))
                for what in ADA_AT.get(s, []):
                    if what in ada_order:
                        ada(what)
            for j in range(2, 4):
                broadcast(2, j)
            h2_turned = y_turned
            for t in range(TT):
                pe.wait_ge(s_h2, t + 1)
                for j in range(4):
                    n = 4 * t + j
                    if n < 4:
                        pe.wait_ge(s_y_gated, 2 * (NB - NB_IN))
                    else:
                        pe.wait_ge(s_h2t_read, n - 3)
                    for k in range(4):
                        mm = pe.transpose(bank[n % 4][:, k * P:(k + 1) * P], y_sb[:, t, 4 * j + k::KC], ident)
                    mm.then_inc(s_h2t, 1)
            pe.wait_ge(s_wr, 16)
            pe.wait_ge(s_h2t_read, 4 * TT)
            for k in range(KC):
                c0 = UPPER * (k % 2)
                mm = pe.matmul(bank[4 + k % 2][c0:c0 + N_LOGITS, 0:SEQ], wr_sb[:, k, :], h2_turned[:, k, :],
                               start=(k < 2), stop=(k >= KC - 2))
            mm.then_inc(s_logit, 1)
            pe.wait_ge(s_logit_act, 1)
            pe.wait_ge(s_logit_dve, 1)
            for t in range(TT):
                for c0 in (0, UPPER):
                    mm = pe.matmul(bank[7][:, N_LOGITS * t:N_LOGITS * (t + 1)],
                                   a_turned[:, P * t:P * (t + 1)], ident[:, c0:c0 + N_LOGITS], start=(c0 == 0), stop=(c0 > 0))
            mm.then_inc(s_logit_sum, 1)
            pe.wait_ge(s_picks, 1)
            pe.wait_ge(s_turn_read, turn_no[("bc", 2, 3)] + 1)
            both = rt[:, R_BOTH:R_BOTH + TT * NE].rearrange("p (t e) -> p t e", t=TT)
            pe.matmul(bank[6][:, 0:NE], tri, both[:, 0, :], start=True, stop=True)
            pe.matmul(bank[6][:, NE:2 * NE], tri, both[:, 1, :], start=True, stop=False)
            mm = pe.matmul(bank[6][:, NE:2 * NE], ones, both[:, 0, :], start=False, stop=True)
            for t in range(TT):
                mm = pe.matmul(bank[7][0:NE, 0:1], both[:, t, :], ones[:, 0:1], start=(t == 0), stop=(t == TT - 1))
            mm.then_inc(s_rank, 1)
            pe.wait_ge(s_extra, 1)
            extra = rt[0:NE, R_EXTRA:R_EXTRA + 1]
            pe.matmul(bank[7][:, 0:NE], extra.to_broadcast([NE, P]), tri[0:NE, 0:NE], start=True, stop=True)
            pe.matmul(bank[7][:, NE:NE + 1], extra.to_broadcast([NE, P]), ones[0:NE, 0:1],
                      start=True, stop=True).then_inc(s_base, 1)
            pe.wait_ge(s_cols, 4)
            pe.wait_ge(s_rank_used, 2)
            for j in range(2):
                broadcast(3, j)
            def pick_rows(b):
                for n, pb in enumerate((bank[1], bank[7])):
                    for t in range(TT):
                        for half in range(2):
                            k0 = 8 * half + 4 * n
                            mm = pe.matmul(pb[UPPER * half:UPPER * half + CAP, :], pick(b, t),
                                           h2_rows[:, t, k0:k0 + 4, :], start=(t == 0), stop=(t == TT - 1))
                return mm

            def turn_rows():
                for k in range(8):
                    for half in range(2):
                        p0 = UPPER * half
                        mm = pe.transpose(bank[2 + half][:, CAP * k:CAP * (k + 1)],
                                          item_rows[p0:p0 + CAP, k, :], ident[p0:p0 + CAP, p0:p0 + CAP])
                return mm

            def gate_up(b, w, done):
                for k in range(KC):
                    if k % 8 == 0:
                        wg, wu = w(2 * (k // 8)), w(2 * (k // 8) + 1)
                    xk = xe_turned[:, b, k, :]
                    g = pe.matmul(bank[0][UPPER:UPPER + CAP, :], xk, wg[:, FE * (k % 8):FE * (k % 8 + 1)],
                                  start=(k == 0), stop=(k == KC - 1))
                    mm = pe.matmul(bank[0][0:CAP, :], xk, wu[:, FE * (k % 8):FE * (k % 8 + 1)],
                                   start=(k == 0), stop=(k == KC - 1))
                    if k % 8 == 7 and done is not None:
                        g.then_inc(done, 1)
                        mm.then_inc(done, 1)
                return mm

            def turn_act():
                for j in range(4):
                    mm = pe.transpose(bank[4][:, CAP * j:CAP * j + CAP], act_rows[:, j::4], ident[0:CAP, 0:CAP])
                return mm

            def down(w, done):
                for j in range(4):
                    if j % 2 == 0:
                        wd = w(4 + j // 2)
                    for n in range(2):
                        for half in range(2):
                            c0 = D * (j % 2) + 1024 * half + 512 * n
                            mm = pe.matmul(bank[5 + n][UPPER * half:UPPER * half + CAP, :], act_turned[:, j, :],
                                           wd[:, c0:c0 + 512], start=(j == 0), stop=(j == 3))
                    if j % 2 == 1 and done is not None:
                        mm.then_inc(done, 1)
                return mm

            pe.wait_ge(s_pick, 1)
            pick_rows(0).then_inc(s_rows_psum, 1)
            pe.wait_ge(s_rows_act, 1)
            pe.wait_ge(s_rows_dve, 1)
            turn_rows().then_inc(s_xe_psum, 1)
            pe.wait_ge(s_hot, 1)
            pe.wait_ge(s_turn_read, turn_no[("bc", 3, 1)] + 1)
            for n in range(2 * TT):
                mm = pe.matmul(bank[6][:, 0:4 * ITEMS], hot_slot(n), hot_item(n).rearrange("p a b -> p (a b)"),
                               start=(n == 0), stop=(n == 2 * TT - 1))
            mm.then_inc(s_table, 1)
            with pe.Fori(0, N_IT) as it:
                for u in range(UNROLL):
                    i = it * UNROLL + u
                    b = u % 2

                    def weights(r):
                        n = 6 * u + r
                        slot = EXPERT_SLOTS[n % RING]
                        pe.wait_ge(s_slot[slot], it * (16 * 6 * UNROLL // RING) + 16 * (USES0[slot] + n // RING + 1))
                        return ring[:, slot, :]

                    pe.wait_ge(s_xe_act, i + 1)
                    pe.wait_ge(s_xe_dve, i + 1)
                    gate_up(b, weights, s_w_used)
                    pe.wait_ge(s_pick, i + 2)
                    pe.sem_inc(s_pe_turn, 1)
                    pick_rows(1 - b).then_inc(s_rows_psum, 1)
                    pe.wait_ge(s_act_rows, i + 1)
                    pe.sem_inc(s_pe_turn, 1)
                    turn_act().then_inc(s_at_psum, 1)
                    pe.wait_ge(s_rows_act, i + 2)
                    pe.sem_inc(s_pe_turn, 1)
                    pe.wait_ge(s_rows_dve, i + 2)
                    pe.sem_inc(s_pe_turn, 1)
                    turn_rows().then_inc(s_xe_psum, 1)
                    pe.wait_ge(s_at, i + 1)
                    pe.wait_ge(s_y_act, i + 1)
                    pe.wait_ge(s_y_dve, i + 1)
                    down(weights, s_w_used)
            nx = pe.value_load(n_extra[0:1, 0:1], min_val=0, max_val=MAX_EXTRA)
            pe.wait_ge(s_xe_act, NE + 1)
            pe.wait_ge(s_xe_dve, NE + 1)
            pe.wait_ge(s_y_act, NE + 1)
            pe.wait_ge(s_y_dve, NE + 1)
            for j in range(2, 4):
                broadcast(3, j)
            pe.wait_ge(s_turn_read, turn_no[("bc", 3, 3)] + 1)
            with pe.If(nx > 0):
                with pe.Fori(0, nx) as j:
                    def weights_x(r):
                        pe.wait_ge(x_load[r], j * 16 + 16)
                        return ring[:, r, :]

                    pe.wait_ge(x_pick, j + 1)
                    pe.sem_inc(s_pe_turn, 1)
                    pick_rows(0).then_inc(x_rows_psum, 1)
                    pe.wait_ge(x_rows_act, j + 1)
                    pe.sem_inc(s_pe_turn, 1)
                    pe.wait_ge(x_rows_dve, j + 1)
                    pe.sem_inc(s_pe_turn, 1)
                    turn_rows().then_inc(x_xe, 1)
                    pe.wait_ge(x_xe_act, j + 1)
                    pe.wait_ge(x_xe_dve, j + 1)
                    gate_up(0, weights_x, None).then_inc(x_gu, 1)
                    pe.wait_ge(x_rows_done, j + 1)
                    pe.sem_inc(s_pe_turn, 1)
                    turn_act().then_inc(x_at, 1)
                    pe.wait_ge(x_atc, j + 1)
                    down(weights_x, None).then_inc(x_dn, 1)

        @block.scalar
        def _(act):
            count = [0]

            def link(ins):
                count[0] += 1
                ins.then_inc(s_act, 1)
                act.wait_ge(s_act, count[0])

            act.wait_ge(s_par, 16)
            act.activation(c_exp, par[:, A_C:A_C + KC], ACT.Exp, bias=zero, scale=-1.0).then_inc(s_cexp, 1)
            act.wait_ge(s_lam, 1)
            act.activation(lam_e, lam_s, ACT.Exp, bias=zero).then_inc(s_lam_e, 1)
            for t in range(TT):
                act.wait_ge(s_x[t], 16)
                act.activation(y_sb[:, t, :], x_rows[:, t, :], ACT.Square, bias=zero,
                               accum_out=ssq[:, t:t + 1]).then_inc(s_ssq, 1)
            act.wait_ge(s_ssq, TT)
            act.activation(rms, ssq, ACT.Sqrt, bias=eps_norm, scale=1.0 / D).then_inc(s_rms, 1)

            def take_quarter(what):
                if what not in ada_order or ada_order.index(what) % 2 == 0:
                    return
                n = ada_order.index(what)
                i, h, q = what[1], what[2], what[3] // 2
                act.wait_ge(*used(what))
                if i == LAST_MOD:
                    act.wait_ge(s_turn, turn_no[("col", i, 0) if h == 1 else ("fin", 1, 1)] + 1)
                elif i >= 2:
                    act.wait_ge(s_turn, turn_no[("col", i - 2, 1)] + 1)
                act.activation(sums(i, h)[:, QUARTER * q:QUARTER * (q + 1)], bank[7][:, :],
                               ACT.Copy).then_inc(s_quarter_read, 1)

            for what in EARLY[:3]:
                take_quarter(what)
            for n in range(KC // 2):
                act.wait_ge(s_xt, n + 1)
                act.activation(h_turned[:, 2 * n:2 * n + 2, :],
                               bank[n % 4][:, :].rearrange("p (j s) -> p j s", j=2),
                               ACT.Copy).then_inc(s_xt_read, 1)

            def read_turn(what, dst, src, scale=1.0):
                act.wait_ge(s_turn, turn_no[what] + 1)
                act.activation(dst, src, ACT.Copy, scale=scale).then_inc(s_turn_read, 1)

            def columns(i, h):
                read_turn(("col", i, h), mods[:, MODS[i], KH * h:KH * h + KH], bank[6][:, 0:KH])

            def broadcast(which, j):
                v = acc[:, which % 2, :].rearrange("p (h n k) -> p h k n", h=2, k=KH)
                if which == 2:
                    act.wait_ge(s_y_gated, 4 if j < 2 else 8)
                read_turn(("bc", which, j), v[:, j // 2, 4 * (j % 2):4 * (j % 2) + 4, :],
                          bank[6][:, :].rearrange("p (k n) -> p k n", k=4))

            def take_block(b):
                if b not in act_evac:
                    return
                act.wait_ge(s_w_used, BLOCK_USED[b])
                banks = [bank[n] for n in BANKS[b]]
                kind, g = BLOCKS[b] if b < NB_IN else ("y", b - NB_IN)
                for n, pb in enumerate(banks):
                    two = pb[:, :].rearrange("p (c s) -> p c s", c=2)
                    if kind == "q":
                        act.activation(q_turned[:, 2 * n:2 * n + 2, :], two, ACT.Copy,
                                       scale=DK ** -0.5).then_inc(s_block_act, 1)
                    elif kind == "k":
                        act.activation(k_turned[:, 2 * n:2 * n + 2, :], two, ACT.Copy).then_inc(s_block_act, 1)
                    elif kind == "C":
                        c0 = HEADS + HG * g + 2 * n
                        act.activation(y_turned[:, c0:c0 + 2, :], two, ACT.Copy).then_inc(s_block_act, 1)
                    elif kind == "v":
                        act.activation(v_rows[:, n, :], pb[:, :], ACT.Copy).then_inc(s_block_act, 1)
                    else:
                        act.activation(bank[5][:, :], pb[:, :], ACT.Square, bias=zero,
                                       accum_out=y_ss[:, n, g:g + 1]).then_inc(s_block_act, 1)
                        act.wait_ge(s_block_act, 2 * act_evac.index(b) + n + 1)

            def split_h(j):
                act.wait_ge(s_h, j + 1)
                act.activation(h_hi[:, 4 * j:4 * j + 4, :], lo_f32[:, 4 * j:4 * j + 4, :],
                               ACT.Copy).then_inc(s_h_hi, 1)

            def split_w(s):
                for v in range(UNITS * s, UNITS * s + UNITS):
                    b, part = SUBSTEPS[s]
                    landed(act, ("w", b, part // 2))
                    w_f32, _, buf = unit_weights(v)
                    if v >= HI_BUFS:
                        act.wait_ge(s_hi_used, v - HI_BUFS + 1)
                        act.wait_ge(s_w_lo, v - HI_BUFS + 1)
                    act.activation(w_hi[:, buf, :], w_f32, ACT.Copy).then_inc(s_w_hi, 1)

            def exps(h):
                act.wait_ge(s_shift, h + 1)
                for m in range(2):
                    for t in range(TT):
                        span = slice(0, P) if t == 0 else slice(P, P + SEQ)
                        n = 2 * m + t
                        ins = act.activation(soft[:, m, span], soft[:, m, span], ACT.Exp,
                                             bias=mx[:, n:n + 1], accum_out=p_sum[:, n:n + 1])
                ins.then_inc(s_prob, 1)

            take_quarter(EARLY[3])
            columns(0, 0)
            for what in EARLY[4:8]:
                take_quarter(what)
            columns(1, 0)
            for j in range(2):
                split_h(j)
            for s in range(AHEAD):
                split_w(s)
                for what in ADA_AT.get(s - 2, []):
                    take_quarter(what)
                if s == 5:
                    columns(0, 1)
            for what in ADA_AT[AHEAD - 1]:
                take_quarter(what)
            columns(1, 1)
            for j in range(2, 4):
                split_h(j)
            for s, (b, part) in enumerate(SUBSTEPS):
                if AHEAD <= s + 1 < len(SUBSTEPS):
                    split_w(s + 1)
                if s > AHEAD:
                    for what in ADA_AT.get(s - 1, []):
                        take_quarter(what)
                if s >= 1 and SUBSTEPS[s - 1][1] == SUB - 1:
                    take_block(SUBSTEPS[s - 1][0])
                if s == NB_IN * SUB:
                    act.wait_ge(s_w_used, BLOCK_USED[NB_IN - 1])
                    act.wait_ge(s_turn_read, turn_no[("fin", 1, 1)] + 1)
                    for j in range(4):
                        if j == 2:
                            act.wait_ge(s_block_dve, 2 * len(dve_evac))
                        act.activation(y_hi[:, 4 * j:4 * j + 4, :], y_turned[:, 4 * j:4 * j + 4, :],
                                       ACT.Copy).then_inc(s_y_hi, 1)
                if s - 3 in SCORE_AT:
                    h = SCORE_AT[s - 3]
                    act.wait_ge(s_turn, turn_no[("out", h)] + 1)
                    if h == HG:
                        act.wait_ge(s_turn, turn_no[("fin", 0, 1)] + 1)
                    act.activation(o_raw[:, h % HG, :, :], bank[6][:, 0:2 * DV].rearrange("p (t n) -> p t n", t=TT),
                                   ACT.Copy).then_inc(s_act, 1)
                    count[0] += 1
                    if h >= 1:
                        act.wait_ge(s_turn_read, turn_no[("out", h - 1)] + 1)
                    for t in range(TT):
                        n = TT * (h % HG) + t
                        ins = act.activation(junk[:, 0:DV], bank[6][:, DV * t:DV * t + DV], ACT.Square, bias=zero,
                                             accum_out=o_ss[:, n:n + 1])
                        if t == 0:
                            link(ins)
                    ins.then_inc(s_turn_read, 1)
                    if h % HG == HG - 1:
                        act.wait_ge(s_turn_read, turn_no[("out", h)] + 1)
                        act.activation(o_ss[:, :], o_ss[:, :], ACT.Sqrt, bias=eps_subln,
                                       scale=1.0 / DV).then_inc(s_o_rms, 1)
                if s - 2 in SCORE_AT:
                    h = SCORE_AT[s - 2]
                    if h >= 1:
                        act.wait_ge(s_turn, turn_no[("out", h - 1)] + 1)
                    read_turn(("head", h), a_turned[:, :], bank[6][:, 0:P + SEQ])
                if s in FINISH_AT:
                    g = FINISH_AT[s]
                    for half in range(2):
                        c0 = HG * g + 2 * half
                        read_turn(("fin", g, half), y_turned[:, c0:c0 + 2, :],
                                  bank[6][:, :].rearrange("p (c s) -> p c s", c=2), scale=gsub)
                if s in COLUMNS_AT:
                    for i, h in COLUMNS_AT[s]:
                        columns(i, h)
                if s == NB_IN * SUB + 1:
                    act.wait_ge(s_w_used, BLOCK_USED[NB_IN - 1])
                    for t in range(TT):
                        act.dma_start(x1[:, t, :], x_v[t]).then_inc(s_x[t], 16)
                    act.wait_ge(s_turn, turn_no[("head", HEADS - 1)] + 1)
                    act.dma_start(wr_sb, wrt.rearrange("(p k) n -> p k n", k=KC)).then_inc(s_wr, 16)
                if s in BCAST_AT:
                    broadcast(*BCAST_AT[s])
                if s in SCORE_AT:
                    exps(SCORE_AT[s])
            take_block(NB - 1)
            act.wait_ge(s_ysum, 1)
            act.activation(yrms, yrms, ACT.Sqrt, bias=eps_norm, scale=1.0 / D).then_inc(s_yrms, 1)
            for j in range(2, 4):
                broadcast(2, j)
            for t in range(TT):
                act.wait_ge(s_x1, t + 1)
                act.activation(x_rows[:, t, :], x1[:, t, :], ACT.Square, bias=zero,
                               accum_out=h2rms[:, t:t + 1]).then_inc(s_xsq, 1)
                act.wait_ge(s_xsq, t + 1)
                act.activation(h2rms[:, t:t + 1], h2rms[:, t:t + 1], ACT.Sqrt, bias=eps_norm,
                               scale=1.0 / D).then_inc(s_h2rms, 1)
            for t in range(TT):
                for j in range(4):
                    act.wait_ge(s_h2t, 4 * t + j + 1)
                    act.activation(y_turned[:, 4 * j:4 * j + 4, t * P:(t + 1) * P],
                                   bank[(4 * t + j) % 4][:, :].rearrange("p (k s) -> p k s", k=4),
                                   ACT.Copy).then_inc(s_h2t_read, 1)
            act.wait_ge(s_logit, 1)
            act.activation(a_turned[UPPER:UPPER + N_LOGITS, 0:SEQ], bank[5][UPPER:UPPER + N_LOGITS, 0:SEQ],
                           ACT.Copy).then_inc(s_logit_act, 1)
            act.wait_ge(s_gexp_in, 1)
            act.activation(rt[:, R_EXP:R_EXP + TT * 5], rt[:, R_EXP:R_EXP + TT * 5], ACT.Exp,
                           bias=zero).then_inc(s_gexp, 1)

            for j in range(2):
                broadcast(3, j)

            def xe_copy(b):
                return act.activation(xe_turned[:, b, 0:8, :], bank[2][:, 0:8 * CAP].rearrange("p (k s) -> p k s", k=8),
                                      ACT.Copy)

            def rows_copy():
                return act.activation(rt[:, 0:512], bank[1][:, :], ACT.Copy)

            def silu():
                return act.activation(silu_g, bank[0][UPPER:UPPER + CAP, :], ACT.Silu, bias=zero[0:CAP, :])

            def turned_copy():
                return act.activation(act_turned, bank[4][:, 0:4 * CAP].rearrange("p (j s) -> p j s", j=4), ACT.Copy)

            def y_copy(b):
                return act.activation(y_item[:, b, 0:512], bank[5][:, :], ACT.Copy)

            act.wait_ge(s_rows_psum, 1)
            act.wait_ge(s_hot, 1)
            rows_copy().then_inc(s_rows_act, 1)
            act.wait_ge(s_xe_psum, 1)
            xe_copy(0).then_inc(s_xe_act, 1)
            act.sem_inc(s_y_act, 1)
            with act.Fori(0, N_IT) as it:
                for u in range(UNROLL):
                    i = it * UNROLL + u
                    b = u % 2
                    act.wait_ge(s_w_used, it * (6 * UNROLL) + W_USED0 + 6 * u + 4)
                    silu().then_inc(s_silu_g, 1)
                    act.wait_ge(s_rows_psum, i + 2)
                    rows_copy().then_inc(s_rows_act, 1)
                    act.wait_ge(s_at_psum, i + 1)
                    turned_copy().then_inc(s_at, 1)
                    act.wait_ge(s_xe_psum, i + 2)
                    xe_copy(1 - b).then_inc(s_xe_act, 1)
                    act.wait_ge(s_w_used, it * (6 * UNROLL) + W_USED0 + 6 * u + 6)
                    act.wait_ge(s_y_free, i + 1)
                    y_copy(b).then_inc(s_y_act, 1)
            for j in range(2, 4):
                broadcast(3, j)
            nx = act.value_load(n_extra[0:1, 0:1], min_val=0, max_val=MAX_EXTRA)
            with act.If(nx > 0):
                act.wait_ge(s_scatter[0], 16 * (NE // 2))
                with act.Fori(0, nx) as j:
                    act.wait_ge(x_rows_psum, j + 1)
                    rows_copy().then_inc(x_rows_act, 1)
                    act.wait_ge(x_xe, j + 1)
                    xe_copy(0).then_inc(x_xe_act, 1)
                    act.wait_ge(x_gu, j + 1)
                    silu().then_inc(x_silu, 1)
                    act.wait_ge(x_at, j + 1)
                    turned_copy().then_inc(x_atc, 1)
                    act.wait_ge(x_dn, j + 1)
                    y_copy(0).then_inc(x_ya, 1)

            for t in range(TT):
                act.wait_ge(s_fsum, 2 * t + 2)
                act.activation(ring[:, t, D:2 * D], ring[:, t, 0:D], ACT.Square, bias=zero,
                               accum_out=f_ss[:, t:t + 1]).then_inc(s_fsq, 1)
                act.wait_ge(s_fsq, t + 1)
                act.activation(f_ss[:, t:t + 1], f_ss[:, t:t + 1], ACT.Sqrt, bias=eps_norm,
                               scale=1.0 / D).then_inc(s_frms, 1)

        @block.vector
        def _(dve):
            count = [0]

            def link(ins):
                count[0] += 1
                ins.then_inc(s_dve, 1)
                dve.wait_ge(s_dve, count[0])

            def ada(what):
                i, h, q = what[1], what[2], what[3] // 2
                n = dve_order.index(what)
                dve.wait_ge(s_turn, turn_no[("col", i - 2, 1)] + 1)
                w = landed(dve, what).rearrange("p (k n) -> p k n", k=8)
                a = sums(i, h)[:, QUARTER * q:QUARTER * (q + 1)]
                for k in range(8):
                    row = 8 * (what[3] % 2) + k
                    sc = silu_c[:, row:row + 1]
                    if row == 0:
                        ins = dve.tensor_scalar(a, w[:, k, :], sc, None, ALU.mult)
                    else:
                        ins = dve.scalar_tensor_tensor(a, w[:, k, :], sc, a, ALU.mult, ALU.add)
                    if k < 7:
                        link(ins)
                ins.then_inc(s_ada_dve, 1)
                dve.wait_ge(s_ada_dve, n + 1)

            dve.wait_ge(s_cexp, 1)
            link(dve.tensor_scalar(c_exp, c_exp, 1.0, None, ALU.add))
            link(dve.reciprocal(c_exp, c_exp))
            dve.tensor_tensor(silu_c, c_exp, par[:, A_C:A_C + KC], ALU.mult).then_inc(s_silu_c, 1)
            dve.wait_ge(s_lam_in, 16)
            for n in range(2):
                ins = dve.tensor_tensor_reduce(junk[:, 0:DK], rt[:, 2 * DK * n:2 * DK * n + DK],
                                               rt[:, 2 * DK * n + DK:2 * DK * (n + 1)], 1.0, 0.0,
                                               ALU.mult, ALU.add, lam_s[:, n:n + 1])
                if n == 0:
                    link(ins)
            ins.then_inc(s_lam, 1)
            dve.wait_ge(s_lam_e, 1)
            link(dve.scalar_tensor_tensor(neg_lam, lam_e[:, 1:2], LAM_INIT, lam_e[:, 0:1],
                                          ALU.subtract, ALU.subtract))
            link(dve.tensor_scalar(gsub, par[:, A_GSUB:A_GSUB + 1], 1.0 - LAM_INIT, None, ALU.mult))
            dve.wait_ge(s_rms, 1)
            link(dve.reciprocal(xrms, rms))
            for t in range(TT):
                dve.tensor_scalar(x_rows[:, t, :], x_rows[:, t, :], xrms[:, t:t + 1], None,
                                  ALU.mult).then_inc(s_xn, 1)

            def col_ready(i, h=1):
                dve.wait_ge(s_turn_read, turn_no[("col", i, h)] + 1)

            def split_w(s, units=range(UNITS)):
                for u in units:
                    v = UNITS * s + u
                    w_f32, w_lo, buf = unit_weights(v)
                    dve.wait_ge(s_w_hi, v + 1)
                    dve.tensor_tensor(w_lo, w_f32, w_hi[:, buf, :].bitcast(F32),
                                      ALU.subtract).then_inc(s_w_lo, 1)

            for h in range(2):
                half = slice(KH * h, KH * h + KH)
                col_ready(0, h)
                link(dve.scalar_tensor_tensor(cols[:, 0, half], mods[:, SC1, half], 1.0,
                                              par[:, A_GPRE1 + KH * h:A_GPRE1 + KH * h + KH],
                                              ALU.add, ALU.mult))
                col_ready(1, h)
                if h == 0:
                    dve.wait_ge(s_xt_read, KC // 2)
                for j in range(2 * h, 2 * h + 2):
                    for k in range(4 * j, 4 * j + 4):
                        ins = dve.tensor_scalar(lo_f32[:, k, :], h_turned[:, k, :], cols[:, 0, k:k + 1],
                                                mods[:, SH1, k:k + 1], ALU.mult, ALU.add)
                    ins.then_inc(s_h, 1)
                for j in range(2 * h, 2 * h + 2):
                    dve.wait_ge(s_h_hi, j + 1)
                    dve.tensor_tensor(h_lo[:, 4 * j:4 * j + 4, :], lo_f32[:, 4 * j:4 * j + 4, :],
                                      h_hi[:, 4 * j:4 * j + 4, :].bitcast(F32), ALU.subtract).then_inc(s_h_lo, 1)
                if h == 0:
                    for s in range(AHEAD):
                        split_w(s)

            def shift(h):
                dve.wait_ge(s_scores, h + 1)
                for m in range(2):
                    link(dve.scalar_tensor_tensor(soft[:, m, :], dist, -(0.5 ** (8.0 / HEADS)) ** (h + 1),
                                                  bank[4 + m][:, 0:P + SEQ], ALU.mult, ALU.add))
                link(dve.tensor_reduce(mx[:, 0::2], soft[:, :, 0:P], AX_X, ALU.max))
                link(dve.tensor_reduce(mx[:, 1::2], soft[:, :, P:P + SEQ], AX_X, ALU.max))
                dve.tensor_scalar(mx[:, :], mx[:, :], -1.0, None, ALU.mult).then_inc(s_shift, 1)

            def combine(h):
                dve.wait_ge(s_prob, h + 1)
                link(dve.reciprocal(p_rec[:, :], p_sum[:, :]))
                link(dve.tensor_scalar(p_rec[:, 2:4], p_rec[:, 2:4], neg_lam, None, ALU.mult))
                for t, span in enumerate((slice(0, P), slice(P, P + SEQ))):
                    link(dve.tensor_scalar(soft[:, 1, span], soft[:, 1, span], p_rec[:, 2 + t:3 + t], None, ALU.mult))
                    ins = dve.scalar_tensor_tensor(soft[:, 0, span], soft[:, 0, span], p_rec[:, t:t + 1],
                                                   soft[:, 1, span], ALU.mult, ALU.add)
                    if t == 0:
                        link(ins)
                ins.then_inc(s_a, 1)

            def split_y(groups):
                for j in groups:
                    dve.wait_ge(s_y_hi, j + 1)
                    dve.tensor_tensor(y_lo[:, 4 * j:4 * j + 4, :], y_turned[:, 4 * j:4 * j + 4, :],
                                      y_hi[:, 4 * j:4 * j + 4, :].bitcast(F32), ALU.subtract).then_inc(s_y_lo, 1)

            def norm_heads(g):
                dve.wait_ge(s_o_rms, g + 1)
                link(dve.reciprocal(o_rec[:, :], o_ss[:, :]))
                for h in range(HG):
                    for t in range(TT):
                        n = TT * h + t
                        ins = dve.tensor_scalar(o_raw[:, h, t, :], o_raw[:, h, t, :], o_rec[:, n:n + 1], None,
                                                ALU.mult)
                        if n < HG * TT - 1:
                            link(ins)
                ins.then_inc(s_o_norm, 1)

            def take_block(b):
                if b >= NB_IN:
                    g = b - NB_IN
                    dve.wait_ge(s_turn_read, turn_no[("bc", 0, 1 if g < 2 else 3)] + 1)
                    for n in range(TT):
                        dve.wait_ge(s_block_act, 2 * act_evac.index(b) + n + 1)
                        span = slice(512 * g, 512 * g + 512)
                        dve.tensor_tensor(y_sb[:, n, span], bank[BANKS[b][n]][:, :], acc[:, 0, span],
                                          ALU.mult).then_inc(s_y_gated, 1)
                    return
                if b not in dve_evac:
                    return
                kind, g = BLOCKS[b]
                dve.wait_ge(s_w_used, BLOCK_USED[b])
                c0 = HEADS + HG * g
                if kind == "X":
                    dve.wait_ge(s_block_act, 2 * (act_evac.index(b - 1) + 1))
                    link(dve.memset(conv_in[:, :, 0:2], 0.0))
                for n in range(2):
                    two = bank[BANKS[b][n]][:, :].rearrange("p (c s) -> p c s", c=2)
                    yc = y_turned[:, c0 + 2 * n:c0 + 2 * n + 2, :]
                    dst = conv_in[:, 2 * n:2 * n + 2, 2:] if kind == "X" else yc
                    dve.tensor_tensor(dst, two, yc, ALU.mult).then_inc(s_block_dve, 1)
                dve.wait_ge(s_block_dve, 2 * (dve_evac.index(b) + 1))
                if kind == "X":
                    for c in range(HG):
                        y = y_turned[:, c0 + c, :]
                        for i in range(3):
                            w = par[:, A_WCONV + HEADS * i + HG * g + c:A_WCONV + HEADS * i + HG * g + c + 1]
                            z = conv_in[:, c, i:i + SEQ]
                            if i == 0:
                                link(dve.tensor_scalar(y, z, w, None, ALU.mult))
                            else:
                                link(dve.scalar_tensor_tensor(y, z, w, y, ALU.mult, ALU.add))

            for s, (b, part) in enumerate(SUBSTEPS):
                if s == NB_IN * SUB:
                    split_y(range(2))
                if s >= 1 and SUBSTEPS[s - 1][1] == SUB - 1:
                    take_block(SUBSTEPS[s - 1][0])
                if s == NB_IN * SUB:
                    split_y(range(2, 4))
                if s - 1 in SCORE_AT:
                    combine(SCORE_AT[s - 1])
                ahead = AHEAD <= s + 1 < len(SUBSTEPS)
                if ahead:
                    split_w(s + 1, [0])
                if s in SCORE_AT:
                    shift(SCORE_AT[s])
                if ahead:
                    split_w(s + 1, [1])
                if s + 1 in FINISH_AT:
                    norm_heads(FINISH_AT[s + 1])
                for what in ADA_AT.get(s, []):
                    if what in dve_order:
                        ada(what)
                if s - 1 in COLUMNS_AT:
                    i, h = COLUMNS_AT[s - 1][-1]
                    if (i, h) == (2, 1):
                        col_ready(i)
                        dve.tensor_tensor(cols[:, 1, :], mods[:, GT1, :], par[:, A_GPOST1:A_GPOST1 + KC],
                                          ALU.mult).then_inc(s_cols, 2)
                    if (i, h) == (4, 1):
                        col_ready(i)
                        dve.scalar_tensor_tensor(cols[:, 2, :], mods[:, SC2, :], 1.0,
                                                 par[:, A_GPRE2:A_GPRE2 + KC], ALU.add, ALU.mult).then_inc(s_cols, 1)
            take_block(NB - 1)

            dve.wait_ge(s_block_act, 2 * len(act_evac))
            dve.tensor_reduce(yrms, y_ss[:, :, :], AX_X, ALU.add).then_inc(s_ysum, 1)
            dve.wait_ge(s_yrms, 1)
            link(dve.reciprocal(yrms, yrms))
            dve.wait_ge(s_turn_read, turn_no[("bc", 1, 3)] + 1)
            dve.wait_ge(s_y_gated, 2 * (NB - NB_IN))

            def residual(t):
                dve.wait_ge(s_x[t], 32)
                dve.scalar_tensor_tensor(x1[:, t, :], y_sb[:, t, :], yrms[:, t:t + 1], x1[:, t, :],
                                         ALU.mult, ALU.add).then_inc(s_x1, 1)

            def scale(t):
                dve.wait_ge(s_x1, t + 1)
                dve.tensor_tensor(y_sb[:, t, :], x1[:, t, :], acc[:, 1, :], ALU.mult).then_inc(s_x1a, 1)

            def second_norm(t):
                dve.wait_ge(s_h2rms, t + 1)
                link(dve.reciprocal(h2rms[:, t:t + 1], h2rms[:, t:t + 1]))
                dve.wait_ge(s_x1a, t + 1)
                dve.scalar_tensor_tensor(y_sb[:, t, :], y_sb[:, t, :], h2rms[:, t:t + 1], acc[:, 0, :],
                                         ALU.mult, ALU.add).then_inc(s_h2, 1)

            residual(0)
            scale(0)
            residual(1)
            dve.wait_ge(s_turn_read, turn_no[("bc", 2, 3)] + 1)
            second_norm(0)
            scale(1)
            second_norm(1)
            col_ready(LAST_MOD)
            dve.tensor_tensor(cols[:, 3, :], mods[:, GT2, :], par[:, A_GPOST2:A_GPOST2 + KC],
                              ALU.mult).then_inc(s_cols, 1)

            logit = rt[:, R_LOGIT:R_LOGIT + TT * N_LOGITS].rearrange("p (t n) -> p t n", t=TT)
            outer = rt[:, R_OUTER:R_OUTER + TT * NE].rearrange("p (t g j) -> p t g j", t=TT, g=N_GROUPS)
            picked = rt[:, R_PICKED:R_PICKED + TT * 8].rearrange("p (t j) -> p t j", t=TT)
            same4 = rt[:, R_SAME4:R_SAME4 + TT * 4].rearrange("p (t g) -> p t g", t=TT)
            group = rt[:, R_GROUP:R_GROUP + TT * 4].rearrange("p (t g) -> p t g", t=TT)
            same8 = rt[:, R_SAME8:R_SAME8 + TT * 8].rearrange("p (t j) -> p t j", t=TT)
            inner = rt[:, R_INNER:R_INNER + 2 * TT * 8].rearrange("p (k t j) -> p k t j", k=2, t=TT)
            top = rt[:, R_MAX:R_MAX + 6 * TT].rearrange("p (n t) -> p n t", t=TT)
            exps = rt[:, R_EXP:R_EXP + TT * 5].rearrange("p (t n) -> p t n", t=TT)
            vals = rt[:, R_VALS:R_VALS + 8 * TT].rearrange("p (n a) -> p n a", a=4)
            wts = vals.rearrange("p (k t) a -> p k t a", k=2)[:, :, :, 1]
            hot = rt[:, R_HOT:R_HOT + 2 * TT * NE].rearrange("p (k t e) -> p k t e", k=2, t=TT)
            both = rt[:, R_BOTH:R_BOTH + TT * NE].rearrange("p (t e) -> p t e", t=TT)
            prod = rt[:, R_PROD:R_PROD + 6 * TT * NE].rearrange("p (n k t e) -> p n k t e", n=3, k=2, t=TT)
            red = rt[:, R_RED:R_RED + 6 * TT]
            pos = rt[:, R_POS:R_POS + 10 * TT]
            kt = 2 * TT

            def over(ap2, n):
                return ap2.unsqueeze(2).to_broadcast([P, TT, n])

            def first_of(values, n, maxima, same, hot_out, priority):
                link(dve.tensor_reduce(maxima, values, AX_X, ALU.max))
                link(dve.tensor_tensor(same, values, over(maxima, n), ALU.is_equal))
                link(dve.tensor_tensor(same, same, priority.unsqueeze(1).to_broadcast([P, TT, n]), ALU.mult))
                link(dve.tensor_reduce(top[:, 3, :], same, AX_X, ALU.max))
                link(dve.tensor_tensor(hot_out, same, over(top[:, 3, :], n), ALU.is_equal))

            dve.tensor_copy(vals, cst[:, C_VALS:C_VALS + 8 * TT].rearrange("p (n a) -> p n a", a=4))
            dve.wait_ge(s_logit, 1)
            dve.tensor_copy(a_turned[0:N_LOGITS, 0:SEQ], bank[4][0:N_LOGITS, 0:SEQ]).then_inc(s_logit_dve, 1)
            dve.wait_ge(s_logit_sum, 1)
            for t in range(TT):
                ins = dve.tensor_tensor(logit[:, t, :], bank[7][:, N_LOGITS * t:N_LOGITS * (t + 1)],
                                        par[:, A_BRT:A_BRT + N_LOGITS], ALU.add)
            link(ins)
            pri4 = cst[:, C_PRI4:C_PRI4 + 4]
            pri8 = cst[:, C_PRI8:C_PRI8 + 8]
            first_of(logit[:, :, 0:4], 4, top[:, 0, :], same4, group, pri4)
            link(dve.tensor_tensor(exps[:, :, 0:4], logit[:, :, 0:4], over(top[:, 0, :], 4), ALU.subtract))
            for t in range(TT):
                ins = dve.tensor_tensor(outer[:, t, :, :],
                                        logit[:, t, N_GROUPS:N_LOGITS].rearrange("p (g j) -> p g j", g=N_GROUPS),
                                        group[:, t, :].unsqueeze(2).to_broadcast([P, N_GROUPS, 8]), ALU.mult)
            link(ins)
            link(dve.tensor_reduce(picked, outer.rearrange("p t g j -> p t j g"), AX_X, ALU.add))
            first_of(picked, 8, top[:, 1, :], same8, inner[:, 0, :, :], pri8)
            link(dve.scalar_tensor_tensor(picked, inner[:, 0, :, :], -1e30, picked, ALU.mult, ALU.add))
            first_of(picked, 8, top[:, 2, :], same8, inner[:, 1, :, :], pri8)
            dve.tensor_tensor(exps[:, :, 4:5], over(top[:, 2, :], 1), over(top[:, 1, :], 1),
                              ALU.subtract).then_inc(s_gexp_in, 1)
            for k in range(2):
                for t in range(TT):
                    ins = dve.tensor_tensor(hot[:, k, t, :].rearrange("p (g j) -> p g j", g=N_GROUPS),
                                            group[:, t, :].unsqueeze(2).to_broadcast([P, N_GROUPS, 8]),
                                            inner[:, k, t, :].unsqueeze(1).to_broadcast([P, N_GROUPS, 8]), ALU.mult)
            link(ins)
            dve.tensor_tensor(both, hot[:, 0, :, :], hot[:, 1, :, :], ALU.add).then_inc(s_picks, 1)
            dve.wait_ge(s_gexp, 1)
            link(dve.tensor_reduce(top[:, 4, :], exps[:, :, 0:4], AX_X, ALU.add))
            link(dve.tensor_scalar(top[:, 5, :].unsqueeze(2), exps[:, :, 4:5], 1.0, None, ALU.add))
            link(dve.tensor_tensor(top[:, 4, :], top[:, 4, :], top[:, 5, :], ALU.mult))
            link(dve.reciprocal(wts[:, 0, :], top[:, 4, :]))
            link(dve.tensor_tensor(wts[:, 1, :].unsqueeze(2), wts[:, 0, :].unsqueeze(2), exps[:, :, 4:5], ALU.mult))
            dve.wait_ge(s_rank, 1)
            n_e = bank[7][0:NE, 0:1]
            extra = rt[0:NE, R_EXTRA:R_EXTRA + 1]
            n_sb = rt[0:NE, R_EXTRA + 1:R_EXTRA + 2]
            link(dve.tensor_scalar(n_sb, n_e, -1.0, None, ALU.add))
            over_lot = rt[0:NE, R_OVER:R_OVER + N_LOTS]
            full = cst[:, C_FULL:C_FULL + N_LOTS]
            link(dve.tensor_scalar(over_lot, full[0:NE, :], n_sb, None, ALU.is_le))
            dve.tensor_reduce(extra, over_lot, AX_X, ALU.add).then_inc(s_extra, 1)
            for k in range(2):
                dve.tensor_tensor(prod[:, 0, k, :, :], hot[:, k, :, :],
                                  bank[6][:, 0:TT * NE].rearrange("p (t e) -> p t e", t=TT),
                                  ALU.mult).then_inc(s_rank_used, 1)
            dve.wait_ge(s_rank_used, 2)
            for k in range(2):
                link(dve.tensor_tensor(prod[:, 2, k, :, :], hot[:, k, :, :],
                                       cst[:, C_IOTA:C_IOTA + NE].unsqueeze(1).to_broadcast([P, TT, NE]), ALU.mult))
            dve.wait_ge(s_base, 1)
            for k in range(2):
                link(dve.tensor_tensor(prod[:, 1, k, :, :], hot[:, k, :, :],
                                       bank[7][:, 0:NE].unsqueeze(1).to_broadcast([P, TT, NE]), ALU.mult))
            link(dve.tensor_copy(n_extra[:, :], bank[7][:, NE:NE + 1]))
            link(dve.tensor_reduce(red, prod.rearrange("p n k t e -> p (n k t) e"), AX_X, ALU.add))
            rank, base, expert = red[:, 0:kt], red[:, kt:2 * kt], red[:, 2 * kt:3 * kt]
            lot, beyond, dlt, slot, item = (pos[:, kt * n:kt * (n + 1)] for n in range(5))
            hot_items = picks[:, G_ITEM:G_ITEM + kt * ITEMS].rearrange("p (n b) -> p n b", n=kt)
            one_slot = picks[:, G_SLOT:G_SLOT + kt * CAP].rearrange("p (n b) -> p n b", n=kt)

            def make_pick(b, item, half, count, done):
                for t in range(TT):
                    ins = dve.scalar_tensor_tensor(pick(b, t), one_slot[:, t, :],
                                                   picks[:, item(G_ITEM + ITEMS * t)],
                                                   one_slot[:, t, :], ALU.mult, ALU.mult)
                ins.then_inc(half, 1)
                dve.wait_ge(half, count)
                for t in range(TT):
                    ins = dve.scalar_tensor_tensor(pick(b, t), one_slot[:, TT + t, :],
                                                   picks[:, item(G_ITEM + ITEMS * (TT + t))],
                                                   pick(b, t), ALU.mult, ALU.add)
                ins.then_inc(done, 1)

            dve.tensor_copy(vals[:, :, 3], expert)
            over_rank = rt[:, R_OVER:R_OVER + kt * N_LOTS].rearrange("p (n l) -> p n l", n=kt)
            link(dve.tensor_tensor(over_rank, rank.unsqueeze(2).to_broadcast([P, kt, N_LOTS]),
                                   full.unsqueeze(1).to_broadcast([P, kt, N_LOTS]), ALU.is_ge))
            link(dve.tensor_reduce(lot, over_rank, AX_X, ALU.add))
            dve.tensor_tensor(beyond.unsqueeze(2), over_rank[:, :, 0:1], over_rank[:, :, 0:1], ALU.mult)
            link(dve.scalar_tensor_tensor(slot, lot, -float(CAP), rank, ALU.mult, ALU.add))
            link(dve.tensor_tensor(dlt, base, lot, ALU.add))
            link(dve.scalar_tensor_tensor(dlt, dlt, NE - 1.0, expert, ALU.add, ALU.subtract))
            link(dve.tensor_tensor(dlt, dlt, beyond, ALU.mult))
            link(dve.tensor_tensor(item, dlt, expert, ALU.add))
            link(dve.tensor_tensor(hot_items, cst[:, C_IOTA:C_IOTA + ITEMS].unsqueeze(1).to_broadcast([P, kt, ITEMS]),
                                   item.unsqueeze(2).to_broadcast([P, kt, ITEMS]), ALU.is_equal))
            dve.tensor_tensor(one_slot, cst[:, C_IOTA:C_IOTA + CAP].unsqueeze(1).to_broadcast([P, kt, CAP]),
                              slot.unsqueeze(2).to_broadcast([P, kt, CAP]), ALU.is_equal).then_inc(s_one_slot, 1)
            dve.wait_ge(s_one_slot, 1)
            make_pick(0, lambda c: slice(c, c + 1), s_half_pick, 1, s_pick)
            for n in range(kt):
                dve.tensor_scalar(hot_slot(n), cst[:, C_SLOT:C_SLOT + P], slot[:, n:n + 1], None, ALU.is_equal)
                ins = dve.tensor_tensor(hot_item(n), hot_items[:, n, :].unsqueeze(1).to_broadcast([P, 4, ITEMS]),
                                        vals[:, n, :].unsqueeze(2).to_broadcast([P, 4, ITEMS]), ALU.mult)
            ins.then_inc(s_hot, 1)
            make_pick(1, lambda c: slice(c + 1, c + 2), s_half_pick, 2, s_pick)
            def xe_copy(b):
                return dve.tensor_copy(xe_turned[:, b, 8:16, :], bank[3][:, 0:8 * CAP].rearrange("p (k s) -> p k s", k=8))

            def rows_copy():
                return dve.tensor_copy(rt[:, 512:1024], bank[7][:, :])

            dve.wait_ge(s_rows_psum, 1)
            rows_copy().then_inc(s_rows_dve, 1)
            dve.wait_ge(s_xe_psum, 1)
            xe_copy(0).then_inc(s_xe_dve, 1)
            dve.wait_ge(s_table, 1)
            table = acc[:, 0, T_TABLE:T_TABLE + 4 * ITEMS].rearrange("p (a b) -> p a b", a=4)
            miss = acc[:, 0, T_MISS:T_MISS + ITEMS]
            row = acc[:, 0, T_MISS + ITEMS:T_MISS + 2 * ITEMS]
            link(dve.tensor_copy(table, bank[6][:, 0:4 * ITEMS].rearrange("p (a b) -> p a b", a=4)))
            link(dve.tensor_scalar(miss, table[:, 2, :], -NOWHERE, NOWHERE, ALU.mult, ALU.add))
            link(dve.scalar_tensor_tensor(row, table[:, 0, :], 2.0, miss, ALU.mult, ALU.add))
            link(dve.tensor_scalar(s_idx[:, :], row, cst[:, C_GRP:C_GRP + 1], None, ALU.add))
            link(dve.tensor_copy(e_idx[:, :], table[:, 3, :]))
            dve.tensor_copy(weight[:, :], table[:, 1, :]).then_inc(s_tables, 1)
            dve.wait_ge(s_tables, 1)

            def weigh(column):
                return dve.scalar_tensor_tensor(act_rows, silu_g, weight[0:CAP, column], bank[0][0:CAP, :],
                                                ALU.mult, ALU.mult)

            def y_copy(b):
                return dve.tensor_copy(y_item[:, b, 512:1024], bank[6][:, :])

            dve.sem_inc(s_y_dve, 1)
            with dve.Fori(0, N_IT) as it:
                for u in range(UNROLL):
                    i = it * UNROLL + u
                    b = u % 2
                    dve.wait_ge(s_silu_g, i + 1)
                    weigh(bass.ds(i, 1)).then_inc(s_act_rows, 1)
                    dve.wait_ge(s_rows_psum, i + 2)
                    rows_copy().then_inc(s_rows_dve, 1)
                    dve.wait_ge(s_xe_psum, i + 2)
                    xe_copy(1 - b).then_inc(s_xe_dve, 1)
                    dve.wait_ge(s_w_used, it * (6 * UNROLL) + W_USED0 + 6 * u + 6)
                    dve.wait_ge(s_y_free, i + 1)
                    y_copy(b).then_inc(s_y_dve, 1)
                    make_pick(b, lambda c: bass.ds(i + (c + 2), 1), s_half_pick, i + 3, s_pick)
            nx = dve.value_load(n_extra[0:1, 0:1], min_val=0, max_val=MAX_EXTRA)
            with dve.If(nx > 0):
                dve.wait_ge(s_scatter[0], 16 * (NE // 2))
                with dve.Fori(0, nx) as j:
                    make_pick(0, lambda c: bass.ds(j + (c + NE), 1), x_half_pick, j + 1, x_pick)
                    dve.wait_ge(x_rows_psum, j + 1)
                    rows_copy().then_inc(x_rows_dve, 1)
                    dve.wait_ge(x_xe, j + 1)
                    xe_copy(0).then_inc(x_xe_dve, 1)
                    dve.wait_ge(x_silu, j + 1)
                    weigh(bass.ds(j + NE, 1)).then_inc(x_rows_done, 1)
                    dve.wait_ge(x_dn, j + 1)
                    y_copy(0).then_inc(x_yd, 1)
            def add_pair(t):
                for c in range(2):
                    span = slice(D // 2 * c, D // 2 * (c + 1))
                    dve.wait_ge(s_pair[2 * t + c], 16)
                    dve.tensor_tensor(ring[:, t, span], ring[:, t, span], ring[:, t, D:2 * D][:, span],
                                      ALU.add).then_inc(s_fsum, 1)
                dve.wait_ge(s_fsum, 2 * t + 2)
                dve.tensor_tensor(ring[:, 2 + t, 0:D], ring[:, t, 0:D], acc[:, 1, :], ALU.mult).then_inc(s_gated, 1)

            def finish_rows(t):
                dve.wait_ge(s_frms, t + 1)
                link(dve.reciprocal(f_ss[:, t:t + 1], f_ss[:, t:t + 1]))
                dve.wait_ge(s_gated, t + 1)
                for c in range(2):
                    span = slice(D // 2 * c, D // 2 * (c + 1))
                    dve.scalar_tensor_tensor(x1[:, t, span], ring[:, 2 + t, span], f_ss[:, t:t + 1],
                                             x1[:, t, span], ALU.mult, ALU.add).then_inc(s_fin, 1)

            dve.wait_ge(s_turn_read, turn_no[("bc", 3, 3)] + 1)
            add_pair(0)
            add_pair(1)
            finish_rows(0)
            finish_rows(1)


def constants():
    import numpy as np
    c = np.zeros((P, C_ALL), np.float32)
    p = np.arange(P)
    c[:, C_ID:C_ID + P] = np.eye(P)
    c[:, C_TRI:C_TRI + P] = p[:, None] < p[None, :]
    c[:, C_ONE:C_ONE + P] = 1.0
    for t, (c0, n) in enumerate(((C_DIST, P), (C_DIST + P, SEQ))):
        q, k = t * P + p[:, None], np.arange(n)[None, :]
        c[:, c0:c0 + n] = np.where(k // CHUNK <= q // CHUNK, np.abs(q - k), 1e37)
    c[:, C_SLOT:C_SLOT + P] = p % UPPER
    c[:, C_IOTA:C_IOTA + ITEMS] = np.arange(ITEMS)
    c[:, C_PRI8:C_PRI8 + 8] = 8 - np.arange(8)
    c[:, C_PRI4:C_PRI4 + 4] = 4 - np.arange(4)
    for n in range(2 * TT):
        c[:, C_VALS + 4 * n] = n * P + p
        c[:, C_VALS + 4 * n + 2] = 1.0
    c[:, C_FULL:C_FULL + N_LOTS] = CAP * np.arange(1, N_LOTS + 1) - 0.5
    c[:, C_GRP] = p >= UPPER
    c[:, C_TILE] = p % COL_TILE == 0
    return c


def kernel(**inputs):
    import numpy as np
    import concourse.bacc as bacc
    from concourse.bass_utils import run_bass_kernel_spmd

    a = {name: np.asarray(v) for name, v in inputs.items()}

    def column(v):
        return v.reshape(2, P, KH).transpose(1, 0, 2).reshape(P, KC)

    def over_partitions(v):
        return np.broadcast_to(v.reshape(1, -1), (P, v.size))

    small = np.concatenate([
        a["c"][0].reshape(P, KC), column(a["g_pre1"][0]), column(a["g_post1"][0]), column(a["g_pre2"][0]),
        column(a["g_post2"][0]),
        a["b_ada"][0].reshape(6, 2, P, KH).transpose(2, 0, 1, 3).reshape(P, 6 * KC),
        a["w_conv"][0].reshape(3, HEADS, P).transpose(2, 0, 1).reshape(P, 3 * HEADS),
        a["g_subln"][0].reshape(P, 1),
        over_partitions(a["b_router_g"][0]), over_partitions(a["b_router_e"][0]),
        over_partitions(np.array([NORM_EPS, SUBLN_EPS, 0.0], np.float32))], axis=1)
    lam = over_partitions(np.concatenate([a[n][0] for n in ("lam_q1", "lam_k1", "lam_q2", "lam_k2")]))
    router = np.concatenate([a["w_router_g"][0], a["w_router_e"][0].reshape(D, NE)], axis=1)
    feeds = {"consts": constants(), "small": small, "lam": lam, "router": router}
    feeds.update({n: a[n] for n in ("x", "w_ada", "w_in", "w_out", "w_gate", "w_up", "w_down")})

    nc = bacc.Bacc("TRN2", target_bir_lowering=False, num_devices=1)
    arrays, args = {}, []
    for name, v in feeds.items():
        v = np.ascontiguousarray(v)
        arrays[name + "_dram"] = v
        args.append(nc.dram_tensor(name + "_dram", v.shape, mybir.dt.from_np(v.dtype), kind="ExternalInput").ap())
    args.append(nc.dram_tensor("out_dram", (1, SEQ, D), F32, kind="ExternalOutput").ap())
    hybrid_layer(nc, *args)
    r = run_bass_kernel_spmd(nc, [arrays], core_ids=[0])
    return r.results[0]["out_dram"]
```
